# Optimizing a Trainium2 kernel written in Bass

```python
import math
import jax, jax.numpy as jnp
from jax import lax
import numpy as np

D_MODEL = 1024
BATCH = 1
SEQ = 1024
DEPTH = 1

HEAD_DIM = 64
FOX_HEADS = 8
SWA_HEADS = 8
SWA_KV_HEADS = 2
SWA_GROUP = SWA_HEADS // SWA_KV_HEADS
FOX_W = FOX_HEADS * HEAD_DIM
SWA_QW = SWA_HEADS * HEAD_DIM
SWA_KVW = SWA_KV_HEADS * HEAD_DIM
MIX_WIDTH = FOX_W + SWA_QW
WINDOW = 128
Q_BLOCK = 128
ROPE_THETA = 10000.0

OFF_FQ = 0
OFF_FK = OFF_FQ + FOX_W
OFF_FV = OFF_FK + FOX_W
OFF_FF = OFF_FV + FOX_W
OFF_SQ = OFF_FF + FOX_HEADS
OFF_SK = OFF_SQ + SWA_QW
OFF_SV = OFF_SK + SWA_KVW
IN_COLS = OFF_SV + SWA_KVW

PEER_HEADS = 8
N_KEYS = 128
N_EXPERTS = N_KEYS * N_KEYS
PEER_DKEY = 256
PEER_HALF = PEER_DKEY // 2
PEER_TOPK = 16
PEER_TOK_BLOCK = 128

LN_EPS = 1e-5
ALPHA = (2.0 * DEPTH) ** 0.25
BETA = (8.0 * DEPTH) ** -0.25

kernel_name = "hymba_fox_swa_sink_peer_deepnorm"

def layer_norm(x, g, b):
    xf = x.astype(jnp.float32)
    mu = jnp.mean(xf, axis=-1, keepdims=True)
    var = jnp.mean(jnp.square(xf - mu), axis=-1, keepdims=True)
    return ((xf - mu) * lax.rsqrt(var + LN_EPS) * g.astype(jnp.float32) + b.astype(jnp.float32)).astype(x.dtype)

def rope(x, pos):
    half = HEAD_DIM // 2
    inv = ROPE_THETA ** (-jnp.arange(half, dtype=jnp.float32) / half)
    ang = pos.astype(jnp.float32)[:, None] * inv[None, :]
    cos = jnp.cos(ang)[None, :, None, :]
    sin = jnp.sin(ang)[None, :, None, :]
    xf = x.astype(jnp.float32)
    x1, x2 = xf[..., :half], xf[..., half:]
    return jnp.concatenate([x1 * cos - x2 * sin, x2 * cos + x1 * sin], axis=-1).astype(x.dtype)

def forgetting_attention(q, k, v, f_logit):
    B, S, H, D = q.shape
    c = jnp.cumsum(jax.nn.log_sigmoid(f_logit.astype(jnp.float32)), axis=1)
    c = jnp.transpose(c, (0, 2, 1))
    scale = D ** -0.5
    outs = []
    for i in range(S // Q_BLOCK):
        q0, q1 = i * Q_BLOCK, (i + 1) * Q_BLOCK
        s = jnp.einsum('bqhd,bkhd->bhqk', q[:, q0:q1], k[:, :q1],
                       preferred_element_type=jnp.float32) * scale
        bias = c[:, :, q0:q1, None] - c[:, :, None, :q1]
        causal = (q0 + jnp.arange(Q_BLOCK))[:, None] >= jnp.arange(q1)[None, :]
        s = jnp.where(causal[None, None], s + bias, -jnp.inf)
        p = jax.nn.softmax(s, axis=-1)
        outs.append(jnp.einsum('bhqk,bkhd->bqhd', p.astype(v.dtype), v[:, :q1]))
    return jnp.concatenate(outs, axis=1)

def sliding_window_attention(q, k, v, sinks):
    B, S, H, D = q.shape
    nb = S // WINDOW
    scale = D ** -0.5
    qb = q.reshape(B, nb, WINDOW, SWA_KV_HEADS, SWA_GROUP, D)

    def banded(t):
        tb = t.reshape(B, nb, WINDOW, SWA_KV_HEADS, D)
        prev = jnp.pad(tb, ((0, 0), (1, 0), (0, 0), (0, 0), (0, 0)))[:, :-1]
        return jnp.concatenate([prev, tb], axis=2)

    kb, vb = banded(k), banded(v)
    s = jnp.einsum('bnqkgd,bnjkd->bnkgqj', qb, kb, preferred_element_type=jnp.float32) * scale
    r = jnp.arange(WINDOW)[:, None]
    j = jnp.arange(2 * WINDOW)[None, :]
    diff = r + WINDOW - j
    in_window = (diff >= 0) & (diff < WINDOW)
    key_pos = jnp.arange(nb)[:, None] * WINDOW - WINDOW + jnp.arange(2 * WINDOW)[None, :]
    mask = in_window[None] & (key_pos >= 0)[:, None, :]
    s = jnp.where(mask[None, :, None, None], s, -jnp.inf)
    sink = sinks.astype(jnp.float32).reshape(SWA_KV_HEADS, SWA_GROUP)[None, None, :, :, None, None]
    sink = jnp.broadcast_to(sink, s.shape[:-1] + (1,))
    p = jax.nn.softmax(jnp.concatenate([s, sink], axis=-1), axis=-1)[..., :-1]
    o = jnp.einsum('bnkgqj,bnjkd->bnqkgd', p.astype(v.dtype), vb)
    return o.reshape(B, S, H, D)

def peer_ffn(x, w_query, sub_keys, expert_u, expert_v):
    B, S, Dm = x.shape
    xt = x.reshape((B * S) // PEER_TOK_BLOCK, PEER_TOK_BLOCK, Dm)

    def block(xb):
        tb = xb.shape[0]
        q = (xb @ w_query).reshape(tb, PEER_HEADS, 2, PEER_HALF)
        s = jnp.einsum('thpc,hpnc->thpn', q, sub_keys, preferred_element_type=jnp.float32)
        top_s, top_i = lax.top_k(s, PEER_TOPK)
        cand_s = (top_s[:, :, 0, :, None] + top_s[:, :, 1, None, :]).reshape(tb, PEER_HEADS, PEER_TOPK * PEER_TOPK)
        cand_i = (top_i[:, :, 0, :, None] * N_KEYS + top_i[:, :, 1, None, :]).reshape(tb, PEER_HEADS, PEER_TOPK * PEER_TOPK)
        best_s, best_pos = lax.top_k(cand_s, PEER_TOPK)
        idx = jnp.take_along_axis(cand_i, best_pos, axis=-1)
        g = jax.nn.softmax(best_s, axis=-1)
        u = expert_u[idx]
        h = jax.nn.gelu(jnp.einsum('thkd,td->thk', u, xb, preferred_element_type=jnp.float32), approximate=False)
        w = (g * h).astype(xb.dtype)
        return jnp.einsum('thk,thkd->td', w, expert_v[idx])

    return lax.map(block, xt).reshape(B, S, Dm)

def setup_inputs(seed: int = 0) -> dict:
    key = jax.random.key(seed)
    ks = jax.random.split(key, 14)
    f32 = jnp.float32
    nrm = lambda k, shape: jax.random.normal(k, shape, dtype=f32)
    x = nrm(ks[0], (BATCH, SEQ, D_MODEL))
    w_in = nrm(ks[1], (DEPTH, D_MODEL, IN_COLS)) * D_MODEL ** -0.5
    b_forget = 0.1 * nrm(ks[2], (DEPTH, FOX_HEADS))
    swa_sinks = 0.1 * nrm(ks[3], (DEPTH, SWA_HEADS))
    w_out = nrm(ks[4], (DEPTH, MIX_WIDTH, D_MODEL)) * MIX_WIDTH ** -0.5 * BETA
    ln1_g = 1.0 + 0.01 * nrm(ks[5], (DEPTH, D_MODEL))
    ln1_b = 0.01 * nrm(ks[6], (DEPTH, D_MODEL))
    w_query = nrm(ks[7], (DEPTH, D_MODEL, PEER_HEADS * PEER_DKEY)) * D_MODEL ** -0.5
    sub_keys = nrm(ks[8], (DEPTH, PEER_HEADS, 2, N_KEYS, PEER_HALF)) * PEER_HALF ** -0.5
    expert_u = nrm(ks[9], (DEPTH, N_EXPERTS, D_MODEL)) * D_MODEL ** -0.5
    expert_v = nrm(ks[10], (DEPTH, N_EXPERTS, D_MODEL)) * BETA
    ln2_g = 1.0 + 0.01 * nrm(ks[11], (DEPTH, D_MODEL))
    ln2_b = 0.01 * nrm(ks[12], (DEPTH, D_MODEL))
    return {"x": x, "w_in": w_in, "b_forget": b_forget, "swa_sinks": swa_sinks, "w_out": w_out,
            "ln1_g": ln1_g, "ln1_b": ln1_b, "w_query": w_query, "sub_keys": sub_keys,
            "expert_u": expert_u, "expert_v": expert_v, "ln2_g": ln2_g, "ln2_b": ln2_b}

def reference(x, w_in, b_forget, swa_sinks, w_out, ln1_g, ln1_b, w_query, sub_keys,
              expert_u, expert_v, ln2_g, ln2_b):
    B, S, _ = x.shape
    pos = jnp.arange(S)
    for l in range(DEPTH):
        proj = x @ w_in[l]
        fq = proj[..., OFF_FQ:OFF_FK].reshape(B, S, FOX_HEADS, HEAD_DIM)
        fk = proj[..., OFF_FK:OFF_FV].reshape(B, S, FOX_HEADS, HEAD_DIM)
        fv = proj[..., OFF_FV:OFF_FF].reshape(B, S, FOX_HEADS, HEAD_DIM)
        ff = proj[..., OFF_FF:OFF_SQ] + b_forget[l]
        sq = rope(proj[..., OFF_SQ:OFF_SK].reshape(B, S, SWA_HEADS, HEAD_DIM), pos)
        sk = rope(proj[..., OFF_SK:OFF_SV].reshape(B, S, SWA_KV_HEADS, HEAD_DIM), pos)
        sv = proj[..., OFF_SV:IN_COLS].reshape(B, S, SWA_KV_HEADS, HEAD_DIM)
        fox_out = forgetting_attention(fq, fk, fv, ff).reshape(B, S, FOX_W)
        swa_out = sliding_window_attention(sq, sk, sv, swa_sinks[l]).reshape(B, S, SWA_QW)
        mix = jnp.concatenate([fox_out, swa_out], axis=-1) @ w_out[l]
        x = layer_norm(ALPHA * x + mix, ln1_g[l], ln1_b[l])
        ffn = peer_ffn(x, w_query[l], sub_keys[l], expert_u[l], expert_v[l])
        x = layer_norm(ALPHA * x + ffn, ln2_g[l], ln2_b[l])
    return x


_drawn_inputs = setup_inputs


def setup_inputs(seed=0):
    import zlib

    import numpy as np

    out = dict(_drawn_inputs(seed))
    spreads = {}
    factors = {'swa_sinks': 51.754, 'ln2_g': 32.004, 'ln2_b': 32.65}
    for name, (base, spread) in spreads.items():
        noise = np.random.default_rng([zlib.crc32(name.encode()), seed]).standard_normal(out[name].shape)
        drawn = base * np.exp(spread * noise) if base else spread * noise
        out[name] = __import__('jax').numpy.asarray(drawn.astype(out[name].dtype))
    for name, factor in factors.items():
        out[name] = (out[name] * factor).astype(out[name].dtype)
    return out
```

```python
from contextlib import ExitStack

import numpy as np

import concourse.bass as bass
from concourse import mybir

P = 128
D_MODEL = 1024
SEQ = 1024
KD = D_MODEL // P
TILES = SEQ // P
HEAD_DIM = 64
FOX_HEADS = 8
SWA_HEADS = 8
PAIRS = FOX_HEADS // 2
N_KEYS = 128
PEER_HEADS = 8
TOPK = 16
SETS = 2 * PEER_HEADS
CHUNK = 32
GROUP = 4
LN_EPS = 1e-5
ALPHA = 2.0 ** 0.25
SCALE = HEAD_DIM ** -0.5
LOW = -3.0e38

F32 = mybir.dt.float32
BF16 = mybir.dt.bfloat16
U32 = mybir.dt.uint32
ALU = mybir.AluOpType
ACT = mybir.ActivationFunctionType
AX = mybir.AxisListType


def past(count):
    return not isinstance(count, int) or count > 0


def newton_rstd(dve, moments, std, rstd, tmp, moments_done, n_moments, std_done, n_std, step, n):
    dve.wait_ge(moments_done, n_moments)
    dve.wait_ge(std_done, n_std)
    dve.reciprocal(rstd, std).then_inc(step, 1)
    dve.tensor_scalar(tmp, moments[:, 1:2], LN_EPS, -0.5, ALU.add, ALU.mult).then_inc(step, 1)
    dve.wait_ge(step, n + 2)
    dve.scalar_tensor_tensor(tmp, tmp, rstd, rstd, ALU.mult, ALU.mult).then_inc(step, 1)
    dve.wait_ge(step, n + 3)
    dve.tensor_scalar(tmp, tmp, 1.5, None, ALU.add).then_inc(step, 1)
    dve.wait_ge(step, n + 4)
    dve.tensor_tensor(rstd, rstd, tmp, ALU.mult).then_inc(step, 1)
    dve.wait_ge(step, n + 5)


def attention_phase(nc, x_t, w_fox, w_swa, w_skv, w_forget, b_forget, sinks, consts, mixed_t):
    with ExitStack() as ctx:
        sb = lambda name, shape, dt=F32: ctx.enter_context(nc.sbuf_tensor("att_" + name, shape, dt))
        sem = lambda name: ctx.enter_context(nc.semaphore(name))
        xt = sb("xt", [P, KD, SEQ])
        w_pair = sb("w_pair", [P, 3, KD, P])
        w_sq = sb("w_sq", [P, KD, P])
        w_kv = sb("w_kv", [P, 2, KD, P])
        w_f = sb("w_f", [P, KD, FOX_HEADS])
        ident = sb("a_ident", [P, P])
        rot = sb("rot", [P, P])
        minus_row = sb("minus_row", [FOX_HEADS, FOX_HEADS, P])
        cos = sb("cos", [P, SEQ])
        sin = sb("sin", [P, SEQ])
        ident16 = sb("ident16", [P, P], BF16)
        masks = sb("masks", [P, 2 * P])
        masks16 = sb("masks16", [P, 2 * P], BF16)
        b_f = sb("b_f", [FOX_HEADS, 1])
        sink = sb("sink", [P, PAIRS, 2])
        neg_sink = sb("neg_sink", [P, PAIRS, 2])
        f_tmp = sb("f_tmp", [FOX_HEADS, 3, SEQ])
        c_row = sb("c_row", [FOX_HEADS, SEQ])
        zeros = sb("a_zeros", [FOX_HEADS, SEQ])
        neg_c = sb("neg_c", [P, FOX_HEADS, SEQ])
        c_col = sb("c_col", [P, TILES, FOX_HEADS])
        q_t = sb("q_t", [P, SEQ])
        k_t = sb("k_t", [P, SEQ])
        v_rows = sb("v_rows", [P, TILES, P])
        sk_t = sb("sk_t", [P, SEQ])
        sv_rows = sb("sv_rows", [P, TILES, P])
        raw = sb("raw", [P, SEQ])
        rope_tmp = sb("rope_tmp", [P, SEQ])
        probs = sb("probs", [P, 2, SEQ])
        probs_t = sb("probs_t", [P, 2, SEQ])
        neg_max = sb("neg_max", [P, 2, 2])
        row_sum = sb("row_sum", [P, 2, 2])
        sink_exp = sb("sink_exp", [P, 2, 2])
        inv_sum = sb("inv_sum", [P, 2, 2])
        pair_out = sb("pair_out", [P, 2, SEQ])
        s_psum = [ctx.enter_context(nc.psum_tensor(f"s_psum{k}", [P, 2, 512], F32)) for k in range(2)]
        t_psum = [ctx.enter_context(nc.psum_tensor(f"t_psum{k}", [P, 512], F32)) for k in range(2)]
        o_psum = [ctx.enter_context(nc.psum_tensor(f"a_o_psum{k}", [P, 512], F32)) for k in range(2)]

        x_in, w_first_in, const_in = sem("x_in"), sem("w_first_in"), sem("const_in")
        w_pair_in, w_sq_in = sem("w_pair_in"), sem("w_sq_in")
        const_made = sem("const_made")
        f_psum_done, f_step, c_done = sem("f_psum_done"), sem("f_step"), sem("c_done")
        fa_step = sem("fa_step")
        bcast_done, bcast_copied = sem("bcast_done"), sem("bcast_copied")
        k_proj, k_raw, k_rot, k_ready = sem("k_proj"), sem("k_raw"), sem("k_rot"), sem("k_ready")
        kr_step, v_proj, v_ready = sem("kr_step"), sem("v_proj"), sem("v_ready")

        with nc.Block() as block:
            @block.sync
            def _(sp):
                for c in range(KD):
                    sp.dma_start(xt[:, c], x_t[c]).then_inc(x_in, 16)
                sp.dma_start(w_f[:, :, :], w_forget).then_inc(w_first_in, 16)
                sp.dma_start(w_kv[:, :, :, :], w_skv).then_inc(w_first_in, 16)
                sp.dma_start(b_f[:, :], b_forget).then_inc(const_in, 16)
                sp.dma_start(ident[:, :], consts["ident"]).then_inc(const_in, 16)
                sp.dma_start(rot[:, :], consts["rot"]).then_inc(const_in, 16)
                sp.dma_start(minus_row[:, :, :], consts["minus_row"]).then_inc(const_in, 16)
                sp.dma_start(cos[:, :], consts["cos"]).then_inc(const_in, 16)
                sp.dma_start(sin[:, :], consts["sin"]).then_inc(const_in, 16)
                sp.dma_start(masks[:, :], consts["masks"]).then_inc(const_in, 16)
                sp.dma_start(sink[:, :, :].rearrange("p j g -> p (j g)"), sinks.partition_broadcast(P)
                             ).then_inc(const_in, 16)
                sp.dma_start(w_pair[:, :, :, :], w_fox[0]).then_inc(w_pair_in, 16)
                sp.dma_start(w_sq[:, :, :], w_swa[0]).then_inc(w_sq_in, 16)

            @block.vector
            def _(dve):
                dve.wait_ge(const_in, 16 * 8)
                dve.tensor_copy(ident16[:, :], ident[:, :]).then_inc(const_made, 1)
                dve.tensor_copy(masks16[:, :], masks[:, :]).then_inc(const_made, 1)
                dve.tensor_scalar(neg_sink[:, :, :], sink[:, :, :], -1.0, None, ALU.mult).then_inc(const_made, 1)
                dve.memset(zeros[:, :], 0.0).then_inc(const_made, 1)
                dve.wait_ge(f_psum_done, 1)
                dve.tensor_scalar(f_tmp[:, 0], s_psum[0][0:FOX_HEADS].rearrange("p a b -> p (a b)"),
                                  b_f[:, :], None, ALU.add).then_inc(f_step, 1)
                dve.wait_ge(f_step, 1)
                dve.tensor_scalar(f_tmp[:, 1], f_tmp[:, 0], -1.0, None, ALU.mult).then_inc(f_step, 1)
                dve.wait_ge(f_step, 2)
                dve.tensor_tensor(f_tmp[:, 1], f_tmp[:, 0], f_tmp[:, 1], ALU.min).then_inc(f_step, 1)
                dve.wait_ge(fa_step, 2)
                dve.tensor_scalar(f_tmp[:, 0], f_tmp[:, 0], 0.0, None, ALU.min).then_inc(f_step, 1)
                dve.wait_ge(f_step, 4)
                dve.tensor_tensor(f_tmp[:, 0], f_tmp[:, 0], f_tmp[:, 2], ALU.subtract).then_inc(f_step, 1)
                dve.wait_ge(f_step, 5)
                dve.wait_ge(const_made, 4)
                dve.tensor_tensor_scan(c_row[:, :], f_tmp[:, 0], zeros[:, :], 0.0, ALU.add, ALU.add
                                       ).then_inc(c_done, 1)
                dve.wait_ge(k_raw, 1)
                dve.tensor_tensor(sk_t[:, :], raw[:, :], cos[:, :], ALU.mult).then_inc(kr_step, 1)
                dve.wait_ge(k_rot, 1)
                dve.tensor_tensor(rope_tmp[:, :], s_psum[1][:, :, :].rearrange("p a b -> p (a b)"), sin[:, :],
                                  ALU.mult).then_inc(kr_step, 1)
                dve.wait_ge(kr_step, 2)
                dve.tensor_tensor(sk_t[:, :], sk_t[:, :], rope_tmp[:, :], ALU.add).then_inc(k_ready, 1)

            @block.scalar
            def _(act):
                act.wait_ge(f_step, 3)
                act.activation(f_tmp[:, 2], f_tmp[:, 1], ACT.Exp).then_inc(fa_step, 1)
                act.wait_ge(fa_step, 1)
                act.activation(f_tmp[:, 2], f_tmp[:, 2], ACT.Ln, bias=1.0).then_inc(fa_step, 1)
                act.wait_ge(k_proj, 1)
                act.activation(raw[:, :], s_psum[1][:, :, :].rearrange("p a b -> p (a b)"), ACT.Copy
                               ).then_inc(k_raw, 1)
                act.wait_ge(v_proj, 1)
                for k in range(2):
                    act.activation(sv_rows[:, 4 * k:4 * k + 4].rearrange("p t c -> p (t c)"), t_psum[k][:, :],
                                   ACT.Copy).then_inc(v_ready, 1)
                for n in range(FOX_HEADS):
                    act.wait_ge(bcast_done, n + 1)
                    act.activation(neg_c[:, n], s_psum[n % 2][:, :, :].rearrange("p a b -> p (a b)"), ACT.Copy
                                   ).then_inc(bcast_copied, 1)
                act.wait_ge(bcast_done, FOX_HEADS + 1)
                act.activation(c_col[:, :, :].rearrange("p t h -> p (t h)"), t_psum[0][:, 0:TILES * FOX_HEADS],
                               ACT.Copy).then_inc(bcast_copied, 1)

            @block.tensor
            def _(pe):
                pe.wait_ge(w_first_in, 32)
                pe.wait_ge(x_in, 16 * KD)
                for half in range(2):
                    for c in range(KD):
                        mm = pe.matmul(s_psum[0][0:FOX_HEADS, half], w_f[:, c], xt[:, c, half * 512:half * 512 + 512],
                                       start=(c == 0), stop=(c == KD - 1))
                mm.then_inc(f_psum_done, 1)
                for half in range(2):
                    for c in range(KD):
                        mm = pe.matmul(s_psum[1][:, half], w_kv[:, 0, c], xt[:, c, half * 512:half * 512 + 512],
                                       start=(c == 0), stop=(c == KD - 1))
                mm.then_inc(k_proj, 1)
                for t in range(TILES):
                    for c in range(KD):
                        mm = pe.matmul(t_psum[t // 4][:, t % 4 * P:t % 4 * P + P], xt[:, c, t * P:(t + 1) * P],
                                       w_kv[:, 1, c], start=(c == 0), stop=(c == KD - 1))
                mm.then_inc(v_proj, 1)
                pe.wait_ge(const_in, 16 * 8)
                pe.wait_ge(const_made, 4)
                pe.wait_ge(k_raw, 1)
                for half in range(2):
                    mm = pe.matmul(s_psum[1][:, half], rot[:, :], raw[:, half * 512:half * 512 + 512],
                                   start=True, stop=True)
                mm.then_inc(k_rot, 1)
                pe.wait_ge(c_done, 1)
                for h in range(FOX_HEADS):
                    if h == 1:
                        pe.wait_ge(k_ready, 1)
                    if h >= 2:
                        pe.wait_ge(bcast_copied, h - 1)
                    for half in range(2):
                        mm = pe.matmul(s_psum[h % 2][:, half], minus_row[:, h], c_row[:, half * 512:half * 512 + 512],
                                       start=True, stop=True)
                    mm.then_inc(bcast_done, 1)
                pe.wait_ge(v_ready, 2)
                for t in range(TILES):
                    mm = pe.transpose(t_psum[0][:, t * FOX_HEADS:(t + 1) * FOX_HEADS], c_row[:, t * P:(t + 1) * P],
                                      ident[0:FOX_HEADS, 0:FOX_HEADS])
                mm.then_inc(bcast_done, 1)

        proj_done, proj_copied = sem("proj_done"), sem("proj_copied")
        scores_done, biased, max_done = sem("scores_done"), sem("biased"), sem("max_done")
        exp_done, inv_done, probs_ready = sem("exp_done"), sem("inv_done"), sem("probs_ready")
        turned, turn_copied = sem("turned"), sem("turn_copied")
        pv_done, out_copied = sem("pv_done"), sem("out_copied")
        pair_stored = [sem(f"pair_stored{k}") for k in range(2)]
        UNITS = 2 * TILES

        with nc.Block() as block:
            @block.sync
            def _(sp):
                for pair in range(PAIRS):
                    if pair + 1 < PAIRS:
                        sp.wait_ge(proj_done, 4 * pair + 4)
                        sp.dma_start(w_pair[:, :, :, :], w_fox[pair + 1]).then_inc(w_pair_in, 16)
                    sp.wait_ge(out_copied, UNITS * (pair + 1))
                    sp.dma_start(mixed_t[:, :, pair, :].rearrange("t p n -> p t n"),
                                 pair_out[:, pair % 2].rearrange("p (t n) -> p t n", t=TILES)
                                 ).then_inc(pair_stored[pair % 2], 16)
                for k in range(2):
                    sp.wait_ge(pair_stored[k], 16 * (PAIRS // 2))

            @block.tensor
            def _(pe):
                def scores(pair, u):
                    qb, hh, k = u // 2, u % 2, u % 2
                    length = (qb + 1) * P
                    if u >= 2:
                        pe.wait_ge(biased, UNITS * pair + u - 1)
                    else:
                        pe.wait_ge(proj_copied, 6 * pair + 6)
                    rows = slice(HEAD_DIM * hh, HEAD_DIM * hh + HEAD_DIM)
                    for half in range((length + 511) // 512):
                        n = min(512, length - half * 512)
                        mm = pe.matmul(s_psum[k][:, half, 0:n], q_t[rows, qb * P:(qb + 1) * P],
                                       k_t[rows, half * 512:half * 512 + n], start=True, stop=True)
                    mm = pe.matmul(s_psum[k][:, half, n - P:n], ident16[:, :], masks16[:, P:2 * P],
                                   start=False, stop=True, skip_group_check=True)
                    mm.then_inc(scores_done, 1)

                def turn(pair, u):
                    qb, k = u // 2, u % 2
                    pe.wait_ge(probs_ready, UNITS * pair + u + 1)
                    if u >= 1:
                        pe.wait_ge(turn_copied, UNITS * pair + u)
                    for b in range(qb + 1):
                        mm = pe.transpose(t_psum[b // 4][:, b % 4 * P:b % 4 * P + P], probs[:, k, b * P:(b + 1) * P],
                                          ident[:, :])
                    mm.then_inc(turned, 1)

                def values(pair, u):
                    qb, hh, k = u // 2, u % 2, u % 2
                    rows = slice(HEAD_DIM * hh, HEAD_DIM * hh + HEAD_DIM)
                    pe.wait_ge(turn_copied, UNITS * pair + u + 1)
                    if u >= 2 or past(pair):
                        pe.wait_ge(out_copied, UNITS * pair + u - 1)
                    for b in range(qb + 1):
                        mm = pe.matmul(o_psum[k][rows, 0:P], v_rows[:, b, rows], probs_t[:, k, b * P:(b + 1) * P],
                                       start=(b == 0), stop=(b == qb))
                    mm.then_inc(pv_done, 1)

                def attend(pair):
                    pe.wait_ge(w_pair_in, 16 * pair + 16)
                    for j, psum in ((0, s_psum[0]), (1, s_psum[1])):
                        for half in range(2):
                            for c in range(KD):
                                mm = pe.matmul(psum[:, half], w_pair[:, j, c], xt[:, c, half * 512:half * 512 + 512],
                                               start=(c == 0), stop=(c == KD - 1))
                        mm.then_inc(proj_done, 1)
                    if past(pair):
                        pe.wait_ge(turn_copied, UNITS * pair)
                    for t in range(TILES):
                        for c in range(KD):
                            mm = pe.matmul(t_psum[t // 4][:, t % 4 * P:t % 4 * P + P], xt[:, c, t * P:(t + 1) * P],
                                           w_pair[:, 2, c], start=(c == 0), stop=(c == KD - 1))
                        if t % 4 == 3:
                            mm.then_inc(proj_done, 1)
                    scores(pair, 0)
                    for u in range(UNITS):
                        if u + 1 < UNITS:
                            scores(pair, u + 1)
                        if u >= 1:
                            values(pair, u - 1)
                        turn(pair, u)
                    values(pair, UNITS - 1)

                attend(0)
                with pe.Fori(1, PAIRS) as pair:
                    attend(pair)

            @block.vector
            def _(dve):
                def bias_and_max(pair, u):
                    qb, hh, k = u // 2, u % 2, u % 2
                    length = (qb + 1) * P
                    head = 2 * pair + hh
                    dve.wait_ge(scores_done, UNITS * pair + u + 1)
                    if u >= 2:
                        dve.wait_ge(turned, UNITS * pair + u - 1)
                    dve.scalar_tensor_tensor(
                        probs[:, k, 0:length],
                        neg_c[:, bass.ds(head, 1), 0:length].rearrange("p o n -> p (o n)"),
                        c_col[:, qb, bass.ds(head, 1)],
                        s_psum[k][:, :, :].rearrange("p a b -> p (a b)")[:, 0:length],
                        ALU.add, ALU.add).then_inc(biased, 1)
                    dve.wait_ge(biased, UNITS * pair + u + 1)
                    dve.tensor_reduce(neg_max[:, k, 0:1], probs[:, k, 0:length], AX.X, ALU.max, negate=True
                                      ).then_inc(max_done, 1)

                def normalise(pair, u):
                    qb, k = u // 2, u % 2
                    length = (qb + 1) * P
                    dve.wait_ge(exp_done, UNITS * pair + u + 1)
                    dve.reciprocal(inv_sum[:, k, 0:1], row_sum[:, k, 0:1]).then_inc(inv_done, 1)
                    dve.wait_ge(inv_done, UNITS * pair + u + 1)
                    dve.tensor_scalar(probs[:, k, 0:length], probs[:, k, 0:length], inv_sum[:, k, 0:1], None,
                                      ALU.mult).then_inc(probs_ready, 1)

                def attend(pair):
                    bias_and_max(pair, 0)
                    for u in range(UNITS):
                        if u + 1 < UNITS:
                            bias_and_max(pair, u + 1)
                        normalise(pair, u)

                attend(0)
                with dve.Fori(1, PAIRS) as pair:
                    attend(pair)

            @block.scalar
            def _(act):
                def exponentials(pair, u):
                    qb, k = u // 2, u % 2
                    length = (qb + 1) * P
                    act.wait_ge(max_done, UNITS * pair + u + 1)
                    act.activation(probs[:, k, 0:length], probs[:, k, 0:length], ACT.Exp, bias=neg_max[:, k, 0:1],
                                   accum_out=row_sum[:, k, 0:1]).then_inc(exp_done, 1)

                def copy_turned(pair, u):
                    qb, k = u // 2, u % 2
                    act.wait_ge(turned, UNITS * pair + u + 1)
                    if u >= 2:
                        act.wait_ge(pv_done, UNITS * pair + u - 1)
                    blocks = qb + 1
                    for bank in range((blocks + 3) // 4):
                        n = min(4, blocks - 4 * bank) * P
                        cp = act.activation(probs_t[:, k, bank * 512:bank * 512 + n], t_psum[bank][:, 0:n], ACT.Copy)
                    cp.then_inc(turn_copied, 1)

                def copy_out(pair, kp, u):
                    qb, hh, k = u // 2, u % 2, u % 2
                    rows = slice(HEAD_DIM * hh, HEAD_DIM * hh + HEAD_DIM)
                    act.wait_ge(pv_done, UNITS * pair + u + 1)
                    act.activation(pair_out[rows, kp, qb * P:(qb + 1) * P], o_psum[k][rows, 0:P], ACT.Copy
                                   ).then_inc(out_copied, 1)

                def attend(pair, kp, stored):
                    act.wait_ge(proj_done, 4 * pair + 1)
                    act.activation(q_t[:, :], s_psum[0][:, :, :].rearrange("p a b -> p (a b)"), ACT.Copy, scale=SCALE
                                   ).then_inc(proj_copied, 2)
                    act.wait_ge(proj_done, 4 * pair + 2)
                    act.activation(k_t[:, :], s_psum[1][:, :, :].rearrange("p a b -> p (a b)"), ACT.Copy
                                   ).then_inc(proj_copied, 2)
                    for bank in range(2):
                        act.wait_ge(proj_done, 4 * pair + 3 + bank)
                        act.activation(v_rows[:, 4 * bank:4 * bank + 4].rearrange("p t c -> p (t c)"),
                                       t_psum[bank][:, :], ACT.Copy).then_inc(proj_copied, 1)
                    if past(stored):
                        act.wait_ge(pair_stored[kp], 16 * stored)
                    exponentials(pair, 0)
                    for u in range(UNITS):
                        if u + 1 < UNITS:
                            exponentials(pair, u + 1)
                        if u >= 1:
                            copy_out(pair, kp, u - 1)
                        copy_turned(pair, u)
                    copy_out(pair, kp, UNITS - 1)

                attend(0, 0, 0)
                attend(1, 1, 0)
                with act.Fori(1, PAIRS // 2) as i:
                    attend(2 * i, 0, i)
                    attend(2 * i + 1, 1, i)

        sq_proj, sq_raw, sq_rot, sq_step, sq_ready = (sem("sq_proj"), sem("sq_raw"), sem("sq_rot"),
                                                     sem("sq_step"), sem("sq_ready"))
        sw_scores, sw_max, sw_neg_max = sem("sw_scores"), sem("sw_max"), sem("sw_neg_max")
        sw_gap, sw_exp, sw_sum, sw_inv, sw_probs = (sem("sw_gap"), sem("sw_exp"), sem("sw_sum"),
                                                    sem("sw_inv"), sem("sw_probs"))
        sw_turned, sw_turn_copied = sem("sw_turned"), sem("sw_turn_copied")
        sw_pv, sw_out_copied = sem("sw_pv"), sem("sw_out_copied")
        sw_stored = [sem(f"sw_stored{k}") for k in range(2)]

        with nc.Block() as block:
            @block.sync
            def _(sp):
                for pair in range(PAIRS):
                    if pair + 1 < PAIRS:
                        sp.wait_ge(sq_proj, pair + 1)
                        sp.dma_start(w_sq[:, :, :], w_swa[pair + 1]).then_inc(w_sq_in, 16)
                    sp.wait_ge(sw_out_copied, TILES * (pair + 1))
                    sp.dma_start(mixed_t[:, :, PAIRS + pair, :].rearrange("t p n -> p t n"),
                                 pair_out[:, pair % 2].rearrange("p (t n) -> p t n", t=TILES)
                                 ).then_inc(sw_stored[pair % 2], 16)
                for k in range(2):
                    sp.wait_ge(sw_stored[k], 16 * (PAIRS // 2))

            @block.tensor
            def _(pe):
                def scores(pair, qb):
                    k = qb % 2
                    if qb >= 2:
                        pe.wait_ge(sw_exp, TILES * pair + qb - 1)
                    first = P * max(qb - 1, 0)
                    keys = (qb + 1) * P - first
                    for g in range(2):
                        rows = slice(HEAD_DIM * g, HEAD_DIM * g + HEAD_DIM)
                        pe.matmul(s_psum[k][:, g, 0:keys], q_t[rows, qb * P:(qb + 1) * P],
                                  sk_t[rows, first:first + keys], start=True, stop=True)
                        mm = pe.matmul(s_psum[k][:, g, 0:keys], ident16[:, :], masks16[:, 2 * P - keys:2 * P],
                                       start=False, stop=True, skip_group_check=True)
                    mm.then_inc(sw_scores, 1)

                def turn(pair, qb):
                    k = qb % 2
                    pe.wait_ge(sw_probs, TILES * pair + qb + 1)
                    if qb >= 2 or past(pair):
                        pe.wait_ge(sw_turn_copied, TILES * pair + qb - 1)
                    for n in range(4):
                        if qb == 0 and n % 2:
                            continue
                        mm = pe.transpose(t_psum[k][:, n * P:(n + 1) * P], probs[:, k, n * P:(n + 1) * P], ident[:, :])
                    mm.then_inc(sw_turned, 1)

                def values(pair, qb):
                    k = qb % 2
                    pe.wait_ge(sw_turn_copied, TILES * pair + qb + 1)
                    if qb >= 2 or past(pair):
                        pe.wait_ge(sw_out_copied, TILES * pair + qb - 1)
                    first, blocks = max(qb - 1, 0), min(qb + 1, 2)
                    for g in range(2):
                        rows = slice(HEAD_DIM * g, HEAD_DIM * g + HEAD_DIM)
                        for b in range(blocks):
                            n = (2 * g + b) * P
                            mm = pe.matmul(o_psum[k][rows, 0:P], sv_rows[:, first + b, rows],
                                           probs_t[:, k, n:n + P], start=(b == 0), stop=(b == blocks - 1))
                    mm.then_inc(sw_pv, 1)

                def attend(pair):
                    pe.wait_ge(w_sq_in, 16 * pair + 16)
                    if past(pair):
                        pe.wait_ge(sw_exp, TILES * pair)
                    for half in range(2):
                        for c in range(KD):
                            mm = pe.matmul(s_psum[0][:, half], w_sq[:, c], xt[:, c, half * 512:half * 512 + 512],
                                           start=(c == 0), stop=(c == KD - 1))
                    mm.then_inc(sq_proj, 1)
                    pe.wait_ge(sq_raw, pair + 1)
                    for half in range(2):
                        mm = pe.matmul(s_psum[1][:, half], rot[:, :], raw[:, half * 512:half * 512 + 512],
                                       start=True, stop=True)
                    mm.then_inc(sq_rot, 1)
                    pe.wait_ge(sq_ready, pair + 1)
                    scores(pair, 0)
                    for qb in range(TILES):
                        if qb + 1 < TILES:
                            scores(pair, qb + 1)
                        if qb >= 1:
                            values(pair, qb - 1)
                        turn(pair, qb)
                    values(pair, TILES - 1)

                attend(0)
                with pe.Fori(1, PAIRS) as pair:
                    attend(pair)

            @block.vector
            def _(dve):
                def maxima(pair, qb):
                    k, n = qb % 2, TILES * pair + qb + 1
                    dve.wait_ge(sw_scores, n)
                    if qb >= 2 or past(pair):
                        dve.wait_ge(sw_exp, n - 2)
                    dve.tensor_reduce(neg_max[:, k], s_psum[k][:, :, 0:min(qb + 1, 2) * P], AX.X, ALU.max, negate=True
                                      ).then_inc(sw_max, 1)
                    dve.wait_ge(sw_max, n)
                    dve.tensor_tensor(neg_max[:, k], neg_max[:, k],
                                      neg_sink[:, bass.ds(pair, 1), :].rearrange("p o g -> p (o g)"), ALU.min
                                      ).then_inc(sw_neg_max, 1)
                    dve.wait_ge(sw_neg_max, n)
                    dve.tensor_tensor(sink_exp[:, k], neg_max[:, k],
                                      neg_sink[:, bass.ds(pair, 1), :].rearrange("p o g -> p (o g)"), ALU.subtract
                                      ).then_inc(sw_gap, 1)

                def normalise(pair, qb):
                    k, n = qb % 2, TILES * pair + qb + 1
                    dve.wait_ge(sw_exp, n)
                    dve.tensor_tensor(inv_sum[:, k], row_sum[:, k], sink_exp[:, k], ALU.add).then_inc(sw_sum, 1)
                    dve.wait_ge(sw_sum, n)
                    dve.reciprocal(inv_sum[:, k], inv_sum[:, k]).then_inc(sw_inv, 1)
                    dve.wait_ge(sw_inv, n)
                    for g in range(2):
                        mm = dve.tensor_scalar(probs[:, k, g * 256:g * 256 + min(qb + 1, 2) * P],
                                               probs[:, k, g * 256:g * 256 + min(qb + 1, 2) * P],
                                               inv_sum[:, k, g:g + 1], None, ALU.mult)
                    mm.then_inc(sw_probs, 1)

                def attend(pair):
                    dve.wait_ge(sq_raw, pair + 1)
                    dve.tensor_tensor(q_t[:, :], raw[:, :], cos[:, :], ALU.mult).then_inc(sq_step, 1)
                    dve.wait_ge(sq_rot, pair + 1)
                    dve.tensor_tensor(rope_tmp[:, :], s_psum[1][:, :, :].rearrange("p a b -> p (a b)"), sin[:, :],
                                      ALU.mult).then_inc(sq_step, 1)
                    dve.wait_ge(sq_step, 2 * pair + 2)
                    dve.tensor_tensor(q_t[:, :], q_t[:, :], rope_tmp[:, :], ALU.add).then_inc(sq_ready, 1)
                    maxima(pair, 0)
                    for qb in range(TILES):
                        if qb + 1 < TILES:
                            maxima(pair, qb + 1)
                        normalise(pair, qb)

                attend(0)
                with dve.Fori(1, PAIRS) as pair:
                    attend(pair)

            @block.scalar
            def _(act):
                def exponentials(pair, qb):
                    k, n = qb % 2, TILES * pair + qb + 1
                    act.wait_ge(sw_gap, n)
                    if qb >= 2 or past(pair):
                        act.wait_ge(sw_turned, n - 2)
                    for g in range(2):
                        keys = min(qb + 1, 2) * P
                        act.activation(probs[:, k, g * 256:g * 256 + keys], s_psum[k][:, g, 0:keys],
                                       ACT.Exp, bias=neg_max[:, k, g:g + 1], accum_out=row_sum[:, k, g:g + 1])
                    act.activation(sink_exp[:, k], sink_exp[:, k], ACT.Exp).then_inc(sw_exp, 1)

                def copy_turned(pair, qb):
                    k, n = qb % 2, TILES * pair + qb + 1
                    act.wait_ge(sw_turned, n)
                    if qb >= 2 or past(pair):
                        act.wait_ge(sw_pv, n - 2)
                    keys = min(qb + 1, 2) * P
                    act.activation(probs_t[:, k, 0:512].rearrange("p (g n) -> p g n", g=2)[:, :, 0:keys],
                                   t_psum[k][:, :].rearrange("p (g n) -> p g n", g=2)[:, :, 0:keys],
                                   ACT.Copy).then_inc(sw_turn_copied, 1)

                def copy_out(pair, kp, qb):
                    k = qb % 2
                    act.wait_ge(sw_pv, TILES * pair + qb + 1)
                    act.activation(pair_out[:, kp, qb * P:(qb + 1) * P], o_psum[k][:, 0:P], ACT.Copy
                                   ).then_inc(sw_out_copied, 1)

                def attend(pair, kp, stored):
                    act.wait_ge(sq_proj, pair + 1)
                    act.activation(raw[:, :], s_psum[0][:, :, :].rearrange("p a b -> p (a b)"), ACT.Copy, scale=SCALE
                                   ).then_inc(sq_raw, 1)
                    if past(stored):
                        act.wait_ge(sw_stored[kp], 16 * stored)
                    exponentials(pair, 0)
                    for qb in range(TILES):
                        if qb + 1 < TILES:
                            exponentials(pair, qb + 1)
                        if qb >= 1:
                            copy_out(pair, kp, qb - 1)
                        copy_turned(pair, qb)
                    copy_out(pair, kp, TILES - 1)

                attend(0, 0, 0)
                attend(1, 1, 0)
                with act.Fori(1, PAIRS // 2) as i:
                    attend(2 * i, 0, i)
                    attend(2 * i + 1, 1, i)


def routing_phase(nc, mixed_t, x_rows, w_out, ln1_g, ln1_b, w_query, sub_keys, consts, x1_rows, x1_split, gates):
    with ExitStack() as ctx:
        sem = lambda name: ctx.enter_context(nc.semaphore(name))

        def tiles_in(scope):
            return lambda name, shape, dt=F32: scope.enter_context(nc.sbuf_tensor("rt_" + name, shape, dt))

        sb = tiles_in(ctx)
        w_q = sb("w_q", [P, SETS, KD, P])
        keys = sb("keys", [P, SETS, N_KEYS])
        x1_t = sb("x1_t", [P, KD, SEQ])
        ident = sb("ident", [P, P])
        iota = sb("iota", [P, N_KEYS])
        wide_psum = ctx.enter_context(nc.psum_tensor("wide_psum", [P, D_MODEL], F32))
        t_psum = [ctx.enter_context(nc.psum_tensor(f"r_t_psum{k}", [P, 512], F32)) for k in range(2)]
        s_psum = [ctx.enter_context(nc.psum_tensor(f"r_s_psum{k}", [P, 512], F32)) for k in range(2)]
        g_psum = [ctx.enter_context(nc.psum_tensor(f"g_psum{k}", [P, 4, N_KEYS], F32)) for k in range(2)]
        keys_in, const_in = sem("keys_in"), sem("r_const_in")

        with ExitStack() as scope:
            sb = tiles_in(scope)
            w_o = sb("w_o", [P, KD, D_MODEL])
            mixed = sb("mixed", [P, 2, KD, P])
            rows = sb("rows", [P, 2, D_MODEL])
            split = sb("split", [P, 2, 2, KD, P], BF16)
            ln_g, ln_b = sb("ln_g", [P, D_MODEL]), sb("ln_b", [P, D_MODEL])
            eps = sb("eps", [P, 1])
            stats, moments = sb("stats", [P, 2, 6]), sb("moments", [P, 2])
            std, rstd, newton = sb("std", [P, 1]), sb("rstd", [P, 1]), sb("newton", [P, 1])
            w_o_in, ln_in = sem("w_o_in"), sem("r_ln_in")
            mixed_in = [sem(f"mixed_in{k}") for k in range(2)]
            rows_in = [sem(f"rows_in{k}") for k in range(2)]
            eps_set, mix_done, summed, stats_done = sem("r_eps_set"), sem("mix_done"), sem("summed"), sem("r_stats_done")
            moments_done, std_done, rstd_step = sem("r_moments_done"), sem("r_std_done"), sem("r_rstd_step")
            norm_step, x1_done, turned = sem("norm_step"), sem("x1_done"), sem("r_turned")
            x1_t_ready, hi_ready, lo_ready = sem("x1_t_ready"), sem("hi_ready"), sem("lo_ready")
            x1_stored = [sem(f"x1_stored{k}") for k in range(2)]
            split_stored = [sem(f"split_stored{k}") for k in range(2)]

            with nc.Block() as block:
                @block.sync
                def _(sp):
                    def load(t):
                        k = t % 2
                        if t >= 2:
                            sp.wait_ge(mix_done, t - 1)
                        sp.dma_start(mixed[:, k], mixed_t[t]).then_inc(mixed_in[k], 16)
                        if t >= 2:
                            sp.wait_ge(x1_stored[k], 16 * (t // 2))
                            sp.wait_ge(turned, t - 1)
                        sp.dma_start(rows[:, k], x_rows[t]).then_inc(rows_in[k], 16)

                    load(0)
                    sp.dma_start(w_o[:, :, :], w_out).then_inc(w_o_in, 16)
                    load(1)
                    sp.dma_start(ident[:, :], consts["ident"]).then_inc(const_in, 16)
                    sp.dma_start(iota[:, :], consts["iota"]).then_inc(const_in, 16)
                    sp.dma_start(ln_g[:, :], ln1_g.partition_broadcast(P)).then_inc(ln_in, 16)
                    sp.dma_start(ln_b[:, :], ln1_b.partition_broadcast(P)).then_inc(ln_in, 16)
                    sp.dma_start(w_q[:, :, :, :], w_query).then_inc(keys_in, 16)
                    sp.dma_start(keys[:, :, :], sub_keys).then_inc(keys_in, 16)
                    for t in range(TILES):
                        k = t % 2
                        sp.wait_ge(x1_done, t + 1)
                        sp.dma_start(x1_rows[t], rows[:, k]).then_inc(x1_stored[k], 16)
                        sp.wait_ge(lo_ready, t + 1)
                        sp.dma_start(x1_split[t], split[:, k]).then_inc(split_stored[k], 16)
                        if t + 2 < TILES:
                            load(t + 2)
                    for k in range(2):
                        sp.wait_ge(x1_stored[k], 16 * (TILES // 2))
                        sp.wait_ge(split_stored[k], 16 * (TILES // 2))
                    sp.wait_ge(keys_in, 32)

                @block.tensor
                def _(pe):
                    def mix(t, k, n):
                        pe.wait_ge(mixed_in[k], 16 * n)
                        if past(t):
                            pe.wait_ge(summed, t)
                        for c in range(KD):
                            for half in range(2):
                                mm = pe.matmul(wide_psum[:, half * 512:half * 512 + 512], mixed[:, k, c],
                                               w_o[:, c, half * 512:half * 512 + 512],
                                               start=(c == 0), stop=(c == KD - 1))
                        mm.then_inc(mix_done, 1)

                    def turn(t, k):
                        pe.wait_ge(x1_done, t + 1)
                        if past(t):
                            pe.wait_ge(hi_ready, t)
                        for c in range(KD):
                            mm = pe.transpose(t_psum[c // 4][:, c % 4 * P:c % 4 * P + P],
                                              rows[:, k, c * P:(c + 1) * P], ident[:, :])
                        mm.then_inc(turned, 1)

                    pe.wait_ge(w_o_in, 16)
                    pe.wait_ge(const_in, 32)
                    mix(0, 0, 1)
                    mix(1, 1, 1)
                    turn(0, 0)
                    with pe.Fori(1, TILES // 2) as i:
                        mix(2 * i, 0, i + 1)
                        turn(2 * i - 1, 1)
                        mix(2 * i + 1, 1, i + 1)
                        turn(2 * i, 0)
                    turn(TILES - 1, 1)

                @block.vector
                def _(dve):
                    dve.memset(eps[:, :], LN_EPS).then_inc(eps_set, 1)

                    def normalise(t, k, n):
                        dve.wait_ge(rows_in[k], 16 * n)
                        dve.wait_ge(mix_done, t + 1)
                        dve.scalar_tensor_tensor(rows[:, k], rows[:, k], ALPHA, wide_psum[:, :], ALU.mult, ALU.add
                                                 ).then_inc(summed, 1)
                        dve.wait_ge(summed, t + 1)
                        dve.bn_stats(stats[:, 0], rows[:, k, 0:512])
                        dve.bn_stats(stats[:, 1], rows[:, k, 512:1024]).then_inc(stats_done, 1)
                        dve.wait_ge(stats_done, t + 1)
                        dve.nop(nofuse=True)
                        dve.bn_aggr(moments[:, :], stats[:, :, :]).then_inc(moments_done, 1)
                        newton_rstd(dve, moments[:, :], std[:, :], rstd[:, :], newton[:, :],
                                    moments_done, t + 1, std_done, t + 1, rstd_step, 5 * t)
                        dve.tensor_scalar(rows[:, k], rows[:, k], moments[:, 0:1], rstd[:, :],
                                          ALU.subtract, ALU.mult).then_inc(norm_step, 1)
                        dve.wait_ge(norm_step, 2 * t + 1)
                        dve.tensor_tensor(rows[:, k], rows[:, k], ln_g[:, :], ALU.mult).then_inc(norm_step, 1)
                        dve.wait_ge(norm_step, 2 * t + 2)
                        dve.tensor_tensor(rows[:, k], rows[:, k], ln_b[:, :], ALU.add).then_inc(x1_done, 1)

                    dve.wait_ge(ln_in, 32)
                    with dve.Fori(0, TILES // 2) as i:
                        normalise(2 * i, 0, i + 1)
                        normalise(2 * i + 1, 1, i + 1)

                @block.scalar
                def _(act):
                    def root_and_copies(t, k, stored):
                        act.wait_ge(moments_done, t + 1)
                        act.activation(std[:, :], moments[:, 1:2], ACT.Sqrt, bias=eps[:, :]).then_inc(std_done, 1)
                        act.wait_ge(turned, t + 1)
                        for bank in range(2):
                            cp = act.activation(x1_t[:, 4 * bank:4 * bank + 4, bass.ds(t * P, P)],
                                                t_psum[bank][:, :].rearrange("p (c n) -> p c n", n=P), ACT.Copy)
                        cp.then_inc(x1_t_ready, 1)
                        if past(stored):
                            act.wait_ge(split_stored[k], 16 * stored)
                        for bank in range(2):
                            cp = act.activation(split[:, k, 0, 4 * bank:4 * bank + 4],
                                                t_psum[bank][:, :].rearrange("p (c n) -> p c n", n=P), ACT.Copy)
                        cp.then_inc(hi_ready, 1)

                    act.wait_ge(eps_set, 1)
                    root_and_copies(0, 0, 0)
                    root_and_copies(1, 1, 0)
                    with act.Fori(1, TILES // 2) as i:
                        root_and_copies(2 * i, 0, i)
                        root_and_copies(2 * i + 1, 1, i)

                @block.gpsimd
                def _(pool):
                    def low_half(t, k):
                        pool.wait_ge(x1_t_ready, t + 1)
                        pool.wait_ge(hi_ready, t + 1)
                        pool.tensor_tensor(split[:, k, 1], x1_t[:, :, bass.ds(t * P, P)], split[:, k, 0],
                                           ALU.subtract).then_inc(lo_ready, 1)

                    with pool.Fori(0, TILES // 2) as i:
                        low_half(2 * i, 0)
                        low_half(2 * i + 1, 1)

        sb = tiles_in(ctx)
        q_t = sb("q_t", [P, 2, 4, P])
        scores = sb("scores", [P, SETS, N_KEYS])
        top = sb("top", [P, SETS, TOPK])
        top_u = sb("top_u", [P, SETS, TOPK], U32)
        top_i = sb("top_i", [P, SETS, TOPK])
        cand = sb("cand", [P, PEER_HEADS, TOPK, TOPK])
        best = sb("best", [P, PEER_HEADS, TOPK])
        pos = sb("pos", [P, PEER_HEADS * TOPK], U32)
        pair_u = sb("pair_u", [P, 2, PEER_HEADS * TOPK], U32)
        pair_i = sb("pair_i", [P, 2, PEER_HEADS * TOPK])
        found = sb("found", [P, 2, PEER_HEADS * TOPK, TOPK])
        picked = sb("picked", [P, 3, PEER_HEADS * TOPK])
        gate_sum = sb("gate_sum", [P, PEER_HEADS])
        picked_t = sb("picked_t", [P, 3, P])
        RING = 4
        POOL_HOTS = 3
        hot = sb("hot", [P, RING, 2, 4, N_KEYS])
        lows = sb("lows", [P, 2 * CHUNK])
        stage = sb("stage", [P, 2, N_KEYS, CHUNK])
        q_done, q_copied, s_done, s_copied = sem("q_done"), sem("q_copied"), sem("s_done"), sem("s_copied")
        top_step, floated = sem("top_step"), sem("floated")
        cand_step, pair_step, soft_step, exp_done = sem("cand_step"), sem("pair_step"), sem("soft_step"), sem("r_exp_done")
        find_dve, find_pool, picked_ready = sem("find_dve"), sem("find_pool"), sem("picked_ready")
        picks_turned, picks_copied = sem("picks_turned"), sem("picks_copied")
        hot_dve, hot_pool, summed_gates, g_copied = sem("hot_dve"), sem("hot_pool"), sem("summed_gates"), sem("g_copied")
        stage_stored = [sem(f"stage_stored{k}") for k in range(2)]
        lows_copied = sem("lows_copied")
        BATCHES = P // 4
        PER_BODY = 2 * CHUNK // 4

        with nc.Block() as block:
            @block.sync
            def _(sp):
                for k in range(2):
                    sp.sem_inc(stage_stored[k], 16)
                with sp.Fori(0, SEQ // (2 * CHUNK)) as i:
                    for k in range(2):
                        sp.wait_ge(g_copied, (2 * i + k + 1) * (CHUNK // 4) + 2)
                        sp.dma_start(gates[:, bass.ds(2 * i + k, 1)].rearrange("p o h t -> p (o h t)"),
                                     stage[:, k].rearrange("p h t -> p (h t)")).then_inc(stage_stored[k], 16)
                for k in range(2):
                    sp.wait_ge(stage_stored[k], 16 * (SEQ // (2 * CHUNK) + 1))

            @block.tensor
            def _(pe):
                def queries(t, n):
                    if n < 2:
                        if past(t):
                            pe.wait_ge(q_copied, 4 * t + n - 1)
                    else:
                        pe.wait_ge(q_copied, 4 * t + n - 1)
                    for j in range(4):
                        for c in range(KD):
                            mm = pe.matmul(t_psum[n % 2][:, j * P:(j + 1) * P], w_q[:, 4 * n + j, c],
                                           x1_t[:, c, bass.ds(t * P, P)], start=(c == 0), stop=(c == KD - 1))
                    mm.then_inc(q_done, 1)

                def key_scores(t, n):
                    pe.wait_ge(q_copied, 4 * t + n + 1)
                    if n >= 2 or past(t):
                        pe.wait_ge(s_copied, 4 * t + n - 1)
                    if n == 0 and past(t - 1):
                        pe.wait_ge(picks_copied, t - 1)
                    for j in range(4):
                        mm = pe.matmul(s_psum[n % 2][:, j * P:(j + 1) * P], q_t[:, n % 2, j], keys[:, 4 * n + j],
                                       start=True, stop=True)
                    mm.then_inc(s_done, 1)

                def route(t):
                    queries(t, 0)
                    for n in range(4):
                        if n < 3:
                            queries(t, n + 1)
                        key_scores(t, n)

                def gate_matrix(t):
                    pe.wait_ge(picked_ready, t + 1)
                    pe.wait_ge(s_copied, 4 * t + 3)
                    for j in range(3):
                        mm = pe.transpose(s_psum[0][:, j * P:(j + 1) * P], picked[:, j], ident[:, :])
                    mm.then_inc(picks_turned, 1)
                    with pe.Fori(0, BATCHES // PER_BODY) as i:
                        for m in range(PER_BODY):
                            n = BATCHES * t + PER_BODY * i + m
                            pe.wait_ge(hot_dve, n + 1)
                            pe.wait_ge(hot_pool, n + 2)
                            pe.wait_ge(g_copied, n + 1)
                            for j in range(4):
                                mm = pe.matmul(g_psum[m % 2][:, j], hot[:, m % RING, 0, j], hot[:, m % RING, 1, j],
                                               start=True, stop=True)
                            mm.then_inc(summed_gates, 1)

                pe.sem_inc(summed_gates, RING)
                pe.sem_inc(g_copied, 2)
                pe.sem_inc(picks_turned, 1)
                route(0)
                with pe.Fori(1, TILES) as t:
                    route(t)
                    gate_matrix(t - 1)
                gate_matrix(TILES - 1)

            @block.scalar
            def _(act):
                def copies(t):
                    for n in range(5):
                        if n < 4:
                            act.wait_ge(q_done, 4 * t + n + 1)
                            if n >= 2 or past(t):
                                act.wait_ge(s_done, 4 * t + n - 1)
                            act.activation(q_t[:, n % 2].rearrange("p j n -> p (j n)"), t_psum[n % 2][:, :],
                                           ACT.Copy).then_inc(q_copied, 1)
                        if n >= 1:
                            act.wait_ge(s_done, 4 * t + n)
                            if n == 1 and past(t):
                                act.wait_ge(top_step, 5 * t)
                            act.activation(scores[:, 4 * n - 4:4 * n].rearrange("p j n -> p (j n)"),
                                           s_psum[(n - 1) % 2][:, :], ACT.Copy).then_inc(s_copied, 1)

                def softmax_and_gates(t):
                    act.wait_ge(soft_step, 3 * t + 1)
                    act.activation(best[:, :, :], best[:, :, :], ACT.Exp).then_inc(exp_done, 1)
                    act.wait_ge(picks_turned, t + 2)
                    act.activation(picked_t[:, :, :].rearrange("p j n -> p (j n)"), s_psum[0][:, 0:3 * P], ACT.Copy
                                   ).then_inc(picks_copied, 1)
                    with act.Fori(0, BATCHES // PER_BODY) as i:
                        for m in range(PER_BODY):
                            k = m // (CHUNK // 4)
                            token = m % (CHUNK // 4) * 4
                            act.wait_ge(summed_gates, BATCHES * t + PER_BODY * i + m + 1 + RING)
                            if token == 0:
                                act.wait_ge(stage_stored[k], 16 * ((BATCHES // PER_BODY) * t + i + 1))
                            act.activation(stage[:, k, :, token:token + 4].rearrange("p h t -> p t h"),
                                           g_psum[m % 2][:, :, :], ACT.Copy).then_inc(g_copied, 1)

                copies(0)
                with act.Fori(1, TILES) as t:
                    copies(t)
                    softmax_and_gates(t - 1)
                softmax_and_gates(TILES - 1)

            @block.gpsimd
            def _(pool):
                pool.sem_inc(floated, 1)
                pool.sem_inc(hot_pool, 1)
                with pool.Fori(0, TILES) as t:
                    pool.wait_ge(top_step, 5 * t + 5)
                    pool.nop(nofuse=True)
                    pool.tensor_copy(top_i[:, :, :], top_u[:, :, :]).then_inc(floated, 1)
                    pool.wait_ge(find_dve, 3 * t + 1)
                    pool.wait_ge(floated, t + 2)
                    pool.tensor_tensor(
                        found[:, 1].rearrange("p (h k) a -> p h k a", k=TOPK),
                        found[:, 1].rearrange("p (h k) a -> p h k a", k=TOPK),
                        top_i[:, :, :].rearrange("p (h s) a -> p h s a", s=2)[:, :, 1:2]
                        .broadcast_to([P, PEER_HEADS, TOPK, TOPK]), ALU.mult).then_inc(find_pool, 1)
                    pool.wait_ge(picks_copied, t + 1)
                    pool.nop(nofuse=True)
                    with pool.Fori(0, BATCHES // PER_BODY) as i:
                        pool.wait_ge(hot_pool, BATCHES * t + PER_BODY * i + 1)
                        pool.nop(nofuse=True)
                        pool.tensor_copy(lows[:, :], picked_t[:, 1, bass.ds(4 * PER_BODY * i, 4 * PER_BODY)]
                                         ).then_inc(lows_copied, 1)
                        pool.wait_ge(lows_copied, (BATCHES // PER_BODY) * t + i + 1)
                        pool.nop(nofuse=True)
                        for m in range(PER_BODY):
                            n = BATCHES * t + PER_BODY * i + m
                            pool.wait_ge(summed_gates, n + 1)
                            pool.nop(nofuse=True)
                            for j in range(POOL_HOTS):
                                op = pool.tensor_scalar(hot[:, m % RING, 0, j], iota[:, :],
                                                        lows[:, 4 * m + j:4 * m + j + 1], None, ALU.is_equal)
                            op.then_inc(hot_pool, 1)

            @block.vector
            def _(dve):
                def top_of_sets(t):
                    dve.wait_ge(s_copied, 4 * t + 4)
                    dve.nop(nofuse=True)
                    for s in range(SETS):
                        op = dve.max(top[:, s, 0:8], scores[:, s])
                    op.then_inc(top_step, 1)
                    dve.wait_ge(top_step, 5 * t + 1)
                    dve.wait_ge(floated, t + 1)
                    dve.nop(nofuse=True)
                    for s in range(SETS):
                        op = dve.max_index(top_u[:, s, 0:8], top[:, s, 0:8], scores[:, s])
                    op.then_inc(top_step, 1)
                    dve.wait_ge(top_step, 5 * t + 2)
                    dve.nop(nofuse=True)
                    for s in range(SETS):
                        op = dve.match_replace(scores[:, s], top[:, s, 0:8], scores[:, s], LOW)
                    op.then_inc(top_step, 1)
                    dve.wait_ge(top_step, 5 * t + 3)
                    dve.nop(nofuse=True)
                    for s in range(SETS):
                        op = dve.max(top[:, s, 8:16], scores[:, s])
                    op.then_inc(top_step, 1)
                    dve.wait_ge(top_step, 5 * t + 4)
                    dve.nop(nofuse=True)
                    for s in range(SETS):
                        op = dve.max_index(top_u[:, s, 8:16], top[:, s, 8:16], scores[:, s])
                    op.then_inc(top_step, 1)

                def top_of_products(t):
                    tops = top[:, :, :].rearrange("p (h s) a -> p h s a", s=2)
                    shape = [P, PEER_HEADS, TOPK, TOPK]
                    dve.tensor_tensor(cand[:, :, :, :], tops[:, :, 0].unsqueeze(3).broadcast_to(shape),
                                      tops[:, :, 1:2].broadcast_to(shape), ALU.add).then_inc(cand_step, 1)
                    dve.wait_ge(cand_step, 6 * t + 1)
                    flat = cand[:, :, :, :].rearrange("p h a b -> p h (a b)")
                    dve.nop(nofuse=True)
                    for h in range(PEER_HEADS):
                        op = dve.max(best[:, h, 0:8], flat[:, h])
                    op.then_inc(cand_step, 1)
                    dve.wait_ge(cand_step, 6 * t + 2)
                    dve.nop(nofuse=True)
                    for h in range(PEER_HEADS):
                        op = dve.max_index(pos[:, h * TOPK:h * TOPK + 8], best[:, h, 0:8], flat[:, h])
                    op.then_inc(cand_step, 1)
                    dve.wait_ge(cand_step, 6 * t + 3)
                    dve.nop(nofuse=True)
                    for h in range(PEER_HEADS):
                        op = dve.match_replace(flat[:, h], best[:, h, 0:8], flat[:, h], LOW)
                    op.then_inc(cand_step, 1)
                    dve.wait_ge(cand_step, 6 * t + 4)
                    dve.nop(nofuse=True)
                    for h in range(PEER_HEADS):
                        op = dve.max(best[:, h, 8:16], flat[:, h])
                    op.then_inc(cand_step, 1)
                    dve.wait_ge(cand_step, 6 * t + 5)
                    dve.nop(nofuse=True)
                    for h in range(PEER_HEADS):
                        op = dve.max_index(pos[:, h * TOPK + 8:h * TOPK + 16], best[:, h, 8:16], flat[:, h])
                    op.then_inc(cand_step, 1)
                    dve.wait_ge(cand_step, 6 * t + 6)

                def softmax_and_keys(t):
                    dve.nop(nofuse=True)
                    dve.tensor_copy(gate_sum[:, :], best[:, :, 0]).then_inc(pair_step, 1)
                    dve.tensor_scalar(pair_u[:, 0], pos[:, :], 4, None, ALU.logical_shift_right)
                    dve.tensor_scalar(pair_u[:, 1], pos[:, :], 15, None, ALU.bitwise_and).then_inc(pair_step, 1)
                    dve.wait_ge(pair_step, 4 * t + 1)
                    dve.tensor_tensor(best[:, :, :], best[:, :, :],
                                      gate_sum[:, :].unsqueeze(2).broadcast_to([P, PEER_HEADS, TOPK]),
                                      ALU.subtract).then_inc(soft_step, 1)
                    dve.wait_ge(pair_step, 4 * t + 2)
                    dve.tensor_copy(pair_i[:, 1], pair_u[:, 1])
                    dve.tensor_copy(pair_i[:, 0], pair_u[:, 0]).then_inc(pair_step, 2)
                    dve.wait_ge(pair_step, 4 * t + 4)
                    dve.tensor_tensor(found[:, 1], pair_i[:, 1].unsqueeze(2).broadcast_to([P, P, TOPK]),
                                      iota[:, 0:TOPK].unsqueeze(1).broadcast_to([P, P, TOPK]), ALU.is_equal
                                      ).then_inc(find_dve, 1)
                    dve.tensor_tensor(found[:, 0], pair_i[:, 0].unsqueeze(2).broadcast_to([P, P, TOPK]),
                                      iota[:, 0:TOPK].unsqueeze(1).broadcast_to([P, P, TOPK]), ALU.is_equal
                                      ).then_inc(find_dve, 1)
                    dve.wait_ge(find_dve, 3 * t + 2)
                    dve.wait_ge(floated, t + 2)
                    view = found[:, 0].rearrange("p (h k) a -> p h k a", k=TOPK)
                    dve.tensor_tensor(view, view, top_i[:, :, :].rearrange("p (h s) a -> p h s a", s=2)[:, :, 0:1]
                                      .broadcast_to([P, PEER_HEADS, TOPK, TOPK]), ALU.mult).then_inc(find_dve, 1)
                    dve.wait_ge(exp_done, t + 1)
                    dve.tensor_reduce(gate_sum[:, :], best[:, :, :], AX.X, ALU.add).then_inc(soft_step, 1)
                    dve.wait_ge(find_dve, 3 * t + 3)
                    dve.wait_ge(picks_turned, t + 1)
                    dve.tensor_reduce(picked[:, 0], found[:, 0], AX.X, ALU.add)
                    dve.wait_ge(soft_step, 3 * t + 2)
                    dve.reciprocal(gate_sum[:, :], gate_sum[:, :]).then_inc(soft_step, 1)
                    dve.wait_ge(find_pool, t + 1)
                    dve.tensor_reduce(picked[:, 1], found[:, 1], AX.X, ALU.add)
                    dve.wait_ge(soft_step, 3 * t + 3)
                    dve.tensor_tensor(picked[:, 2].rearrange("p (h k) -> p h k", k=TOPK), best[:, :, :],
                                      gate_sum[:, :].unsqueeze(2).broadcast_to([P, PEER_HEADS, TOPK]),
                                      ALU.mult).then_inc(picked_ready, 1)

                def one_hots(t):
                    dve.wait_ge(picks_copied, t + 1)
                    dve.nop(nofuse=True)
                    with dve.Fori(0, BATCHES // PER_BODY) as i:
                        for m in range(PER_BODY):
                            n = BATCHES * t + PER_BODY * i + m
                            dve.wait_ge(summed_gates, n + 1)
                            for j in range(4):
                                token = 4 * PER_BODY * i + 4 * m + j
                                dve.tensor_scalar(hot[:, m % RING, 1, j], iota[:, :],
                                                  picked_t[:, 0, bass.ds(token, 1)],
                                                  picked_t[:, 2, bass.ds(token, 1)], ALU.is_equal, ALU.mult)
                            for j in range(POOL_HOTS, 4):
                                token = 4 * PER_BODY * i + 4 * m + j
                                op = dve.tensor_scalar(hot[:, m % RING, 0, j], iota[:, :],
                                                       picked_t[:, 1, bass.ds(token, 1)], None, ALU.is_equal)
                            op.then_inc(hot_dve, 1)

                def route(t):
                    top_of_sets(t)
                    top_of_products(t)
                    softmax_and_keys(t)
                    one_hots(t)

                with dve.Fori(0, TILES) as t:
                    route(t)


def expert_phase(nc, u_blocks, v_blocks, gates, x1_rows, x1_split, ln2_g, ln2_b, out, blocks=N_KEYS):
    groups = blocks // GROUP
    with ExitStack() as ctx:
        sb = lambda name, shape, dt: ctx.enter_context(nc.sbuf_tensor(name, shape, dt))
        sem = lambda name: ctx.enter_context(nc.semaphore(name))
        xs = sb("xs", [P, TILES, 2, KD, P], BF16)
        acc = sb("acc", [P, TILES, D_MODEL], F32)
        u_raw = sb("u_raw", [P, 2, KD, P], F32)
        u_split = sb("u_split", [P, 2, 2, KD, P], BF16)
        v_raw = sb("v_raw", [P, 2, D_MODEL], F32)
        v_split = sb("v_split", [P, 2, GROUP, 2, D_MODEL], BF16)
        gate = sb("gate", [P, 2, SEQ // CHUNK, GROUP, CHUNK], F32)
        act_out = sb("act_out", [P, 2, SEQ], F32)
        w_split = sb("w_split", [P, 2, GROUP, 2, SEQ], BF16)
        ln_g = sb("ln2_g_sb", [P, D_MODEL], F32)
        ln_b = sb("ln2_b_sb", [P, D_MODEL], F32)
        stats = sb("c_stats", [P, 2, 6], F32)
        moments = sb("c_moments", [P, TILES, 2], F32)
        eps = sb("c_eps", [P, 1], F32)
        std = sb("c_std", [P, TILES], F32)
        rstd = sb("c_rstd", [P, TILES], F32)
        newton = sb("c_newton", [P, TILES], F32)
        h_psum = [ctx.enter_context(nc.psum_tensor(f"h_psum{k}", [P, SEQ], F32)) for k in range(2)]
        o_psum = [ctx.enter_context(nc.psum_tensor(f"o_psum{k}", [P, D_MODEL], F32)) for k in range(2)]

        xs_in, acc_in, ln_in = sem("xs_in"), sem("acc_in"), sem("ln_in")
        u_in = [sem(f"u_in{k}") for k in range(2)]
        v_in = [sem(f"v_in{k}") for k in range(2)]
        gate_in = [sem(f"gate_in{k}") for k in range(2)]
        u_hi_done, u_lo_done = sem("u_hi_done"), sem("u_lo_done")
        v_hi_done, v_split_done = sem("v_hi_done"), sem("v_split_done")
        h_done, gelu_done = sem("h_done"), sem("gelu_done")
        gated, w_hi_done, w_done = sem("gated"), sem("w_hi_done"), sem("w_done")
        o_done, o_added = sem("o_done"), sem("o_added")
        eps_set, stats_done, moments_done = sem("eps_set"), sem("stats_done2"), sem("moments_done2")
        std_done, rstd_step, centred = sem("std_done2"), sem("rstd_step2"), sem("centred2")
        scaled, rows_done, out_stored = sem("scaled2"), sem("rows_done2"), sem("out_stored")

        last = groups // 2 - 1

        with nc.Block() as block:
            @block.sync
            def _(sp):
                for t in range(TILES):
                    sp.dma_start(xs[:, t], x1_split[t]).then_inc(xs_in, 16)

                def load_u(b, k):
                    sp.dma_start(u_raw[:, k], u_blocks[bass.ds(b, 1)].rearrange("o p (c i) -> p (o c) i", c=KD)
                                 ).then_inc(u_in[k], 16)

                def load_v(b, k):
                    sp.dma_start(v_raw[:, k], v_blocks[bass.ds(b, 1)].rearrange("o p d -> p (o d)")
                                 ).then_inc(v_in[k], 16)

                def load_gate(g, p):
                    sp.dma_start(gate[:, p], gates[:, :, bass.ds(g * GROUP, GROUP), :]).then_inc(gate_in[p], 16)

                load_u(0, 0)
                load_u(1, 1)
                load_gate(0, 0)
                load_v(0, 0)
                load_v(1, 1)
                load_gate(1, 1)
                for t in range(TILES):
                    sp.dma_start(acc[:, t], x1_rows[t]).then_inc(acc_in, 16)
                sp.dma_start(ln_g[:, :], ln2_g.partition_broadcast(P)).then_inc(ln_in, 16)
                sp.dma_start(ln_b[:, :], ln2_b.partition_broadcast(P)).then_inc(ln_in, 16)

                def refill(i, end):
                    for j in range(2 * GROUP):
                        b = 2 * GROUP * i + j
                        if not (end and j >= 2 * GROUP - 2):
                            sp.wait_ge(u_hi_done, b + 1)
                            sp.wait_ge(u_lo_done, b + 1)
                            load_u(b + 2, j % 2)
                            sp.wait_ge(v_split_done, b + 1)
                            load_v(b + 2, j % 2)
                        if j % GROUP == GROUP - 1 and not end:
                            sp.wait_ge(w_done, b + 1)
                            load_gate(2 * i + 2 + j // GROUP, j // GROUP)

                with sp.Fori(0, last) as i:
                    refill(i, False)
                refill(last, True)
                for t in range(TILES):
                    sp.wait_ge(rows_done, t + 1)
                    sp.dma_start(out[t], acc[:, t]).then_inc(out_stored, 16)
                sp.wait_ge(out_stored, 16 * TILES)

            @block.scalar
            def _(act):
                def split_u_hi(b, k, n):
                    act.wait_ge(u_in[k], 16 * n)
                    if past(b - 1):
                        act.wait_ge(h_done, b - 1)
                    act.activation(u_split[:, k, 0], u_raw[:, k], ACT.Copy).then_inc(u_hi_done, 1)

                def gelu(b, k):
                    act.wait_ge(h_done, b + 1)
                    if past(b - 1):
                        act.wait_ge(w_done, b - 1)
                    act.activation(act_out[:, k], h_psum[k][:, :], ACT.Gelu).then_inc(gelu_done, 1)

                def split_v_hi(i, j):
                    p, q = j // GROUP, j % GROUP
                    act.wait_ge(v_in[j % 2], 16 * (GROUP * i + j // 2 + 1))
                    if q == 0 and past(2 * i + p - 1):
                        act.wait_ge(o_done, TILES * (2 * i + p - 1))
                    act.activation(v_split[:, p, q, 0], v_raw[:, j % 2], ACT.Copy).then_inc(v_hi_done, 1)

                def blocks_of(i, end):
                    for j in range(2 * GROUP):
                        b = 2 * GROUP * i + j
                        gelu(b, j % 2)
                        split_v_hi(i, j)
                        if not (end and j >= 2 * GROUP - 2):
                            split_u_hi(b + 2, j % 2, GROUP * i + j // 2 + 2)

                split_u_hi(0, 0, 1)
                split_u_hi(1, 1, 1)
                blocks_of(0, last == 0)
                if last > 1:
                    with act.Fori(1, last) as i:
                        blocks_of(i, False)
                if last > 0:
                    blocks_of(last, True)
                act.wait_ge(eps_set, 1)
                for t in range(TILES):
                    act.wait_ge(moments_done, t + 1)
                    act.activation(std[:, t:t + 1], moments[:, t, 1:2], ACT.Sqrt, bias=eps[:, :]
                                   ).then_inc(std_done, 1)

            @block.gpsimd
            def _(pool):
                def split_u_lo(b, k, n):
                    pool.wait_ge(u_in[k], 16 * n)
                    pool.wait_ge(u_hi_done, b + 1)
                    if past(b - 1):
                        pool.wait_ge(h_done, b - 1)
                    pool.tensor_tensor(u_split[:, k, 1], u_raw[:, k], u_split[:, k, 0], ALU.subtract
                                       ).then_inc(u_lo_done, 1)

                def split_v(i, b, j, n):
                    p, q = j // GROUP, j % GROUP
                    pool.wait_ge(v_in[j % 2], 16 * n)
                    pool.wait_ge(v_hi_done, b + 1)
                    pool.tensor_tensor(v_split[:, p, q, 1], v_raw[:, j % 2], v_split[:, p, q, 0], ALU.subtract
                                       ).then_inc(v_split_done, 1)

                def blocks_of(i, end):
                    for j in range(2 * GROUP):
                        b = 2 * GROUP * i + j
                        n = GROUP * i + j // 2 + 1
                        split_v(i, b, j, n)
                        if not (end and j >= 2 * GROUP - 2):
                            split_u_lo(b + 2, j % 2, n + 1)

                split_u_lo(0, 0, 1)
                split_u_lo(1, 1, 1)
                blocks_of(0, last == 0)
                if last > 1:
                    with pool.Fori(1, last) as i:
                        blocks_of(i, False)
                if last > 0:
                    blocks_of(last, True)
                pool.wait_ge(ln_in, 32)
                for t in range(TILES):
                    pool.wait_ge(centred, t + 1)
                    pool.tensor_tensor(acc[:, t], acc[:, t], ln_g[:, :], ALU.mult).then_inc(scaled, 1)

            @block.vector
            def _(dve):
                dve.memset(eps[:, :], LN_EPS).then_inc(eps_set, 1)

                def gate_and_split(b, g, p, q, n):
                    k = q % 2
                    dve.wait_ge(gelu_done, b + 1)
                    if q == 0:
                        dve.wait_ge(gate_in[p], 16 * n)
                        if past(g - 1):
                            dve.wait_ge(o_done, TILES * (g - 1))
                    rows = act_out[:, k].rearrange("p (c t) -> p c t", t=CHUNK)
                    dve.tensor_tensor(rows, rows, gate[:, p, :, q, :], ALU.mult).then_inc(gated, 1)
                    dve.wait_ge(gated, b + 1)
                    dve.tensor_copy(w_split[:, p, q, 0], act_out[:, k]).then_inc(w_hi_done, 1)
                    dve.wait_ge(w_hi_done, b + 1)
                    dve.tensor_tensor(w_split[:, p, q, 1], act_out[:, k], w_split[:, p, q, 0], ALU.subtract
                                      ).then_inc(w_done, 1)

                def weights_of(g, p, n):
                    for q in range(GROUP):
                        gate_and_split(GROUP * g + q, g, p, q, n)

                def add(g, t, scale):
                    dve.wait_ge(o_done, TILES * g + t + 1)
                    dve.scalar_tensor_tensor(acc[:, t], acc[:, t], scale, o_psum[t % 2][:, :], ALU.mult, ALU.add
                                             ).then_inc(o_added, 1)

                def add_all(g, scale=1.0):
                    for t in range(TILES):
                        add(g, t, scale)

                weights_of(0, 0, 1)
                weights_of(1, 1, 1)
                dve.wait_ge(acc_in, 16 * TILES)
                add_all(0, ALPHA)
                if last > 0:
                    with dve.Fori(0, last) as i:
                        weights_of(2 * i + 2, 0, i + 2)
                        dve.wait_ge(o_added, TILES * (2 * i + 1))
                        add_all(2 * i + 1)
                        weights_of(2 * i + 3, 1, i + 2)
                        dve.wait_ge(o_added, TILES * (2 * i + 2))
                        add_all(2 * i + 2)
                dve.wait_ge(ln_in, 32)

                def finish(t):
                    dve.wait_ge(scaled, t + 1)
                    dve.tensor_tensor(acc[:, t], acc[:, t], ln_b[:, :], ALU.add).then_inc(rows_done, 1)

                for t in range(TILES):
                    add(groups - 1, t, 1.0)
                    dve.wait_ge(o_added, TILES * (groups - 1) + t + 1)
                    dve.bn_stats(stats[:, 0], acc[:, t, 0:512])
                    dve.bn_stats(stats[:, 1], acc[:, t, 512:1024]).then_inc(stats_done, 1)
                    dve.wait_ge(stats_done, t + 1)
                    dve.bn_aggr(moments[:, t], stats[:, :, :]).then_inc(moments_done, 1)
                    if t:
                        finish(t - 1)
                    newton_rstd(dve, moments[:, t], std[:, t:t + 1], rstd[:, t:t + 1], newton[:, t:t + 1],
                                moments_done, t + 1, std_done, t + 1, rstd_step, 5 * t)
                    dve.tensor_scalar(acc[:, t], acc[:, t], moments[:, t, 0:1], rstd[:, t:t + 1],
                                      ALU.subtract, ALU.mult).then_inc(centred, 1)
                finish(TILES - 1)

            @block.tensor
            def _(pe):
                def up(b, k):
                    pe.wait_ge(u_hi_done, b + 1)
                    pe.wait_ge(u_lo_done, b + 1)
                    if past(b - 1):
                        pe.wait_ge(gelu_done, b - 1)
                    for c in range(KD):
                        for part in range(2):
                            for xpart in range(2 - part):
                                for half in range(2):
                                    mm = pe.matmul(
                                        h_psum[k][:, half * 512:half * 512 + 512], u_split[:, k, part, c],
                                        xs[:, half * 4:half * 4 + 4, xpart, c, :],
                                        start=(c == 0 and part == 0 and xpart == 0),
                                        stop=(c == KD - 1 and part == 1))
                    mm.then_inc(h_done, 1)

                def down(g, p):
                    pe.wait_ge(w_done, GROUP * (g + 1))
                    pe.wait_ge(v_split_done, GROUP * (g + 1))
                    for t in range(TILES):
                        if past(TILES * g + t - 1):
                            pe.wait_ge(o_added, TILES * g + t - 1)
                        for q in range(GROUP):
                            for part in range(2):
                                for vpart in range(2 - part):
                                    for half in range(2):
                                        mm = pe.matmul(
                                            o_psum[t % 2][:, half * 512:half * 512 + 512],
                                            w_split[:, p, q, part, t * P:(t + 1) * P],
                                            v_split[:, p, q, vpart, half * 512:half * 512 + 512],
                                            start=(q == 0 and part == 0 and vpart == 0),
                                            stop=(q == GROUP - 1 and part == 1))
                        mm.then_inc(o_done, 1)

                def pair(i, end=False):
                    for q in range(GROUP):
                        up(GROUP * (2 * i + 1) + q, q % 2)
                    down(2 * i, 0)
                    if not end:
                        for q in range(GROUP):
                            up(GROUP * (2 * i + 2) + q, q % 2)
                    down(2 * i + 1, 1)

                pe.wait_ge(xs_in, 16 * TILES)
                for q in range(GROUP):
                    up(q, q % 2)
                pair(0, last == 0)
                if last > 1:
                    with pe.Fori(1, last) as i:
                        pair(i)
                if last > 0:
                    pair(last, True)


def shape_constants():
    token = np.arange(SEQ, dtype=np.float32)
    half = HEAD_DIM // 2
    inv = (10000.0 ** (-(np.arange(half, dtype=np.float32) / half)).astype(np.float64)).astype(np.float32)
    angle = (token[None, :] * inv[:, None]).astype(np.float64)
    rot = np.zeros((P, P), np.float32)
    for d in range(P):
        rot[d + half if d % HEAD_DIM < half else d - half, d] = -1.0 if d % HEAD_DIM < half else 1.0
    minus_row = np.zeros((FOX_HEADS, FOX_HEADS, P), np.float32)
    for h in range(FOX_HEADS):
        minus_row[h, h] = -1.0
    q, k = np.arange(P)[:, None], np.arange(P)[None, :]
    masks = np.concatenate([np.where(k > q, 0.0, LOW), np.where(k <= q, 0.0, LOW)], 1).astype(np.float32)
    return {
        "ident": np.eye(P, dtype=np.float32),
        "rot": rot,
        "minus_row": minus_row,
        "cos": np.tile(np.cos(angle).astype(np.float32), (P // half, 1)),
        "sin": np.tile(np.sin(angle).astype(np.float32), (P // half, 1)),
        "masks": masks,
        "iota": np.tile(np.arange(P, dtype=np.float32), (P, 1)),
    }


def column_blocks(w):
    return np.ascontiguousarray(w.reshape(KD, P, -1, P).transpose(2, 1, 0, 3))


def laid_out(x, w_in, b_forget, swa_sinks, w_out, ln1_g, ln1_b, w_query, sub_keys, expert_u, expert_v,
             ln2_g, ln2_b):
    fox = FOX_HEADS * HEAD_DIM
    w, x = w_in[0], x[0]
    swa = 3 * fox + FOX_HEADS
    skv = swa + SWA_HEADS * HEAD_DIM
    beside = (np.arange(SWA_HEADS * HEAD_DIM).reshape(2, PAIRS, HEAD_DIM).transpose(1, 0, 2)).ravel()
    w_fox = column_blocks(w[:, :3 * fox]).reshape(3, PAIRS, P, KD, P).transpose(1, 2, 0, 3, 4)
    rows = np.concatenate([np.arange(fox), fox + beside])
    return {
        "x_t": np.ascontiguousarray(x.T.reshape(KD, P, SEQ)),
        "x_rows": np.ascontiguousarray(x.reshape(TILES, P, D_MODEL)),
        "w_fox": np.ascontiguousarray(w_fox),
        "w_swa": column_blocks(w[:, swa:skv][:, beside]),
        "w_skv": np.ascontiguousarray(column_blocks(w[:, skv:]).transpose(1, 0, 2, 3)),
        "w_forget": np.ascontiguousarray(w[:, 3 * fox:swa].reshape(KD, P, FOX_HEADS).transpose(1, 0, 2)),
        "b_forget": np.ascontiguousarray(b_forget[0][:, None]),
        "sinks": np.ascontiguousarray(swa_sinks[0].reshape(2, PAIRS).T.ravel()),
        "w_out": np.ascontiguousarray(w_out[0][rows].reshape(KD, P, D_MODEL).transpose(1, 0, 2)),
        "ln1_g": np.ascontiguousarray(ln1_g[0]),
        "ln1_b": np.ascontiguousarray(ln1_b[0]),
        "w_query": np.ascontiguousarray(w_query[0].reshape(KD, P, SETS, P).transpose(1, 2, 0, 3)),
        "sub_keys": np.ascontiguousarray(sub_keys[0].reshape(SETS, N_KEYS, P).transpose(2, 0, 1)),
        "u_blocks": np.ascontiguousarray(
            expert_u[0].reshape(N_KEYS, P, KD, P).transpose(0, 3, 2, 1).reshape(N_KEYS, P, D_MODEL)),
        "v_blocks": np.ascontiguousarray(expert_v[0].reshape(N_KEYS, P, D_MODEL)),
        "ln2_g": np.ascontiguousarray(ln2_g[0]),
        "ln2_b": np.ascontiguousarray(ln2_b[0]),
    }


def build(nc, dram, out):
    mixed_t = nc.dram_tensor("mixed_t", (TILES, P, 2 * PAIRS, P), F32, kind="Internal").ap()
    x1_rows = nc.dram_tensor("x1_rows", (TILES, P, D_MODEL), F32, kind="Internal").ap()
    x1_split = nc.dram_tensor("x1_split", (TILES, P, 2, KD, P), BF16, kind="Internal").ap()
    gates = nc.dram_tensor("gates", (P, SEQ // CHUNK, N_KEYS, CHUNK), F32, kind="Internal").ap()
    attention_phase(nc, dram["x_t"], dram["w_fox"], dram["w_swa"], dram["w_skv"], dram["w_forget"],
                    dram["b_forget"], dram["sinks"], dram, mixed_t)
    routing_phase(nc, mixed_t, dram["x_rows"], dram["w_out"], dram["ln1_g"], dram["ln1_b"], dram["w_query"],
                  dram["sub_keys"], dram, x1_rows, x1_split, gates)
    expert_phase(nc, dram["u_blocks"], dram["v_blocks"], gates, x1_rows, x1_split, dram["ln2_g"], dram["ln2_b"], out)


def kernel(**inputs):
    import concourse.bacc as bacc
    from concourse.bass_utils import run_bass_kernel_spmd

    arrays = laid_out(**{name: np.asarray(a) for name, a in inputs.items()}) | shape_constants()
    nc = bacc.Bacc("TRN2", target_bir_lowering=False, num_devices=1)
    dram = {name: nc.dram_tensor(name, a.shape, F32, kind="ExternalInput").ap() for name, a in arrays.items()}
    out = nc.dram_tensor("out", (TILES, P, D_MODEL), F32, kind="ExternalOutput").ap()
    build(nc, dram, out)
    result = run_bass_kernel_spmd(nc, [arrays], core_ids=[0])
    return result.results[0]["out"].reshape(1, SEQ, D_MODEL)
```

```python
from contextlib import ExitStack

import numpy as np

import concourse.bass as bass
from concourse import mybir

P = 128
D_MODEL = 1024
SEQ = 1024
KD = D_MODEL // P
TILES = SEQ // P
HEAD_DIM = 64
FOX_HEADS = 8
SWA_HEADS = 8
PAIRS = FOX_HEADS // 2
N_KEYS = 128
PEER_HEADS = 8
TOPK = 16
SETS = 2 * PEER_HEADS
CHUNK = 32
GROUP = 4
GATHERED = 2
DENSE = TILES - GATHERED
TOKENS = DENSE * P
STINT = N_KEYS // GROUP // 2 // (2 * GATHERED)
PICKS = PEER_HEADS * TOPK // STINT
RING = 4
LN_EPS = 1e-5
ALPHA = 2.0 ** 0.25
SCALE = HEAD_DIM ** -0.5
LOW = -3.0e38

F32 = mybir.dt.float32
BF16 = mybir.dt.bfloat16
U32 = mybir.dt.uint32
ALU = mybir.AluOpType
ACT = mybir.ActivationFunctionType
AX = mybir.AxisListType


def past(count):
    return not isinstance(count, int) or count > 0


def newton_rstd(dve, moments, std, rstd, tmp, moments_done, n_moments, std_done, n_std, step, n):
    dve.wait_ge(moments_done, n_moments)
    dve.wait_ge(std_done, n_std)
    dve.reciprocal(rstd, std).then_inc(step, 1)
    dve.tensor_scalar(tmp, moments[:, 1:2], LN_EPS, -0.5, ALU.add, ALU.mult).then_inc(step, 1)
    dve.wait_ge(step, n + 2)
    dve.scalar_tensor_tensor(tmp, tmp, rstd, rstd, ALU.mult, ALU.mult).then_inc(step, 1)
    dve.wait_ge(step, n + 3)
    dve.tensor_scalar(tmp, tmp, 1.5, None, ALU.add).then_inc(step, 1)
    dve.wait_ge(step, n + 4)
    dve.tensor_tensor(rstd, rstd, tmp, ALU.mult).then_inc(step, 1)
    dve.wait_ge(step, n + 5)


def attention_phase(nc, x_t, w_fox, w_swa, w_skv, w_forget, b_forget, sinks, consts, mixed_t):
    with ExitStack() as ctx:
        sb = lambda name, shape, dt=F32: ctx.enter_context(nc.sbuf_tensor("att_" + name, shape, dt))
        sem = lambda name: ctx.enter_context(nc.semaphore(name))
        xt = sb("xt", [P, KD, SEQ])
        w_pair = sb("w_pair", [P, 3, KD, P])
        w_sq = sb("w_sq", [P, KD, P])
        w_kv = sb("w_kv", [P, 2, KD, P])
        w_f = sb("w_f", [P, KD, FOX_HEADS])
        ident = sb("a_ident", [P, P])
        rot = sb("rot", [P, P])
        minus_row = sb("minus_row", [FOX_HEADS, FOX_HEADS, P])
        cos = sb("cos", [P, SEQ])
        sin = sb("sin", [P, SEQ])
        ident16 = sb("ident16", [P, P], BF16)
        masks = sb("masks", [P, 2 * P])
        masks16 = sb("masks16", [P, 2 * P], BF16)
        b_f = sb("b_f", [FOX_HEADS, 1])
        sink = sb("sink", [P, PAIRS, 2])
        neg_sink = sb("neg_sink", [P, PAIRS, 2])
        f_tmp = sb("f_tmp", [FOX_HEADS, 3, SEQ])
        c_row = sb("c_row", [FOX_HEADS, SEQ])
        zeros = sb("a_zeros", [FOX_HEADS, SEQ])
        neg_c = sb("neg_c", [P, FOX_HEADS, SEQ])
        c_col = sb("c_col", [P, TILES, FOX_HEADS])
        q_t = sb("q_t", [P, SEQ])
        k_t = sb("k_t", [P, SEQ])
        v_rows = sb("v_rows", [P, TILES, P])
        sk_t = sb("sk_t", [P, SEQ])
        sv_rows = sb("sv_rows", [P, TILES, P])
        raw = sb("raw", [P, SEQ])
        rope_tmp = sb("rope_tmp", [P, SEQ])
        probs = sb("probs", [P, 2, SEQ])
        probs_t = sb("probs_t", [P, 2, SEQ])
        neg_max = sb("neg_max", [P, 2, 2])
        row_sum = sb("row_sum", [P, 2, 2])
        sink_exp = sb("sink_exp", [P, 2, 2])
        inv_sum = sb("inv_sum", [P, 2, 2])
        pair_out = sb("pair_out", [P, 2, SEQ])
        s_psum = [ctx.enter_context(nc.psum_tensor(f"s_psum{k}", [P, 2, 512], F32)) for k in range(2)]
        t_psum = [ctx.enter_context(nc.psum_tensor(f"t_psum{k}", [P, 512], F32)) for k in range(2)]
        o_psum = [ctx.enter_context(nc.psum_tensor(f"a_o_psum{k}", [P, 512], F32)) for k in range(2)]

        x_in, w_first_in, const_in = sem("x_in"), sem("w_first_in"), sem("const_in")
        w_pair_in, w_sq_in = sem("w_pair_in"), sem("w_sq_in")
        const_made = sem("const_made")
        f_psum_done, f_step, c_done = sem("f_psum_done"), sem("f_step"), sem("c_done")
        fa_step = sem("fa_step")
        bcast_done, bcast_copied = sem("bcast_done"), sem("bcast_copied")
        k_proj, k_raw, k_rot, k_ready = sem("k_proj"), sem("k_raw"), sem("k_rot"), sem("k_ready")
        kr_step, v_proj, v_ready = sem("kr_step"), sem("v_proj"), sem("v_ready")

        with nc.Block() as block:
            @block.sync
            def _(sp):
                for c in range(KD):
                    sp.dma_start(xt[:, c], x_t[c]).then_inc(x_in, 16)
                sp.dma_start(w_f[:, :, :], w_forget).then_inc(w_first_in, 16)
                sp.dma_start(w_kv[:, :, :, :], w_skv).then_inc(w_first_in, 16)
                sp.dma_start(b_f[:, :], b_forget).then_inc(const_in, 16)
                sp.dma_start(ident[:, :], consts["ident"]).then_inc(const_in, 16)
                sp.dma_start(rot[:, :], consts["rot"]).then_inc(const_in, 16)
                sp.dma_start(minus_row[:, :, :], consts["minus_row"]).then_inc(const_in, 16)
                sp.dma_start(cos[:, :], consts["cos"]).then_inc(const_in, 16)
                sp.dma_start(sin[:, :], consts["sin"]).then_inc(const_in, 16)
                sp.dma_start(masks[:, :], consts["masks"]).then_inc(const_in, 16)
                sp.dma_start(sink[:, :, :].rearrange("p j g -> p (j g)"), sinks.partition_broadcast(P)
                             ).then_inc(const_in, 16)
                sp.dma_start(w_pair[:, :, :, :], w_fox[0]).then_inc(w_pair_in, 16)
                sp.dma_start(w_sq[:, :, :], w_swa[0]).then_inc(w_sq_in, 16)

            @block.vector
            def _(dve):
                dve.wait_ge(const_in, 16 * 8)
                dve.tensor_copy(ident16[:, :], ident[:, :]).then_inc(const_made, 1)
                dve.tensor_copy(masks16[:, :], masks[:, :]).then_inc(const_made, 1)
                dve.tensor_scalar(neg_sink[:, :, :], sink[:, :, :], -1.0, None, ALU.mult).then_inc(const_made, 1)
                dve.memset(zeros[:, :], 0.0).then_inc(const_made, 1)
                dve.wait_ge(f_psum_done, 1)
                dve.tensor_scalar(f_tmp[:, 0], s_psum[0][0:FOX_HEADS].rearrange("p a b -> p (a b)"),
                                  b_f[:, :], None, ALU.add).then_inc(f_step, 1)
                dve.wait_ge(f_step, 1)
                dve.tensor_scalar(f_tmp[:, 1], f_tmp[:, 0], -1.0, None, ALU.mult).then_inc(f_step, 1)
                dve.wait_ge(f_step, 2)
                dve.tensor_tensor(f_tmp[:, 1], f_tmp[:, 0], f_tmp[:, 1], ALU.min).then_inc(f_step, 1)
                dve.wait_ge(fa_step, 2)
                dve.tensor_scalar(f_tmp[:, 0], f_tmp[:, 0], 0.0, None, ALU.min).then_inc(f_step, 1)
                dve.wait_ge(f_step, 4)
                dve.tensor_tensor(f_tmp[:, 0], f_tmp[:, 0], f_tmp[:, 2], ALU.subtract).then_inc(f_step, 1)
                dve.wait_ge(f_step, 5)
                dve.wait_ge(const_made, 4)
                dve.tensor_tensor_scan(c_row[:, :], f_tmp[:, 0], zeros[:, :], 0.0, ALU.add, ALU.add
                                       ).then_inc(c_done, 1)
                dve.wait_ge(k_raw, 1)
                dve.tensor_tensor(sk_t[:, :], raw[:, :], cos[:, :], ALU.mult).then_inc(kr_step, 1)
                dve.wait_ge(k_rot, 1)
                dve.tensor_tensor(rope_tmp[:, :], s_psum[1][:, :, :].rearrange("p a b -> p (a b)"), sin[:, :],
                                  ALU.mult).then_inc(kr_step, 1)
                dve.wait_ge(kr_step, 2)
                dve.tensor_tensor(sk_t[:, :], sk_t[:, :], rope_tmp[:, :], ALU.add).then_inc(k_ready, 1)

            @block.scalar
            def _(act):
                act.wait_ge(f_step, 3)
                act.activation(f_tmp[:, 2], f_tmp[:, 1], ACT.Exp).then_inc(fa_step, 1)
                act.wait_ge(fa_step, 1)
                act.activation(f_tmp[:, 2], f_tmp[:, 2], ACT.Ln, bias=1.0).then_inc(fa_step, 1)
                act.wait_ge(k_proj, 1)
                act.activation(raw[:, :], s_psum[1][:, :, :].rearrange("p a b -> p (a b)"), ACT.Copy
                               ).then_inc(k_raw, 1)
                act.wait_ge(v_proj, 1)
                for k in range(2):
                    act.activation(sv_rows[:, 4 * k:4 * k + 4].rearrange("p t c -> p (t c)"), t_psum[k][:, :],
                                   ACT.Copy).then_inc(v_ready, 1)
                for n in range(FOX_HEADS):
                    act.wait_ge(bcast_done, n + 1)
                    act.activation(neg_c[:, n], s_psum[n % 2][:, :, :].rearrange("p a b -> p (a b)"), ACT.Copy
                                   ).then_inc(bcast_copied, 1)
                act.wait_ge(bcast_done, FOX_HEADS + 1)
                act.activation(c_col[:, :, :].rearrange("p t h -> p (t h)"), t_psum[0][:, 0:TILES * FOX_HEADS],
                               ACT.Copy).then_inc(bcast_copied, 1)

            @block.tensor
            def _(pe):
                pe.wait_ge(w_first_in, 32)
                pe.wait_ge(x_in, 16 * KD)
                for half in range(2):
                    for c in range(KD):
                        mm = pe.matmul(s_psum[0][0:FOX_HEADS, half], w_f[:, c], xt[:, c, half * 512:half * 512 + 512],
                                       start=(c == 0), stop=(c == KD - 1))
                mm.then_inc(f_psum_done, 1)
                for half in range(2):
                    for c in range(KD):
                        mm = pe.matmul(s_psum[1][:, half], w_kv[:, 0, c], xt[:, c, half * 512:half * 512 + 512],
                                       start=(c == 0), stop=(c == KD - 1))
                mm.then_inc(k_proj, 1)
                for t in range(TILES):
                    for c in range(KD):
                        mm = pe.matmul(t_psum[t // 4][:, t % 4 * P:t % 4 * P + P], xt[:, c, t * P:(t + 1) * P],
                                       w_kv[:, 1, c], start=(c == 0), stop=(c == KD - 1))
                mm.then_inc(v_proj, 1)
                pe.wait_ge(const_in, 16 * 8)
                pe.wait_ge(const_made, 4)
                pe.wait_ge(k_raw, 1)
                for half in range(2):
                    mm = pe.matmul(s_psum[1][:, half], rot[:, :], raw[:, half * 512:half * 512 + 512],
                                   start=True, stop=True)
                mm.then_inc(k_rot, 1)
                pe.wait_ge(c_done, 1)
                for h in range(FOX_HEADS):
                    if h == 1:
                        pe.wait_ge(k_ready, 1)
                    if h >= 2:
                        pe.wait_ge(bcast_copied, h - 1)
                    for half in range(2):
                        mm = pe.matmul(s_psum[h % 2][:, half], minus_row[:, h], c_row[:, half * 512:half * 512 + 512],
                                       start=True, stop=True)
                    mm.then_inc(bcast_done, 1)
                pe.wait_ge(v_ready, 2)
                for t in range(TILES):
                    mm = pe.transpose(t_psum[0][:, t * FOX_HEADS:(t + 1) * FOX_HEADS], c_row[:, t * P:(t + 1) * P],
                                      ident[0:FOX_HEADS, 0:FOX_HEADS])
                mm.then_inc(bcast_done, 1)

        proj_done, proj_copied = sem("proj_done"), sem("proj_copied")
        scores_done, biased, max_done = sem("scores_done"), sem("biased"), sem("max_done")
        exp_done, inv_done, probs_ready = sem("exp_done"), sem("inv_done"), sem("probs_ready")
        turned, turn_copied = sem("turned"), sem("turn_copied")
        pv_done, out_copied = sem("pv_done"), sem("out_copied")
        pair_stored = [sem(f"pair_stored{k}") for k in range(2)]
        UNITS = 2 * TILES

        with nc.Block() as block:
            @block.sync
            def _(sp):
                for pair in range(PAIRS):
                    if pair + 1 < PAIRS:
                        sp.wait_ge(proj_done, 4 * pair + 4)
                        sp.dma_start(w_pair[:, :, :, :], w_fox[pair + 1]).then_inc(w_pair_in, 16)
                    sp.wait_ge(out_copied, UNITS * (pair + 1))
                    sp.dma_start(mixed_t[:, :, pair, :].rearrange("t p n -> p t n"),
                                 pair_out[:, pair % 2].rearrange("p (t n) -> p t n", t=TILES)
                                 ).then_inc(pair_stored[pair % 2], 16)
                for k in range(2):
                    sp.wait_ge(pair_stored[k], 16 * (PAIRS // 2))

            @block.tensor
            def _(pe):
                def scores(pair, u):
                    qb, hh, k = u // 2, u % 2, u % 2
                    length = (qb + 1) * P
                    if u >= 2:
                        pe.wait_ge(biased, UNITS * pair + u - 1)
                    else:
                        pe.wait_ge(proj_copied, 6 * pair + 6)
                    rows = slice(HEAD_DIM * hh, HEAD_DIM * hh + HEAD_DIM)
                    for half in range((length + 511) // 512):
                        n = min(512, length - half * 512)
                        mm = pe.matmul(s_psum[k][:, half, 0:n], q_t[rows, qb * P:(qb + 1) * P],
                                       k_t[rows, half * 512:half * 512 + n], start=True, stop=True)
                    mm = pe.matmul(s_psum[k][:, half, n - P:n], ident16[:, :], masks16[:, P:2 * P],
                                   start=False, stop=True, skip_group_check=True)
                    mm.then_inc(scores_done, 1)

                def turn(pair, u):
                    qb, k = u // 2, u % 2
                    pe.wait_ge(probs_ready, UNITS * pair + u + 1)
                    if u >= 1:
                        pe.wait_ge(turn_copied, UNITS * pair + u)
                    for b in range(qb + 1):
                        mm = pe.transpose(t_psum[b // 4][:, b % 4 * P:b % 4 * P + P], probs[:, k, b * P:(b + 1) * P],
                                          ident[:, :])
                    mm.then_inc(turned, 1)

                def values(pair, u):
                    qb, hh, k = u // 2, u % 2, u % 2
                    rows = slice(HEAD_DIM * hh, HEAD_DIM * hh + HEAD_DIM)
                    pe.wait_ge(turn_copied, UNITS * pair + u + 1)
                    if u >= 2 or past(pair):
                        pe.wait_ge(out_copied, UNITS * pair + u - 1)
                    for b in range(qb + 1):
                        mm = pe.matmul(o_psum[k][rows, 0:P], v_rows[:, b, rows], probs_t[:, k, b * P:(b + 1) * P],
                                       start=(b == 0), stop=(b == qb))
                    mm.then_inc(pv_done, 1)

                def attend(pair):
                    pe.wait_ge(w_pair_in, 16 * pair + 16)
                    for j, psum in ((0, s_psum[0]), (1, s_psum[1])):
                        for half in range(2):
                            for c in range(KD):
                                mm = pe.matmul(psum[:, half], w_pair[:, j, c], xt[:, c, half * 512:half * 512 + 512],
                                               start=(c == 0), stop=(c == KD - 1))
                        mm.then_inc(proj_done, 1)
                    if past(pair):
                        pe.wait_ge(turn_copied, UNITS * pair)
                    for t in range(TILES):
                        for c in range(KD):
                            mm = pe.matmul(t_psum[t // 4][:, t % 4 * P:t % 4 * P + P], xt[:, c, t * P:(t + 1) * P],
                                           w_pair[:, 2, c], start=(c == 0), stop=(c == KD - 1))
                        if t % 4 == 3:
                            mm.then_inc(proj_done, 1)
                    scores(pair, 0)
                    for u in range(UNITS):
                        if u + 1 < UNITS:
                            scores(pair, u + 1)
                        if u >= 1:
                            values(pair, u - 1)
                        turn(pair, u)
                    values(pair, UNITS - 1)

                attend(0)
                with pe.Fori(1, PAIRS) as pair:
                    attend(pair)

            @block.vector
            def _(dve):
                def bias_and_max(pair, u):
                    qb, hh, k = u // 2, u % 2, u % 2
                    length = (qb + 1) * P
                    head = 2 * pair + hh
                    dve.wait_ge(scores_done, UNITS * pair + u + 1)
                    if u >= 2:
                        dve.wait_ge(turned, UNITS * pair + u - 1)
                    dve.scalar_tensor_tensor(
                        probs[:, k, 0:length],
                        neg_c[:, bass.ds(head, 1), 0:length].rearrange("p o n -> p (o n)"),
                        c_col[:, qb, bass.ds(head, 1)],
                        s_psum[k][:, :, :].rearrange("p a b -> p (a b)")[:, 0:length],
                        ALU.add, ALU.add).then_inc(biased, 1)
                    dve.wait_ge(biased, UNITS * pair + u + 1)
                    dve.tensor_reduce(neg_max[:, k, 0:1], probs[:, k, 0:length], AX.X, ALU.max, negate=True
                                      ).then_inc(max_done, 1)

                def normalise(pair, u):
                    qb, k = u // 2, u % 2
                    length = (qb + 1) * P
                    dve.wait_ge(exp_done, UNITS * pair + u + 1)
                    dve.reciprocal(inv_sum[:, k, 0:1], row_sum[:, k, 0:1]).then_inc(inv_done, 1)
                    dve.wait_ge(inv_done, UNITS * pair + u + 1)
                    dve.tensor_scalar(probs[:, k, 0:length], probs[:, k, 0:length], inv_sum[:, k, 0:1], None,
                                      ALU.mult).then_inc(probs_ready, 1)

                def attend(pair):
                    bias_and_max(pair, 0)
                    for u in range(UNITS):
                        if u + 1 < UNITS:
                            bias_and_max(pair, u + 1)
                        normalise(pair, u)

                attend(0)
                with dve.Fori(1, PAIRS) as pair:
                    attend(pair)

            @block.scalar
            def _(act):
                def exponentials(pair, u):
                    qb, k = u // 2, u % 2
                    length = (qb + 1) * P
                    act.wait_ge(max_done, UNITS * pair + u + 1)
                    act.activation(probs[:, k, 0:length], probs[:, k, 0:length], ACT.Exp, bias=neg_max[:, k, 0:1],
                                   accum_out=row_sum[:, k, 0:1]).then_inc(exp_done, 1)

                def copy_turned(pair, u):
                    qb, k = u // 2, u % 2
                    act.wait_ge(turned, UNITS * pair + u + 1)
                    if u >= 2:
                        act.wait_ge(pv_done, UNITS * pair + u - 1)
                    blocks = qb + 1
                    for bank in range((blocks + 3) // 4):
                        n = min(4, blocks - 4 * bank) * P
                        cp = act.activation(probs_t[:, k, bank * 512:bank * 512 + n], t_psum[bank][:, 0:n], ACT.Copy)
                    cp.then_inc(turn_copied, 1)

                def copy_out(pair, kp, u):
                    qb, hh, k = u // 2, u % 2, u % 2
                    rows = slice(HEAD_DIM * hh, HEAD_DIM * hh + HEAD_DIM)
                    act.wait_ge(pv_done, UNITS * pair + u + 1)
                    act.activation(pair_out[rows, kp, qb * P:(qb + 1) * P], o_psum[k][rows, 0:P], ACT.Copy
                                   ).then_inc(out_copied, 1)

                def attend(pair, kp, stored):
                    act.wait_ge(proj_done, 4 * pair + 1)
                    act.activation(q_t[:, :], s_psum[0][:, :, :].rearrange("p a b -> p (a b)"), ACT.Copy, scale=SCALE
                                   ).then_inc(proj_copied, 2)
                    act.wait_ge(proj_done, 4 * pair + 2)
                    act.activation(k_t[:, :], s_psum[1][:, :, :].rearrange("p a b -> p (a b)"), ACT.Copy
                                   ).then_inc(proj_copied, 2)
                    for bank in range(2):
                        act.wait_ge(proj_done, 4 * pair + 3 + bank)
                        act.activation(v_rows[:, 4 * bank:4 * bank + 4].rearrange("p t c -> p (t c)"),
                                       t_psum[bank][:, :], ACT.Copy).then_inc(proj_copied, 1)
                    if past(stored):
                        act.wait_ge(pair_stored[kp], 16 * stored)
                    exponentials(pair, 0)
                    for u in range(UNITS):
                        if u + 1 < UNITS:
                            exponentials(pair, u + 1)
                        if u >= 1:
                            copy_out(pair, kp, u - 1)
                        copy_turned(pair, u)
                    copy_out(pair, kp, UNITS - 1)

                attend(0, 0, 0)
                attend(1, 1, 0)
                with act.Fori(1, PAIRS // 2) as i:
                    attend(2 * i, 0, i)
                    attend(2 * i + 1, 1, i)

        sq_proj, sq_raw, sq_rot, sq_step, sq_ready = (sem("sq_proj"), sem("sq_raw"), sem("sq_rot"),
                                                     sem("sq_step"), sem("sq_ready"))
        sw_scores, sw_max, sw_neg_max = sem("sw_scores"), sem("sw_max"), sem("sw_neg_max")
        sw_gap, sw_exp, sw_sum, sw_inv, sw_probs = (sem("sw_gap"), sem("sw_exp"), sem("sw_sum"),
                                                    sem("sw_inv"), sem("sw_probs"))
        sw_turned, sw_turn_copied = sem("sw_turned"), sem("sw_turn_copied")
        sw_pv, sw_out_copied = sem("sw_pv"), sem("sw_out_copied")
        sw_stored = [sem(f"sw_stored{k}") for k in range(2)]

        with nc.Block() as block:
            @block.sync
            def _(sp):
                for pair in range(PAIRS):
                    if pair + 1 < PAIRS:
                        sp.wait_ge(sq_proj, pair + 1)
                        sp.dma_start(w_sq[:, :, :], w_swa[pair + 1]).then_inc(w_sq_in, 16)
                    sp.wait_ge(sw_out_copied, TILES * (pair + 1))
                    sp.dma_start(mixed_t[:, :, PAIRS + pair, :].rearrange("t p n -> p t n"),
                                 pair_out[:, pair % 2].rearrange("p (t n) -> p t n", t=TILES)
                                 ).then_inc(sw_stored[pair % 2], 16)
                for k in range(2):
                    sp.wait_ge(sw_stored[k], 16 * (PAIRS // 2))

            @block.tensor
            def _(pe):
                def scores(pair, qb):
                    k = qb % 2
                    if qb >= 2:
                        pe.wait_ge(sw_exp, TILES * pair + qb - 1)
                    first = P * max(qb - 1, 0)
                    keys = (qb + 1) * P - first
                    for g in range(2):
                        rows = slice(HEAD_DIM * g, HEAD_DIM * g + HEAD_DIM)
                        pe.matmul(s_psum[k][:, g, 0:keys], q_t[rows, qb * P:(qb + 1) * P],
                                  sk_t[rows, first:first + keys], start=True, stop=True)
                        mm = pe.matmul(s_psum[k][:, g, 0:keys], ident16[:, :], masks16[:, 2 * P - keys:2 * P],
                                       start=False, stop=True, skip_group_check=True)
                    mm.then_inc(sw_scores, 1)

                def turn(pair, qb):
                    k = qb % 2
                    pe.wait_ge(sw_probs, TILES * pair + qb + 1)
                    if qb >= 2 or past(pair):
                        pe.wait_ge(sw_turn_copied, TILES * pair + qb - 1)
                    for n in range(4):
                        if qb == 0 and n % 2:
                            continue
                        mm = pe.transpose(t_psum[k][:, n * P:(n + 1) * P], probs[:, k, n * P:(n + 1) * P], ident[:, :])
                    mm.then_inc(sw_turned, 1)

                def values(pair, qb):
                    k = qb % 2
                    pe.wait_ge(sw_turn_copied, TILES * pair + qb + 1)
                    if qb >= 2 or past(pair):
                        pe.wait_ge(sw_out_copied, TILES * pair + qb - 1)
                    first, blocks = max(qb - 1, 0), min(qb + 1, 2)
                    for g in range(2):
                        rows = slice(HEAD_DIM * g, HEAD_DIM * g + HEAD_DIM)
                        for b in range(blocks):
                            n = (2 * g + b) * P
                            mm = pe.matmul(o_psum[k][rows, 0:P], sv_rows[:, first + b, rows],
                                           probs_t[:, k, n:n + P], start=(b == 0), stop=(b == blocks - 1))
                    mm.then_inc(sw_pv, 1)

                def attend(pair):
                    pe.wait_ge(w_sq_in, 16 * pair + 16)
                    if past(pair):
                        pe.wait_ge(sw_exp, TILES * pair)
                    for half in range(2):
                        for c in range(KD):
                            mm = pe.matmul(s_psum[0][:, half], w_sq[:, c], xt[:, c, half * 512:half * 512 + 512],
                                           start=(c == 0), stop=(c == KD - 1))
                    mm.then_inc(sq_proj, 1)
                    pe.wait_ge(sq_raw, pair + 1)
                    for half in range(2):
                        mm = pe.matmul(s_psum[1][:, half], rot[:, :], raw[:, half * 512:half * 512 + 512],
                                       start=True, stop=True)
                    mm.then_inc(sq_rot, 1)
                    pe.wait_ge(sq_ready, pair + 1)
                    scores(pair, 0)
                    for qb in range(TILES):
                        if qb + 1 < TILES:
                            scores(pair, qb + 1)
                        if qb >= 1:
                            values(pair, qb - 1)
                        turn(pair, qb)
                    values(pair, TILES - 1)

                attend(0)
                with pe.Fori(1, PAIRS) as pair:
                    attend(pair)

            @block.vector
            def _(dve):
                def maxima(pair, qb):
                    k, n = qb % 2, TILES * pair + qb + 1
                    dve.wait_ge(sw_scores, n)
                    if qb >= 2 or past(pair):
                        dve.wait_ge(sw_exp, n - 2)
                    dve.tensor_reduce(neg_max[:, k], s_psum[k][:, :, 0:min(qb + 1, 2) * P], AX.X, ALU.max, negate=True
                                      ).then_inc(sw_max, 1)
                    dve.wait_ge(sw_max, n)
                    dve.tensor_tensor(neg_max[:, k], neg_max[:, k],
                                      neg_sink[:, bass.ds(pair, 1), :].rearrange("p o g -> p (o g)"), ALU.min
                                      ).then_inc(sw_neg_max, 1)
                    dve.wait_ge(sw_neg_max, n)
                    dve.tensor_tensor(sink_exp[:, k], neg_max[:, k],
                                      neg_sink[:, bass.ds(pair, 1), :].rearrange("p o g -> p (o g)"), ALU.subtract
                                      ).then_inc(sw_gap, 1)

                def normalise(pair, qb):
                    k, n = qb % 2, TILES * pair + qb + 1
                    dve.wait_ge(sw_exp, n)
                    dve.tensor_tensor(inv_sum[:, k], row_sum[:, k], sink_exp[:, k], ALU.add).then_inc(sw_sum, 1)
                    dve.wait_ge(sw_sum, n)
                    dve.reciprocal(inv_sum[:, k], inv_sum[:, k]).then_inc(sw_inv, 1)
                    dve.wait_ge(sw_inv, n)
                    for g in range(2):
                        mm = dve.tensor_scalar(probs[:, k, g * 256:g * 256 + min(qb + 1, 2) * P],
                                               probs[:, k, g * 256:g * 256 + min(qb + 1, 2) * P],
                                               inv_sum[:, k, g:g + 1], None, ALU.mult)
                    mm.then_inc(sw_probs, 1)

                def attend(pair):
                    dve.wait_ge(sq_raw, pair + 1)
                    dve.tensor_tensor(q_t[:, :], raw[:, :], cos[:, :], ALU.mult).then_inc(sq_step, 1)
                    dve.wait_ge(sq_rot, pair + 1)
                    dve.tensor_tensor(rope_tmp[:, :], s_psum[1][:, :, :].rearrange("p a b -> p (a b)"), sin[:, :],
                                      ALU.mult).then_inc(sq_step, 1)
                    dve.wait_ge(sq_step, 2 * pair + 2)
                    dve.tensor_tensor(q_t[:, :], q_t[:, :], rope_tmp[:, :], ALU.add).then_inc(sq_ready, 1)
                    maxima(pair, 0)
                    for qb in range(TILES):
                        if qb + 1 < TILES:
                            maxima(pair, qb + 1)
                        normalise(pair, qb)

                attend(0)
                with dve.Fori(1, PAIRS) as pair:
                    attend(pair)

            @block.scalar
            def _(act):
                def exponentials(pair, qb):
                    k, n = qb % 2, TILES * pair + qb + 1
                    act.wait_ge(sw_gap, n)
                    if qb >= 2 or past(pair):
                        act.wait_ge(sw_turned, n - 2)
                    for g in range(2):
                        keys = min(qb + 1, 2) * P
                        act.activation(probs[:, k, g * 256:g * 256 + keys], s_psum[k][:, g, 0:keys],
                                       ACT.Exp, bias=neg_max[:, k, g:g + 1], accum_out=row_sum[:, k, g:g + 1])
                    act.activation(sink_exp[:, k], sink_exp[:, k], ACT.Exp).then_inc(sw_exp, 1)

                def copy_turned(pair, qb):
                    k, n = qb % 2, TILES * pair + qb + 1
                    act.wait_ge(sw_turned, n)
                    if qb >= 2 or past(pair):
                        act.wait_ge(sw_pv, n - 2)
                    keys = min(qb + 1, 2) * P
                    act.activation(probs_t[:, k, 0:512].rearrange("p (g n) -> p g n", g=2)[:, :, 0:keys],
                                   t_psum[k][:, :].rearrange("p (g n) -> p g n", g=2)[:, :, 0:keys],
                                   ACT.Copy).then_inc(sw_turn_copied, 1)

                def copy_out(pair, kp, qb):
                    k = qb % 2
                    act.wait_ge(sw_pv, TILES * pair + qb + 1)
                    act.activation(pair_out[:, kp, qb * P:(qb + 1) * P], o_psum[k][:, 0:P], ACT.Copy
                                   ).then_inc(sw_out_copied, 1)

                def attend(pair, kp, stored):
                    act.wait_ge(sq_proj, pair + 1)
                    act.activation(raw[:, :], s_psum[0][:, :, :].rearrange("p a b -> p (a b)"), ACT.Copy, scale=SCALE
                                   ).then_inc(sq_raw, 1)
                    if past(stored):
                        act.wait_ge(sw_stored[kp], 16 * stored)
                    exponentials(pair, 0)
                    for qb in range(TILES):
                        if qb + 1 < TILES:
                            exponentials(pair, qb + 1)
                        if qb >= 1:
                            copy_out(pair, kp, qb - 1)
                        copy_turned(pair, qb)
                    copy_out(pair, kp, TILES - 1)

                attend(0, 0, 0)
                attend(1, 1, 0)
                with act.Fori(1, PAIRS // 2) as i:
                    attend(2 * i, 0, i)
                    attend(2 * i + 1, 1, i)


def routing_phase(nc, mixed_t, x_rows, w_out, ln1_g, ln1_b, w_query, sub_keys, consts, x1_rows, x1_split, gates,
                  pick_index, pick_gate):
    with ExitStack() as ctx:
        sem = lambda name: ctx.enter_context(nc.semaphore(name))

        def tiles_in(scope):
            return lambda name, shape, dt=F32: scope.enter_context(nc.sbuf_tensor("rt_" + name, shape, dt))

        sb = tiles_in(ctx)
        w_q = sb("w_q", [P, SETS, KD, P])
        keys = sb("keys", [P, SETS, N_KEYS])
        x1_t = sb("x1_t", [P, KD, SEQ])
        ident = sb("ident", [P, P])
        iota = sb("iota", [P, N_KEYS])
        wide_psum = ctx.enter_context(nc.psum_tensor("wide_psum", [P, D_MODEL], F32))
        t_psum = [ctx.enter_context(nc.psum_tensor(f"r_t_psum{k}", [P, 512], F32)) for k in range(2)]
        s_psum = [ctx.enter_context(nc.psum_tensor(f"r_s_psum{k}", [P, 512], F32)) for k in range(2)]
        g_psum = [ctx.enter_context(nc.psum_tensor(f"g_psum{k}", [P, 4, N_KEYS], F32)) for k in range(2)]
        keys_in, const_in = sem("keys_in"), sem("r_const_in")

        with ExitStack() as scope:
            sb = tiles_in(scope)
            w_o = sb("w_o", [P, KD, D_MODEL])
            mixed = sb("mixed", [P, 2, KD, P])
            rows = sb("rows", [P, 2, D_MODEL])
            split = sb("split", [P, 2, 2, KD, P], BF16)
            ln_g, ln_b = sb("ln_g", [P, D_MODEL]), sb("ln_b", [P, D_MODEL])
            eps = sb("eps", [P, 1])
            stats, moments = sb("stats", [P, 2, 6]), sb("moments", [P, 2])
            std, rstd, newton = sb("std", [P, 1]), sb("rstd", [P, 1]), sb("newton", [P, 1])
            w_o_in, ln_in = [sem(f"w_o_in{k}") for k in range(4)], sem("r_ln_in")
            mixed_in = [sem(f"mixed_in{k}") for k in range(2)]
            rows_in = [sem(f"rows_in{k}") for k in range(2)]
            eps_set, mix_done, summed, stats_done = sem("r_eps_set"), sem("mix_done"), sem("summed"), sem("r_stats_done")
            moments_done, std_done, rstd_step = sem("r_moments_done"), sem("r_std_done"), sem("r_rstd_step")
            norm_step, x1_done, turned = sem("norm_step"), sem("x1_done"), sem("r_turned")
            x1_t_ready, hi_ready, lo_ready = sem("x1_t_ready"), sem("hi_ready"), sem("lo_ready")
            x1_stored = [sem(f"x1_stored{k}") for k in range(2)]
            split_stored = [sem(f"split_stored{k}") for k in range(2)]

            with nc.Block() as block:
                @block.sync
                def _(sp):
                    def load_mixed(t):
                        sp.dma_start(mixed[:, t % 2], mixed_t[t]).then_inc(mixed_in[t % 2], 16)

                    def load_rows(t):
                        sp.dma_start(rows[:, t % 2], x_rows[t]).then_inc(rows_in[t % 2], 16)

                    load_mixed(0)
                    for c in range(KD):
                        sp.dma_start(w_o[:, c], w_out[:, c]).then_inc(w_o_in[c % 4], 16)
                    load_rows(0)
                    sp.dma_start(ln_g[:, :], ln1_g.partition_broadcast(P)).then_inc(ln_in, 16)
                    sp.dma_start(ln_b[:, :], ln1_b.partition_broadcast(P)).then_inc(ln_in, 16)
                    load_mixed(1)
                    load_rows(1)
                    sp.dma_start(ident[:, :], consts["ident"]).then_inc(const_in, 16)
                    sp.dma_start(iota[:, :], consts["iota"]).then_inc(const_in, 16)
                    for t in range(TILES):
                        k = t % 2
                        if t + 2 < TILES:
                            sp.wait_ge(mix_done, t + 1)
                            load_mixed(t + 2)
                        sp.wait_ge(x1_done, t + 1)
                        sp.dma_start(x1_rows[t], rows[:, k]).then_inc(x1_stored[k], 16)
                        sp.dma_start(w_q[:, 2 * t:2 * t + 2], w_query[:, 2 * t:2 * t + 2]).then_inc(keys_in, 16)
                        if t + 2 < TILES:
                            sp.wait_ge(x1_stored[k], 16 * (t // 2 + 1))
                            sp.wait_ge(turned, t + 1)
                            load_rows(t + 2)
                        sp.wait_ge(lo_ready, t + 1)
                        sp.dma_start(x1_split[t], split[:, k]).then_inc(split_stored[k], 16)
                    sp.dma_start(keys[:, :, :], sub_keys).then_inc(keys_in, 16)
                    for k in range(2):
                        sp.wait_ge(x1_stored[k], 16 * (TILES // 2))
                        sp.wait_ge(split_stored[k], 16 * (TILES // 2))
                    sp.wait_ge(keys_in, 16 * (TILES + 1))

                @block.tensor
                def _(pe):
                    def mix(t, k, n):
                        pe.wait_ge(mixed_in[k], 16 * n)
                        if past(t):
                            pe.wait_ge(summed, t)
                        for c in range(KD):
                            for half in range(2):
                                mm = pe.matmul(wide_psum[:, half * 512:half * 512 + 512], mixed[:, k, c],
                                               w_o[:, c, half * 512:half * 512 + 512],
                                               start=(c == 0), stop=(c == KD - 1))
                        mm.then_inc(mix_done, 1)

                    def turn(t, k):
                        pe.wait_ge(x1_done, t + 1)
                        if past(t):
                            pe.wait_ge(hi_ready, t)
                        for c in range(KD):
                            mm = pe.transpose(t_psum[c // 4][:, c % 4 * P:c % 4 * P + P],
                                              rows[:, k, c * P:(c + 1) * P], ident[:, :])
                        mm.then_inc(turned, 1)

                    for k in range(4):
                        pe.wait_ge(w_o_in[k], 32)
                    mix(0, 0, 1)
                    pe.wait_ge(const_in, 32)
                    mix(1, 1, 1)
                    turn(0, 0)
                    with pe.Fori(1, TILES // 2) as i:
                        mix(2 * i, 0, i + 1)
                        turn(2 * i - 1, 1)
                        mix(2 * i + 1, 1, i + 1)
                        turn(2 * i, 0)
                    turn(TILES - 1, 1)

                @block.vector
                def _(dve):
                    dve.memset(eps[:, :], LN_EPS).then_inc(eps_set, 1)

                    def normalise(t, k, n):
                        dve.wait_ge(rows_in[k], 16 * n)
                        dve.wait_ge(mix_done, t + 1)
                        dve.scalar_tensor_tensor(rows[:, k], rows[:, k], ALPHA, wide_psum[:, :], ALU.mult, ALU.add
                                                 ).then_inc(summed, 1)
                        dve.wait_ge(summed, t + 1)
                        dve.bn_stats(stats[:, 0], rows[:, k, 0:512])
                        dve.bn_stats(stats[:, 1], rows[:, k, 512:1024]).then_inc(stats_done, 1)
                        dve.wait_ge(stats_done, t + 1)
                        dve.nop(nofuse=True)
                        dve.bn_aggr(moments[:, :], stats[:, :, :]).then_inc(moments_done, 1)
                        newton_rstd(dve, moments[:, :], std[:, :], rstd[:, :], newton[:, :],
                                    moments_done, t + 1, std_done, t + 1, rstd_step, 5 * t)
                        dve.tensor_scalar(rows[:, k], rows[:, k], moments[:, 0:1], rstd[:, :],
                                          ALU.subtract, ALU.mult).then_inc(norm_step, 1)
                        dve.wait_ge(norm_step, 2 * t + 1)
                        dve.tensor_tensor(rows[:, k], rows[:, k], ln_g[:, :], ALU.mult).then_inc(norm_step, 1)
                        dve.wait_ge(norm_step, 2 * t + 2)
                        dve.tensor_tensor(rows[:, k], rows[:, k], ln_b[:, :], ALU.add).then_inc(x1_done, 1)

                    dve.wait_ge(ln_in, 32)
                    with dve.Fori(0, TILES // 2) as i:
                        normalise(2 * i, 0, i + 1)
                        normalise(2 * i + 1, 1, i + 1)

                @block.scalar
                def _(act):
                    def root_and_copies(t, k, stored):
                        act.wait_ge(moments_done, t + 1)
                        act.activation(std[:, :], moments[:, 1:2], ACT.Sqrt, bias=eps[:, :]).then_inc(std_done, 1)
                        act.wait_ge(turned, t + 1)
                        for bank in range(2):
                            cp = act.activation(x1_t[:, 4 * bank:4 * bank + 4, bass.ds(t * P, P)],
                                                t_psum[bank][:, :].rearrange("p (c n) -> p c n", n=P), ACT.Copy)
                        cp.then_inc(x1_t_ready, 1)
                        if past(stored):
                            act.wait_ge(split_stored[k], 16 * stored)
                        for bank in range(2):
                            cp = act.activation(split[:, k, 0, 4 * bank:4 * bank + 4],
                                                t_psum[bank][:, :].rearrange("p (c n) -> p c n", n=P), ACT.Copy)
                        cp.then_inc(hi_ready, 1)

                    act.wait_ge(eps_set, 1)
                    root_and_copies(0, 0, 0)
                    root_and_copies(1, 1, 0)
                    with act.Fori(1, TILES // 2) as i:
                        root_and_copies(2 * i, 0, i)
                        root_and_copies(2 * i + 1, 1, i)

                @block.gpsimd
                def _(pool):
                    def low_half(t, k):
                        pool.wait_ge(x1_t_ready, t + 1)
                        pool.wait_ge(hi_ready, t + 1)
                        pool.tensor_tensor(split[:, k, 1], x1_t[:, :, bass.ds(t * P, P)], split[:, k, 0],
                                           ALU.subtract).then_inc(lo_ready, 1)

                    with pool.Fori(0, TILES // 2) as i:
                        low_half(2 * i, 0)
                        low_half(2 * i + 1, 1)

        sb = tiles_in(ctx)
        q_t = sb("q_t", [P, 2, 4, P])
        scores = sb("scores", [P, SETS, N_KEYS])
        top = sb("top", [P, SETS, TOPK])
        top_u = sb("top_u", [P, SETS, TOPK], U32)
        top_i = sb("top_i", [P, SETS, TOPK], BF16)
        cand = sb("cand", [P, PEER_HEADS, TOPK, TOPK])
        best = sb("best", [P, PEER_HEADS, TOPK])
        pos = sb("pos", [P, PEER_HEADS * TOPK], U32)
        pair_u = sb("pair_u", [P, 2, PEER_HEADS * TOPK], U32)
        pair_i = sb("pair_i", [P, 2, PEER_HEADS * TOPK], BF16)
        found = sb("found", [P, 2, PEER_HEADS * TOPK, TOPK], BF16)
        picked = sb("picked", [P, 3, PEER_HEADS * TOPK])
        gate_sum = sb("gate_sum", [P, PEER_HEADS])
        picked_t = sb("picked_t", [P, 4, P], BF16)
        gate_t = sb("gate_t", [P, P])
        HOTS = 2
        BATCH = 8
        hot = sb("hot", [P, HOTS, 4, N_KEYS, BATCH], BF16)
        key_table = sb("key_table", [P, N_KEYS, BATCH], BF16)
        stage = sb("stage", [P, 2, N_KEYS, CHUNK])
        q_done, q_copied, s_done, s_copied = sem("q_done"), sem("q_copied"), sem("s_done"), sem("s_copied")
        top_step, floated = sem("top_step"), sem("floated")
        cand_step, pair_step, soft_step, exp_done = sem("cand_step"), sem("pair_step"), sem("soft_step"), sem("r_exp_done")
        find_dve, find_pool, picked_ready = sem("find_dve"), sem("find_pool"), sem("picked_ready")
        table_made, high_made, gate_split, kept = sem("table_made"), sem("high_made"), sem("gate_split"), sem("kept")
        picks_turned, picks_copied = sem("picks_turned"), sem("picks_copied")
        hot_dve, hot_pool, summed_gates, g_copied = sem("hot_dve"), sem("hot_pool"), sem("summed_gates"), sem("g_copied")
        stage_stored = [sem(f"stage_stored{k}") for k in range(2)]
        BATCHES = P // BATCH
        PER_BODY = 2 * CHUNK // BATCH
        BODIES = BATCHES // PER_BODY

        with nc.Block() as block:
            @block.sync
            def _(sp):
                for k in range(2):
                    sp.sem_inc(stage_stored[k], 16)
                with sp.Fori(0, DENSE * BODIES) as i:
                    for k in range(2):
                        sp.wait_ge(g_copied, (2 * i + k + 1) * (CHUNK // 4) + 2)
                        sp.dma_start(gates[:, bass.ds(2 * i + k, 1)].rearrange("p o h t -> p (o h t)"),
                                     stage[:, k].rearrange("p h t -> p (h t)")).then_inc(stage_stored[k], 16)
                for k in range(2):
                    sp.wait_ge(stage_stored[k], 16 * (DENSE * BODIES + 1))

            @block.tensor
            def _(pe):
                def queries(t, n):
                    if n < 2:
                        if past(t):
                            pe.wait_ge(q_copied, 4 * t + n - 1)
                    else:
                        pe.wait_ge(q_copied, 4 * t + n - 1)
                    for j in range(4):
                        for c in range(KD):
                            mm = pe.matmul(t_psum[n % 2][:, j * P:(j + 1) * P], w_q[:, 4 * n + j, c],
                                           x1_t[:, c, bass.ds(t * P, P)], start=(c == 0), stop=(c == KD - 1))
                    mm.then_inc(q_done, 1)

                def key_scores(t, n):
                    pe.wait_ge(q_copied, 4 * t + n + 1)
                    if n >= 2 or past(t):
                        pe.wait_ge(s_copied, 4 * t + n - 1)
                    if n == 0 and past(t - GATHERED - 1):
                        pe.wait_ge(picks_copied, t - GATHERED - 1)
                    for j in range(4):
                        mm = pe.matmul(s_psum[n % 2][:, j * P:(j + 1) * P], q_t[:, n % 2, j], keys[:, 4 * n + j],
                                       start=True, stop=True)
                    mm.then_inc(s_done, 1)

                def route(t):
                    queries(t, 0)
                    for n in range(4):
                        if n < 3:
                            queries(t, n + 1)
                        key_scores(t, n)

                def gate_matrix(d):
                    pe.wait_ge(picked_ready, GATHERED + d + 1)
                    pe.wait_ge(s_copied, 4 * (GATHERED + d) + 3)
                    for j in range(3):
                        mm = pe.transpose(s_psum[0][:, j * P:(j + 1) * P], picked[:, j], ident[:, :])
                    mm.then_inc(picks_turned, 1)
                    with pe.Fori(0, BODIES) as i:
                        for m in range(PER_BODY):
                            n = BATCHES * d + PER_BODY * i + m
                            pe.wait_ge(hot_dve, n + 1)
                            pe.wait_ge(hot_pool, n + 1)
                            for four in range(BATCH // 4):
                                pe.wait_ge(g_copied, 2 * n + four + 1)
                                for j in range(4 * four, 4 * four + 4):
                                    for part in range(2):
                                        mm = pe.matmul(g_psum[four % 2][:, j % 4], hot[:, m % HOTS, 0, :, j],
                                                       hot[:, m % HOTS, 2 + part, :, j],
                                                       start=(part == 0), stop=(part == 1))
                                mm.then_inc(summed_gates, 1)

                pe.sem_inc(summed_gates, 2 * HOTS)
                pe.sem_inc(g_copied, 2)
                pe.sem_inc(picks_turned, 1)
                for t in range(GATHERED + 1):
                    route(t)
                with pe.Fori(1, DENSE) as d:
                    route(GATHERED + d)
                    gate_matrix(d - 1)
                gate_matrix(DENSE - 1)

            @block.scalar
            def _(act):
                def copies(t):
                    for n in range(5):
                        if n < 4:
                            act.wait_ge(q_done, 4 * t + n + 1)
                            if n >= 2 or past(t):
                                act.wait_ge(s_done, 4 * t + n - 1)
                            act.activation(q_t[:, n % 2].rearrange("p j n -> p (j n)"), t_psum[n % 2][:, :],
                                           ACT.Copy).then_inc(q_copied, 1)
                        if n >= 1:
                            act.wait_ge(s_done, 4 * t + n)
                            if n == 1 and past(t):
                                act.wait_ge(top_step, 5 * t)
                            act.activation(scores[:, 4 * n - 4:4 * n].rearrange("p j n -> p (j n)"),
                                           s_psum[(n - 1) % 2][:, :], ACT.Copy).then_inc(s_copied, 1)

                def softmax(t):
                    act.wait_ge(soft_step, 3 * t + 1)
                    act.activation(best[:, :, :], best[:, :, :], ACT.Exp).then_inc(exp_done, 1)

                def copy_gates(d):
                    act.wait_ge(picks_turned, d + 2)
                    act.activation(picked_t[:, 0:2].rearrange("p j n -> p (j n)"), s_psum[0][:, 0:2 * P], ACT.Copy)
                    act.activation(gate_t[:, :], s_psum[0][:, 2 * P:3 * P], ACT.Copy)
                    act.activation(picked_t[:, 2], s_psum[0][:, 2 * P:3 * P], ACT.Copy).then_inc(picks_copied, 1)
                    with act.Fori(0, BODIES) as i:
                        for m in range(2 * PER_BODY):
                            k = m // (CHUNK // 4)
                            token = m % (CHUNK // 4) * 4
                            act.wait_ge(summed_gates, 2 * (BATCHES * d + PER_BODY * i) + m + 1 + 2 * HOTS)
                            if token == 0:
                                act.wait_ge(stage_stored[k], 16 * (BODIES * d + i + 1))
                            act.activation(stage[:, k, :, token:token + 4].rearrange("p h t -> p t h"),
                                           g_psum[m % 2][:, :, :], ACT.Copy).then_inc(g_copied, 1)

                copies(0)
                for t in range(1, GATHERED + 1):
                    copies(t)
                    softmax(t - 1)
                with act.Fori(1, DENSE) as d:
                    copies(GATHERED + d)
                    softmax(GATHERED + d - 1)
                    copy_gates(d - 1)
                softmax(TILES - 1)
                copy_gates(DENSE - 1)

            @block.gpsimd
            def _(pool):
                def low_key(t):
                    pool.wait_ge(top_step, 5 * t + 5)
                    pool.nop(nofuse=True)
                    pool.tensor_copy(top_i[:, :, :], top_u[:, :, :]).then_inc(floated, 1)
                    pool.wait_ge(find_dve, 3 * t + 1)
                    pool.wait_ge(floated, t + 2)
                    pool.tensor_tensor(
                        found[:, 1].rearrange("p (h k) a -> p h k a", k=TOPK),
                        found[:, 1].rearrange("p (h k) a -> p h k a", k=TOPK),
                        top_i[:, :, :].rearrange("p (h s) a -> p h s a", s=2)[:, :, 1:2]
                        .broadcast_to([P, PEER_HEADS, TOPK, TOPK]), ALU.mult).then_inc(find_pool, 1)

                def low_halves(d):
                    pool.wait_ge(picks_copied, d + 1)
                    pool.tensor_tensor(picked_t[:, 3], gate_t[:, :], picked_t[:, 2], ALU.subtract
                                       ).then_inc(gate_split, 1)
                    pool.wait_ge(gate_split, d + 1)
                    pool.nop(nofuse=True)
                    with pool.Fori(0, BODIES) as i:
                        for m in range(PER_BODY):
                            n = BATCHES * d + PER_BODY * i + m
                            pool.wait_ge(high_made, n + 1)
                            pool.wait_ge(summed_gates, 2 * n + 2)
                            pool.nop(nofuse=True)
                            pool.tensor_tensor(
                                hot[:, m % HOTS, 3], hot[:, m % HOTS, 1],
                                picked_t[:, 3, bass.ds(BATCH * (PER_BODY * i + m), BATCH)].unsqueeze(1)
                                .broadcast_to([P, N_KEYS, BATCH]), ALU.mult).then_inc(hot_pool, 1)

                pool.sem_inc(floated, 1)
                for t in range(GATHERED):
                    low_key(t)
                with pool.Fori(0, DENSE) as d:
                    low_key(GATHERED + d)
                    low_halves(d)

            @block.vector
            def _(dve):
                def top_of_sets(t):
                    dve.wait_ge(s_copied, 4 * t + 4)
                    dve.nop(nofuse=True)
                    for s in range(SETS):
                        op = dve.max(top[:, s, 0:8], scores[:, s])
                    op.then_inc(top_step, 1)
                    dve.wait_ge(top_step, 5 * t + 1)
                    dve.wait_ge(floated, t + 1)
                    dve.nop(nofuse=True)
                    for s in range(SETS):
                        op = dve.max_index(top_u[:, s, 0:8], top[:, s, 0:8], scores[:, s])
                    op.then_inc(top_step, 1)
                    dve.wait_ge(top_step, 5 * t + 2)
                    dve.nop(nofuse=True)
                    for s in range(SETS):
                        op = dve.match_replace(scores[:, s], top[:, s, 0:8], scores[:, s], LOW)
                    op.then_inc(top_step, 1)
                    dve.wait_ge(top_step, 5 * t + 3)
                    dve.nop(nofuse=True)
                    for s in range(SETS):
                        op = dve.max(top[:, s, 8:16], scores[:, s])
                    op.then_inc(top_step, 1)
                    dve.wait_ge(top_step, 5 * t + 4)
                    dve.nop(nofuse=True)
                    for s in range(SETS):
                        op = dve.max_index(top_u[:, s, 8:16], top[:, s, 8:16], scores[:, s])
                    op.then_inc(top_step, 1)

                def top_of_products(t):
                    tops = top[:, :, :].rearrange("p (h s) a -> p h s a", s=2)
                    shape = [P, PEER_HEADS, TOPK, TOPK]
                    dve.tensor_tensor(cand[:, :, :, :], tops[:, :, 0].unsqueeze(3).broadcast_to(shape),
                                      tops[:, :, 1:2].broadcast_to(shape), ALU.add).then_inc(cand_step, 1)
                    dve.wait_ge(cand_step, 6 * t + 1)
                    flat = cand[:, :, :, :].rearrange("p h a b -> p h (a b)")
                    dve.nop(nofuse=True)
                    for h in range(PEER_HEADS):
                        op = dve.max(best[:, h, 0:8], flat[:, h])
                    op.then_inc(cand_step, 1)
                    dve.wait_ge(cand_step, 6 * t + 2)
                    dve.nop(nofuse=True)
                    for h in range(PEER_HEADS):
                        op = dve.max_index(pos[:, h * TOPK:h * TOPK + 8], best[:, h, 0:8], flat[:, h])
                    op.then_inc(cand_step, 1)
                    dve.wait_ge(cand_step, 6 * t + 3)
                    dve.nop(nofuse=True)
                    for h in range(PEER_HEADS):
                        op = dve.match_replace(flat[:, h], best[:, h, 0:8], flat[:, h], LOW)
                    op.then_inc(cand_step, 1)
                    dve.wait_ge(cand_step, 6 * t + 4)
                    dve.nop(nofuse=True)
                    for h in range(PEER_HEADS):
                        op = dve.max(best[:, h, 8:16], flat[:, h])
                    op.then_inc(cand_step, 1)
                    dve.wait_ge(cand_step, 6 * t + 5)
                    dve.nop(nofuse=True)
                    for h in range(PEER_HEADS):
                        op = dve.max_index(pos[:, h * TOPK + 8:h * TOPK + 16], best[:, h, 8:16], flat[:, h])
                    op.then_inc(cand_step, 1)
                    dve.wait_ge(cand_step, 6 * t + 6)

                def softmax_and_keys(t):
                    dve.nop(nofuse=True)
                    dve.tensor_copy(gate_sum[:, :], best[:, :, 0]).then_inc(pair_step, 1)
                    dve.tensor_scalar(pair_u[:, 0], pos[:, :], 4, None, ALU.logical_shift_right)
                    dve.tensor_scalar(pair_u[:, 1], pos[:, :], 15, None, ALU.bitwise_and).then_inc(pair_step, 1)
                    dve.wait_ge(pair_step, 4 * t + 1)
                    dve.tensor_tensor(best[:, :, :], best[:, :, :],
                                      gate_sum[:, :].unsqueeze(2).broadcast_to([P, PEER_HEADS, TOPK]),
                                      ALU.subtract).then_inc(soft_step, 1)
                    dve.wait_ge(pair_step, 4 * t + 2)
                    dve.tensor_copy(pair_i[:, 1], pair_u[:, 1])
                    dve.tensor_copy(pair_i[:, 0], pair_u[:, 0]).then_inc(pair_step, 2)
                    dve.wait_ge(pair_step, 4 * t + 4)
                    dve.tensor_tensor(found[:, 1], pair_i[:, 1].unsqueeze(2).broadcast_to([P, P, TOPK]),
                                      iota[:, 0:TOPK].unsqueeze(1).broadcast_to([P, P, TOPK]), ALU.is_equal
                                      ).then_inc(find_dve, 1)
                    dve.tensor_tensor(found[:, 0], pair_i[:, 0].unsqueeze(2).broadcast_to([P, P, TOPK]),
                                      iota[:, 0:TOPK].unsqueeze(1).broadcast_to([P, P, TOPK]), ALU.is_equal
                                      ).then_inc(find_dve, 1)
                    dve.wait_ge(find_dve, 3 * t + 2)
                    dve.wait_ge(floated, t + 2)
                    view = found[:, 0].rearrange("p (h k) a -> p h k a", k=TOPK)
                    dve.tensor_tensor(view, view, top_i[:, :, :].rearrange("p (h s) a -> p h s a", s=2)[:, :, 0:1]
                                      .broadcast_to([P, PEER_HEADS, TOPK, TOPK]), ALU.mult).then_inc(find_dve, 1)
                    dve.wait_ge(exp_done, t + 1)
                    dve.tensor_reduce(gate_sum[:, :], best[:, :, :], AX.X, ALU.add).then_inc(soft_step, 1)
                    dve.wait_ge(find_dve, 3 * t + 3)
                    if past(t - GATHERED):
                        dve.wait_ge(picks_turned, t - GATHERED + 1)
                    dve.tensor_reduce(picked[:, 0], found[:, 0], AX.X, ALU.add)
                    dve.wait_ge(soft_step, 3 * t + 2)
                    dve.reciprocal(gate_sum[:, :], gate_sum[:, :]).then_inc(soft_step, 1)
                    dve.wait_ge(find_pool, t + 1)
                    dve.tensor_reduce(picked[:, 1], found[:, 1], AX.X, ALU.add)
                    dve.wait_ge(soft_step, 3 * t + 3)
                    dve.tensor_tensor(picked[:, 2].rearrange("p (h k) -> p h k", k=TOPK), best[:, :, :],
                                      gate_sum[:, :].unsqueeze(2).broadcast_to([P, PEER_HEADS, TOPK]),
                                      ALU.mult).then_inc(picked_ready, 1)

                def keep_picks(t):
                    dve.wait_ge(picked_ready, t + 1)
                    dve.scalar_tensor_tensor(pick_index[:, t], picked[:, 0], float(N_KEYS), picked[:, 1],
                                             ALU.mult, ALU.add)
                    dve.tensor_copy(pick_gate[:, t], picked[:, 2]).then_inc(kept, 1)

                def one_hots(d):
                    dve.wait_ge(picks_copied, d + 1)
                    dve.nop(nofuse=True)
                    with dve.Fori(0, BODIES) as i:
                        for m in range(PER_BODY):
                            n = BATCHES * d + PER_BODY * i + m
                            slot = m % HOTS

                            def of_batch(j):
                                return (picked_t[:, j, bass.ds(BATCH * (PER_BODY * i + m), BATCH)].unsqueeze(1)
                                        .broadcast_to([P, N_KEYS, BATCH]))

                            dve.wait_ge(summed_gates, 2 * n + 2)
                            dve.tensor_tensor(hot[:, slot, 1], key_table[:, :, :], of_batch(0), ALU.is_equal
                                              ).then_inc(high_made, 1)
                            dve.tensor_tensor(hot[:, slot, 0], key_table[:, :, :], of_batch(1), ALU.is_equal)
                            dve.wait_ge(high_made, n + 1)
                            dve.tensor_tensor(hot[:, slot, 2], hot[:, slot, 1], of_batch(2), ALU.mult
                                              ).then_inc(hot_dve, 1)

                def pick(t):
                    top_of_sets(t)
                    top_of_products(t)
                    softmax_and_keys(t)

                dve.tensor_copy(key_table[:, :, :], iota[:, :].unsqueeze(2).broadcast_to([P, N_KEYS, BATCH])
                                ).then_inc(table_made, 1)
                dve.wait_ge(table_made, 1)
                for t in range(GATHERED):
                    pick(t)
                    keep_picks(t)
                dve.wait_ge(kept, GATHERED)
                with dve.Fori(0, DENSE) as d:
                    pick(GATHERED + d)
                    one_hots(d)


def expert_phase(nc, u_blocks, v_blocks, u_rows, v_rows, gates, x1_rows, x1_split, ln2_g, ln2_b, out,
                 pick_index, pick_gate):
    groups = N_KEYS // GROUP
    with ExitStack() as ctx:
        sb = lambda name, shape, dt: ctx.enter_context(nc.sbuf_tensor(name, shape, dt))
        sem = lambda name: ctx.enter_context(nc.semaphore(name))
        xs = sb("xs", [P, DENSE, 2, KD, P], BF16)
        acc = sb("acc", [P, TILES, D_MODEL], F32)
        u_raw = sb("u_raw", [P, 2, KD, P], F32)
        u_split = sb("u_split", [P, 2, 2, KD, P], BF16)
        v_raw = sb("v_raw", [P, 2, D_MODEL], F32)
        v_split = sb("v_split", [P, 2, GROUP, 2, D_MODEL], BF16)
        gate = sb("gate", [P, 2, TOKENS // CHUNK, GROUP, CHUNK], F32)
        act_out = sb("act_out", [P, 2, TOKENS], F32)
        w_split = sb("w_split", [P, 2, GROUP, 2, TOKENS], BF16)
        ln_g = sb("ln2_g_sb", [P, D_MODEL], F32)
        ln_b = sb("ln2_b_sb", [P, D_MODEL], F32)
        fetched = sb("fetched", [P, RING, D_MODEL], F32)
        index_now = sb("index_now", [P, PICKS], U32)
        gate_now = sb("gate_now", [P, PICKS], F32)
        dots = sb("dots", [P, PICKS], F32)
        dots_all = sb("dots_all", [P, STINT * PICKS], F32)
        stats = sb("c_stats", [P, 2, 6], F32)
        moments = sb("c_moments", [P, TILES, 2], F32)
        eps = sb("c_eps", [P, 1], F32)
        std = sb("c_std", [P, TILES], F32)
        rstd = sb("c_rstd", [P, TILES], F32)
        newton = sb("c_newton", [P, TILES], F32)
        h_psum = [ctx.enter_context(nc.psum_tensor(f"h_psum{k}", [P, 2, 512], F32)) for k in range(2)]
        o_psum = [ctx.enter_context(nc.psum_tensor(f"o_psum{k}", [P, D_MODEL], F32)) for k in range(2)]

        xs_in, acc_in, ln_in = sem("xs_in"), sem("acc_in"), sem("ln_in")
        u_in = [sem(f"u_in{k}") for k in range(2)]
        v_in = [sem(f"v_in{k}") for k in range(2)]
        gate_in = [sem(f"gate_in{k}") for k in range(2)]
        u_hi_done, u_lo_done = sem("u_hi_done"), sem("u_lo_done")
        v_hi_done, v_split_done = sem("v_hi_done"), sem("v_split_done")
        h_done, gelu_done = sem("h_done"), sem("gelu_done")
        gated, w_hi_done, w_done = sem("gated"), sem("w_hi_done"), sem("w_done")
        o_done, o_added = sem("o_done"), sem("o_added")
        eps_set, stats_done, moments_done = sem("eps_set"), sem("stats_done2"), sem("moments_done2")
        std_done, rstd_step, centred = sem("std_done2"), sem("rstd_step2"), sem("centred2")
        scaled, rows_done, out_stored = sem("scaled2"), sem("rows_done2"), sem("out_stored")

        fetched_in = [sem(f"fetched_in{k}") for k in range(RING)]
        row_used, index_copied, dots_kept, dots_ready = sem("row_used"), sem("index_copied"), sem("dots_kept"), sem("dots_ready")
        weight_step, weights_copied, rows_scaled = sem("weight_step"), sem("weights_copied"), sem("rows_scaled")
        dots_gelu = sem("dots_gelu")

        last = groups // 2 - 1

        with nc.Block() as block:
            @block.sync
            def _(sp):
                for t in range(DENSE):
                    sp.dma_start(xs[:, t], x1_split[GATHERED + t]).then_inc(xs_in, 16)

                def load_u(b, k):
                    sp.dma_start(u_raw[:, k], u_blocks[bass.ds(b, 1)].rearrange("o p (c i) -> p (o c) i", c=KD)
                                 ).then_inc(u_in[k], 16)

                def load_v(b, k):
                    sp.dma_start(v_raw[:, k], v_blocks[bass.ds(b, 1)].rearrange("o p d -> p (o d)")
                                 ).then_inc(v_in[k], 16)

                def load_gate(g, p):
                    sp.dma_start(gate[:, p], gates[:, :, bass.ds(g * GROUP, GROUP), :]).then_inc(gate_in[p], 16)

                load_u(0, 0)
                load_u(1, 1)
                load_gate(0, 0)
                load_v(0, 0)
                load_v(1, 1)
                load_gate(1, 1)
                for t in range(TILES):
                    sp.dma_start(acc[:, t], x1_rows[t]).then_inc(acc_in, 16)
                sp.dma_start(ln_g[:, :], ln2_g.partition_broadcast(P)).then_inc(ln_in, 16)
                sp.dma_start(ln_b[:, :], ln2_b.partition_broadcast(P)).then_inc(ln_in, 16)

                def refill(i, end):
                    for j in range(2 * GROUP):
                        b = 2 * GROUP * i + j
                        if not (end and j >= 2 * GROUP - 2):
                            sp.wait_ge(u_hi_done, b + 1)
                            sp.wait_ge(u_lo_done, b + 1)
                            load_u(b + 2, j % 2)
                            sp.wait_ge(v_split_done, b + 1)
                            load_v(b + 2, j % 2)
                        if j % GROUP == GROUP - 1 and not end:
                            sp.wait_ge(w_done, b + 1)
                            load_gate(2 * i + 2 + j // GROUP, j // GROUP)

                with sp.Fori(0, last) as i:
                    refill(i, False)
                refill(last, True)
                for n in range(TILES):
                    sp.wait_ge(rows_done, n + 1)
                    sp.dma_start(out[n], acc[:, n]).then_inc(out_stored, 16)
                sp.wait_ge(out_stored, 16 * TILES)

            @block.scalar
            def _(act):
                def split_u_hi(b, k, n):
                    act.wait_ge(u_in[k], 16 * n)
                    if past(b - 1):
                        act.wait_ge(h_done, b - 1)
                    act.activation(u_split[:, k, 0], u_raw[:, k], ACT.Copy).then_inc(u_hi_done, 1)

                def gelu(b, k):
                    act.wait_ge(h_done, b + 1)
                    if past(b - 1):
                        act.wait_ge(w_done, b - 1)
                    act.activation(act_out[:, k].rearrange("p (a n) -> p a n", a=2), h_psum[k][:, :, 0:TOKENS // 2],
                                   ACT.Gelu).then_inc(gelu_done, 1)

                def split_v_hi(i, j):
                    p, q = j // GROUP, j % GROUP
                    act.wait_ge(v_in[j % 2], 16 * (GROUP * i + j // 2 + 1))
                    if q == 0 and past(2 * i + p - 1):
                        act.wait_ge(o_done, DENSE * (2 * i + p - 1))
                    act.activation(v_split[:, p, q, 0], v_raw[:, j % 2], ACT.Copy).then_inc(v_hi_done, 1)

                def blocks_of(i, end):
                    for j in range(2 * GROUP):
                        b = 2 * GROUP * i + j
                        gelu(b, j % 2)
                        split_v_hi(i, j)
                        if not (end and j >= 2 * GROUP - 2):
                            split_u_hi(b + 2, j % 2, GROUP * i + j // 2 + 2)

                split_u_hi(0, 0, 1)
                split_u_hi(1, 1, 1)
                blocks_of(0, False)
                for stint in range(2 * GATHERED):
                    with act.Fori(max(1, stint * STINT), min(last, (stint + 1) * STINT)) as i:
                        blocks_of(i, False)
                    if stint % 2 == 0:
                        act.wait_ge(dots_ready, stint // 2 + 1)
                        act.activation(dots_all[:, :], dots_all[:, :], ACT.Gelu).then_inc(dots_gelu, 1)
                blocks_of(last, True)
                act.wait_ge(eps_set, 1)
                for t in range(TILES):
                    act.wait_ge(moments_done, t + 1)
                    act.activation(std[:, t:t + 1], moments[:, t, 1:2], ACT.Sqrt, bias=eps[:, :]
                                   ).then_inc(std_done, 1)

            @block.gpsimd
            def _(pool):
                def split_u_lo(b, k, n):
                    pool.wait_ge(u_in[k], 16 * n)
                    pool.wait_ge(u_hi_done, b + 1)
                    if past(b - 1):
                        pool.wait_ge(h_done, b - 1)
                    pool.tensor_tensor(u_split[:, k, 1], u_raw[:, k], u_split[:, k, 0], ALU.subtract
                                       ).then_inc(u_lo_done, 1)

                def split_v(i, b, j, n):
                    p, q = j // GROUP, j % GROUP
                    pool.wait_ge(v_in[j % 2], 16 * n)
                    pool.wait_ge(v_hi_done, b + 1)
                    pool.tensor_tensor(v_split[:, p, q, 1], v_raw[:, j % 2], v_split[:, p, q, 0], ALU.subtract
                                       ).then_inc(v_split_done, 1)

                def fetch(i, source, n, first=False):
                    if not (first and n < RING):
                        pool.wait_ge(row_used, PICKS * i + n - RING + 1)
                        pool.nop(nofuse=True)
                    pool.indirect_dma_start(fetched[:, n % RING], None, source,
                                            bass.IndirectOffsetOnAxis(ap=index_now[:, n:n + 1], axis=0)
                                            ).then_inc(fetched_in[n % RING], 16)

                def blocks_of(i, j0, tile, source, end=False, first=False):
                    if not first:
                        pool.wait_ge(row_used, PICKS * i)
                        pool.nop(nofuse=True)
                    pool.tensor_copy(index_now[:, :], pick_index[:, tile, bass.ds(PICKS * (i - j0), PICKS)]
                                     ).then_inc(index_copied, 1)
                    pool.wait_ge(index_copied, i + 1)
                    pool.nop(nofuse=True)
                    for p in range(2):
                        for q in range(GROUP):
                            j = p * GROUP + q
                            b = 2 * GROUP * i + j
                            n = GROUP * i + j // 2 + 1
                            split_v(i, b, j, n)
                            if not (end and j >= 2 * GROUP - 2):
                                split_u_lo(b + 2, j % 2, n + 1)
                            for r in range(2):
                                fetch(i, source, PICKS // 2 * p + 2 * q + r, first)
                        for r in range(2 * GROUP, PICKS // 2):
                            fetch(i, source, PICKS // 2 * p + r, first)

                split_u_lo(0, 0, 1)
                split_u_lo(1, 1, 1)
                blocks_of(0, 0, 0, u_rows, first=True)
                for stint in range(2 * GATHERED):
                    j0 = stint * STINT
                    args = (j0, stint // 2, v_rows if stint % 2 else u_rows)
                    with pool.Fori(max(1, j0), min(last, j0 + STINT)) as i:
                        blocks_of(i, *args)
                blocks_of(last, *args, end=True)
                pool.wait_ge(ln_in, 32)
                for n, t in enumerate(range(TILES)):
                    pool.wait_ge(centred, n + 1)
                    pool.tensor_tensor(acc[:, t], acc[:, t], ln_g[:, :], ALU.mult).then_inc(scaled, 1)

            @block.vector
            def _(dve):
                dve.memset(eps[:, :], LN_EPS).then_inc(eps_set, 1)

                def gate_and_split(b, g, p, q, n):
                    k = q % 2
                    dve.wait_ge(gelu_done, b + 1)
                    if q == 0:
                        dve.wait_ge(gate_in[p], 16 * n)
                        if past(g - 1):
                            dve.wait_ge(o_done, DENSE * (g - 1))
                    rows = act_out[:, k].rearrange("p (c t) -> p c t", t=CHUNK)
                    dve.tensor_tensor(rows, rows, gate[:, p, :, q, :], ALU.mult).then_inc(gated, 1)
                    dve.wait_ge(gated, b + 1)
                    dve.tensor_copy(w_split[:, p, q, 0], act_out[:, k]).then_inc(w_hi_done, 1)
                    dve.wait_ge(w_hi_done, b + 1)
                    dve.tensor_tensor(w_split[:, p, q, 1], act_out[:, k], w_split[:, p, q, 0], ALU.subtract
                                      ).then_inc(w_done, 1)

                def add(g, t, scale=1.0):
                    dve.wait_ge(o_done, DENSE * g + t + 1)
                    row = acc[:, GATHERED + t]
                    dve.scalar_tensor_tensor(row, row, scale, o_psum[t % 2][:, :], ALU.mult, ALU.add
                                             ).then_inc(o_added, 1)

                def take(i, j0, tile, kind, n):
                    dve.wait_ge(fetched_in[n % RING], 16 * (PICKS // RING * i + n // RING + 1))
                    if kind == "U":
                        dve.tensor_tensor_reduce(fetched[:, n % RING], fetched[:, n % RING], acc[:, tile], 1.0, 0.0,
                                                 ALU.mult, ALU.add, dots[:, n:n + 1]).then_inc(row_used, 1)
                    else:
                        dve.wait_ge(row_used, PICKS * i + n)
                        dve.scalar_tensor_tensor(acc[:, tile], fetched[:, n % RING], dots[:, n:n + 1], acc[:, tile],
                                                 ALU.mult, ALU.add).then_inc(row_used, 1)

                def step(g, i, p, n, j0, tile, kind, first=False):
                    for q in range(GROUP):
                        gate_and_split(GROUP * g + q, g, p, q, n)
                        for r in range(2):
                            take(i, j0, tile, kind, PICKS // 2 * p + 2 * q + r)
                    r = 2 * GROUP
                    for t in range(DENSE):
                        if not first:
                            if t == 0:
                                dve.wait_ge(o_added, DENSE * (g - 1))
                            add(g - 1, t)
                        upto = 2 * GROUP + (PICKS // 2 - 2 * GROUP) * (t + 1) // DENSE
                        for r in range(r, upto):
                            take(i, j0, tile, kind, PICKS // 2 * p + r)
                        r = upto

                def pair(i, j0, tile, kind, first=False):
                    if kind == "V":
                        dve.wait_ge(row_used, PICKS * i)
                        dve.tensor_copy(dots[:, :], dots_all[:, bass.ds(PICKS * (i - j0), PICKS)]
                                        ).then_inc(weights_copied, 1)
                        dve.wait_ge(weights_copied, i - j0 + 1 + STINT * tile)
                    step(2 * i, i, 0, i + 1, j0, tile, kind, first)
                    step(2 * i + 1, i, 1, i + 1, j0, tile, kind)
                    if kind == "U":
                        dve.wait_ge(row_used, PICKS * (i + 1))
                        dve.tensor_copy(dots_all[:, bass.ds(PICKS * (i - j0), PICKS)], dots[:, :]
                                        ).then_inc(dots_kept, 1)
                        dve.wait_ge(dots_kept, i - j0 + 1 + STINT * tile)

                def weigh(tile):
                    dve.tensor_scalar(acc[:, tile], acc[:, tile], ALPHA, None, ALU.mult).then_inc(rows_scaled, 1)
                    dve.wait_ge(dots_gelu, tile + 1)
                    dve.tensor_tensor(dots_all[:, :], dots_all[:, :], pick_gate[:, tile], ALU.mult
                                      ).then_inc(weight_step, 1)
                    dve.wait_ge(weight_step, tile + 1)
                    dve.wait_ge(rows_scaled, DENSE + tile + 1)

                dve.wait_ge(acc_in, 16 * TILES)
                for t in range(DENSE):
                    dve.tensor_scalar(acc[:, GATHERED + t], acc[:, GATHERED + t], ALPHA, None, ALU.mult
                                      ).then_inc(rows_scaled, 1)
                dve.wait_ge(rows_scaled, DENSE)
                pair(0, 0, 0, "U", first=True)
                for stint in range(2 * GATHERED):
                    j0, tile, kind = stint * STINT, stint // 2, "UV"[stint % 2]
                    if kind == "V":
                        weigh(tile)
                    with dve.Fori(max(1, j0), min(last + 1, j0 + STINT)) as i:
                        pair(i, j0, tile, kind)
                    if kind == "U":
                        dve.drain().then_inc(dots_ready, 1)

                dve.wait_ge(ln_in, 32)
                dve.wait_ge(row_used, PICKS * groups // 2)

                def finish(t):
                    dve.wait_ge(scaled, t + 1)
                    dve.tensor_tensor(acc[:, t], acc[:, t], ln_b[:, :], ALU.add).then_inc(rows_done, 1)

                for t in range(TILES):
                    if t >= GATHERED:
                        add(groups - 1, t - GATHERED)
                        dve.wait_ge(o_added, DENSE * (groups - 1) + t - GATHERED + 1)
                    dve.bn_stats(stats[:, 0], acc[:, t, 0:512])
                    dve.bn_stats(stats[:, 1], acc[:, t, 512:1024]).then_inc(stats_done, 1)
                    dve.wait_ge(stats_done, t + 1)
                    dve.bn_aggr(moments[:, t], stats[:, :, :]).then_inc(moments_done, 1)
                    if t:
                        finish(t - 1)
                    newton_rstd(dve, moments[:, t], std[:, t:t + 1], rstd[:, t:t + 1], newton[:, t:t + 1],
                                moments_done, t + 1, std_done, t + 1, rstd_step, 5 * t)
                    dve.tensor_scalar(acc[:, t], acc[:, t], moments[:, t, 0:1], rstd[:, t:t + 1],
                                      ALU.subtract, ALU.mult).then_inc(centred, 1)
                finish(TILES - 1)

            @block.tensor
            def _(pe):
                def up(b, k):
                    pe.wait_ge(u_hi_done, b + 1)
                    pe.wait_ge(u_lo_done, b + 1)
                    if past(b - 1):
                        pe.wait_ge(gelu_done, b - 1)
                    for c in range(KD):
                        for part in range(2):
                            for xpart in range(2 - part):
                                for half in range(2):
                                    mm = pe.matmul(
                                        h_psum[k][:, half, 0:TOKENS // 2], u_split[:, k, part, c],
                                        xs[:, DENSE // 2 * half:DENSE // 2 * (half + 1), xpart, c, :],
                                        start=(c == 0 and part == 0 and xpart == 0),
                                        stop=(c == KD - 1 and part == 1))
                    mm.then_inc(h_done, 1)

                def down(g, p):
                    pe.wait_ge(w_done, GROUP * (g + 1))
                    pe.wait_ge(v_split_done, GROUP * (g + 1))
                    for t in range(DENSE):
                        if past(DENSE * g + t - 1):
                            pe.wait_ge(o_added, DENSE * g + t - 1)
                        for q in range(GROUP):
                            for part in range(2):
                                for vpart in range(2 - part):
                                    for half in range(2):
                                        mm = pe.matmul(
                                            o_psum[t % 2][:, half * 512:half * 512 + 512],
                                            w_split[:, p, q, part, t * P:(t + 1) * P],
                                            v_split[:, p, q, vpart, half * 512:half * 512 + 512],
                                            start=(q == 0 and part == 0 and vpart == 0),
                                            stop=(q == GROUP - 1 and part == 1))
                        mm.then_inc(o_done, 1)

                def pair(i, end=False):
                    for q in range(GROUP):
                        up(GROUP * (2 * i + 1) + q, q % 2)
                    down(2 * i, 0)
                    if not end:
                        for q in range(GROUP):
                            up(GROUP * (2 * i + 2) + q, q % 2)
                    down(2 * i + 1, 1)

                pe.wait_ge(xs_in, 16 * DENSE)
                for q in range(GROUP):
                    up(q, q % 2)
                pair(0, last == 0)
                if last > 1:
                    with pe.Fori(1, last) as i:
                        pair(i)
                if last > 0:
                    pair(last, True)


def shape_constants():
    token = np.arange(SEQ, dtype=np.float32)
    half = HEAD_DIM // 2
    inv = (10000.0 ** (-(np.arange(half, dtype=np.float32) / half)).astype(np.float64)).astype(np.float32)
    angle = (token[None, :] * inv[:, None]).astype(np.float64)
    rot = np.zeros((P, P), np.float32)
    for d in range(P):
        rot[d + half if d % HEAD_DIM < half else d - half, d] = -1.0 if d % HEAD_DIM < half else 1.0
    minus_row = np.zeros((FOX_HEADS, FOX_HEADS, P), np.float32)
    for h in range(FOX_HEADS):
        minus_row[h, h] = -1.0
    q, k = np.arange(P)[:, None], np.arange(P)[None, :]
    masks = np.concatenate([np.where(k > q, 0.0, LOW), np.where(k <= q, 0.0, LOW)], 1).astype(np.float32)
    return {
        "ident": np.eye(P, dtype=np.float32),
        "rot": rot,
        "minus_row": minus_row,
        "cos": np.tile(np.cos(angle).astype(np.float32), (P // half, 1)),
        "sin": np.tile(np.sin(angle).astype(np.float32), (P // half, 1)),
        "masks": masks,
        "iota": np.tile(np.arange(P, dtype=np.float32), (P, 1)),
    }


def column_blocks(w):
    return np.ascontiguousarray(w.reshape(KD, P, -1, P).transpose(2, 1, 0, 3))


def laid_out(x, w_in, b_forget, swa_sinks, w_out, ln1_g, ln1_b, w_query, sub_keys, expert_u, expert_v,
             ln2_g, ln2_b):
    fox = FOX_HEADS * HEAD_DIM
    w, x = w_in[0], x[0]
    swa = 3 * fox + FOX_HEADS
    skv = swa + SWA_HEADS * HEAD_DIM
    beside = (np.arange(SWA_HEADS * HEAD_DIM).reshape(2, PAIRS, HEAD_DIM).transpose(1, 0, 2)).ravel()
    w_fox = column_blocks(w[:, :3 * fox]).reshape(3, PAIRS, P, KD, P).transpose(1, 2, 0, 3, 4)
    rows = np.concatenate([np.arange(fox), fox + beside])
    return {
        "x_t": np.ascontiguousarray(x.T.reshape(KD, P, SEQ)),
        "x_rows": np.ascontiguousarray(x.reshape(TILES, P, D_MODEL)),
        "w_fox": np.ascontiguousarray(w_fox),
        "w_swa": column_blocks(w[:, swa:skv][:, beside]),
        "w_skv": np.ascontiguousarray(column_blocks(w[:, skv:]).transpose(1, 0, 2, 3)),
        "w_forget": np.ascontiguousarray(w[:, 3 * fox:swa].reshape(KD, P, FOX_HEADS).transpose(1, 0, 2)),
        "b_forget": np.ascontiguousarray(b_forget[0][:, None]),
        "sinks": np.ascontiguousarray(swa_sinks[0].reshape(2, PAIRS).T.ravel()),
        "w_out": np.ascontiguousarray(w_out[0][rows].reshape(KD, P, D_MODEL).transpose(1, 0, 2)),
        "ln1_g": np.ascontiguousarray(ln1_g[0]),
        "ln1_b": np.ascontiguousarray(ln1_b[0]),
        "w_query": np.ascontiguousarray(w_query[0].reshape(KD, P, SETS, P).transpose(1, 2, 0, 3)),
        "sub_keys": np.ascontiguousarray(sub_keys[0].reshape(SETS, N_KEYS, P).transpose(2, 0, 1)),
        "u_blocks": np.ascontiguousarray(
            expert_u[0].reshape(N_KEYS, P, KD, P).transpose(0, 3, 2, 1).reshape(N_KEYS, P, D_MODEL)),
        "u_rows": np.ascontiguousarray(expert_u[0]),
        "v_blocks": np.ascontiguousarray(expert_v[0].reshape(N_KEYS, P, D_MODEL)),
        "ln2_g": np.ascontiguousarray(ln2_g[0]),
        "ln2_b": np.ascontiguousarray(ln2_b[0]),
    }


def build(nc, dram, out):
    mixed_t = nc.dram_tensor("mixed_t", (TILES, P, 2 * PAIRS, P), F32, kind="Internal").ap()
    x1_rows = nc.dram_tensor("x1_rows", (TILES, P, D_MODEL), F32, kind="Internal").ap()
    x1_split = nc.dram_tensor("x1_split", (TILES, P, 2, KD, P), BF16, kind="Internal").ap()
    gates = nc.dram_tensor("gates", (P, TOKENS // CHUNK, N_KEYS, CHUNK), F32, kind="Internal").ap()
    with (nc.sbuf_tensor("pick_index", [P, GATHERED, PEER_HEADS * TOPK], U32) as pick_index,
          nc.sbuf_tensor("pick_gate", [P, GATHERED, PEER_HEADS * TOPK], F32) as pick_gate):
        attention_phase(nc, dram["x_t"], dram["w_fox"], dram["w_swa"], dram["w_skv"], dram["w_forget"],
                        dram["b_forget"], dram["sinks"], dram, mixed_t)
        routing_phase(nc, mixed_t, dram["x_rows"], dram["w_out"], dram["ln1_g"], dram["ln1_b"], dram["w_query"],
                      dram["sub_keys"], dram, x1_rows, x1_split, gates, pick_index, pick_gate)
        expert_phase(nc, dram["u_blocks"], dram["v_blocks"], dram["u_rows"],
                     dram["v_blocks"].rearrange("b p d -> (b p) d"), gates, x1_rows, x1_split,
                     dram["ln2_g"], dram["ln2_b"], out, pick_index, pick_gate)


def kernel(**inputs):
    import concourse.bacc as bacc
    from concourse.bass_utils import run_bass_kernel_spmd

    arrays = laid_out(**{name: np.asarray(a) for name, a in inputs.items()}) | shape_constants()
    nc = bacc.Bacc("TRN2", target_bir_lowering=False, num_devices=1)
    dram = {name: nc.dram_tensor(name, a.shape, F32, kind="ExternalInput").ap() for name, a in arrays.items()}
    out = nc.dram_tensor("out", (TILES, P, D_MODEL), F32, kind="ExternalOutput").ap()
    build(nc, dram, out)
    result = run_bass_kernel_spmd(nc, [arrays], core_ids=[0])
    return result.results[0]["out"].reshape(1, SEQ, D_MODEL)
```

```python
from contextlib import ExitStack

import numpy as np

import concourse.bass as bass
from concourse import mybir

P = 128
D_MODEL = 1024
SEQ = 1024
KD = D_MODEL // P
TILES = SEQ // P
HEAD_DIM = 64
FOX_HEADS = 8
SWA_HEADS = 8
PAIRS = FOX_HEADS // 2
N_KEYS = 128
PEER_HEADS = 8
TOPK = 16
SETS = 2 * PEER_HEADS
CHUNK = 32
GROUP = 4
GATHERED = 2
DENSE = TILES - GATHERED
TOKENS = DENSE * P
STINT = N_KEYS // GROUP // 2 // (2 * GATHERED)
PICKS = PEER_HEADS * TOPK // STINT
RING = 4
LN_EPS = 1e-5
ALPHA = 2.0 ** 0.25
SCALE = HEAD_DIM ** -0.5
LOW = -3.0e38

F32 = mybir.dt.float32
BF16 = mybir.dt.bfloat16
U32 = mybir.dt.uint32
ALU = mybir.AluOpType
ACT = mybir.ActivationFunctionType
AX = mybir.AxisListType

UNITS = 2 * TILES
PROBS = 4
FOX_CHUNKS = 6
SWA_CHUNKS = 4
FOX_SHARES = (4, 4, 4, 4, 4, 4, 3, 3, 2, 3, 3, 2, 2, 2, 2, 2)
FOX_PROJECTED = (1, 3, 5, 8, 11, 15)
LAST_FOX_SHARES = (1,) * 8 + (2,) * 4 + (1, 1, 0, 0)
LAST_FOX_PROJECTED, LAST_FOX_ROTATED = (7, 11), (12, 13)
SWA_SHARES = (4, 4, 4, 4, 1, 1, 0, 0)
SWA_PROJECTED, SWA_ROTATED = (1, 3), (4, 5)


def past(count):
    return not isinstance(count, int) or count > 0


def newton_rstd(dve, moments, std, rstd, tmp, moments_done, n_moments, std_done, n_std, step, n):
    dve.wait_ge(moments_done, n_moments)
    dve.wait_ge(std_done, n_std)
    dve.reciprocal(rstd, std).then_inc(step, 1)
    dve.tensor_scalar(tmp, moments[:, 1:2], LN_EPS, -0.5, ALU.add, ALU.mult).then_inc(step, 1)
    dve.wait_ge(step, n + 2)
    dve.scalar_tensor_tensor(tmp, tmp, rstd, rstd, ALU.mult, ALU.mult).then_inc(step, 1)
    dve.wait_ge(step, n + 3)
    dve.tensor_scalar(tmp, tmp, 1.5, None, ALU.add).then_inc(step, 1)
    dve.wait_ge(step, n + 4)
    dve.tensor_tensor(rstd, rstd, tmp, ALU.mult).then_inc(step, 1)
    dve.wait_ge(step, n + 5)


def attention_phase(nc, x_t, w_fox, w_swa, w_skv, w_forget, b_forget, sinks, w_out, consts, mixed_t, wide):
    with ExitStack() as ctx:
        sb = lambda name, shape, dt=F32: ctx.enter_context(nc.sbuf_tensor("att_" + name, shape, dt))
        sem = lambda name: ctx.enter_context(nc.semaphore(name))
        xt = wide.rearrange("p c n -> p (c n)").bitcast(BF16).rearrange("p (h c n) -> p h c n", h=2, c=KD)
        w_raw = sb("w_raw", [P, 3, KD, P])
        w_pair = sb("w_pair", [P, 2, 2, 3, KD, P], BF16)
        w_sq = sb("w_sq", [P, 2, 2, KD, P], BF16)
        w_f_raw = sb("w_f_raw", [P, KD, FOX_HEADS])
        w_f = sb("w_f", [P, 2, KD, FOX_HEADS], BF16)
        ident = sb("a_ident", [P, P])
        rot = sb("rot", [P, P])
        cos = sb("cos", [P, SEQ])
        sin = sb("sin", [P, SEQ])
        ident16 = sb("ident16", [P, P], BF16)
        masks = sb("masks", [P, 2 * P])
        masks16 = sb("masks16", [P, 2 * P], BF16)
        b_f = sb("b_f", [FOX_HEADS, 1])
        sink = sb("sink", [P, PAIRS, 2])
        neg_sink = sb("neg_sink", [P, PAIRS, 2])
        neg_c = sb("neg_c", [P, FOX_HEADS, SEQ])
        c_col = sb("c_col", [P, TILES, FOX_HEADS])
        q_t = [sb(f"q_t{k}", [P, SEQ]) for k in range(2)]
        k_t = [sb(f"k_t{k}", [P, SEQ]) for k in range(2)]
        v_rows = [sb(f"v_rows{k}", [P, TILES, P]) for k in range(2)]
        sk_t = sb("sk_t", [P, SEQ])
        sv_rows = sb("sv_rows", [P, TILES, P])
        raw = sb("raw", [P, SEQ])
        rope_tmp = sb("rope_tmp", [P, SEQ])
        probs = sb("probs", [P, PROBS, SEQ])
        probs_t = sb("probs_t", [P, 2, SEQ])
        neg_max = sb("neg_max", [P, PROBS, 2])
        row_sum = sb("row_sum", [P, PROBS, 2])
        sink_exp = sb("sink_exp", [P, PROBS, 2])
        o_rows = sb("o_rows", [P, P])
        pair_out = sb("pair_out", [P, 2, 2, SEQ], BF16)
        x_raw = neg_c
        w_kv_raw = probs[:, 0:2].rearrange("p j (c n) -> p j c n", c=KD)
        w_kv = (probs[:, 2:4].rearrange("p j n -> p (j n)").bitcast(BF16)
                .rearrange("p (h j c n) -> p h j c n", h=2, j=2, c=KD))
        f_tmp = [buffer[0:FOX_HEADS] for buffer in (q_t[1], k_t[1], v_rows[1].rearrange("p t c -> p (t c)"))]
        c_row = rope_tmp[0:FOX_HEADS]
        zeros = probs_t[0:FOX_HEADS, 0]
        minus_row = probs_t[0:FOX_HEADS, 1].rearrange("p (h n) -> p h n", h=FOX_HEADS)
        s_psum = [ctx.enter_context(nc.psum_tensor(f"s_psum{k}", [P, 2, 512], F32)) for k in range(2)]
        t_psum = [ctx.enter_context(nc.psum_tensor(f"t_psum{k}", [P, 512], F32)) for k in range(2)]
        o_psum = ctx.enter_context(nc.psum_tensor("a_o_psum", [P, 2, P], F32))
        p_psum = ctx.enter_context(nc.psum_tensor("p_psum", [P, 512], F32))
        s_flat = [s_psum[k][:, :, :].rearrange("p a b -> p (a b)") for k in range(2)]

        w_o_raw = neg_c
        w_o_in, w_o_hi, w_o_lo = sem("w_o_in"), sem("w_o_hi"), sem("w_o_lo")
        x_in = [sem(f"x_in{c}") for c in range(KD // 2)]
        w_first_in, const_in, w_pair_in = sem("w_first_in"), sem("const_in"), sem("w_pair_in")
        const_made = sem("const_made")
        x_hi, x_lo, w_hi, w_lo, pair_hi, pair_lo = (sem("x_hi"), sem("x_lo"), sem("w_hi"), sem("w_lo"),
                                                    sem("pair_hi"), sem("pair_lo"))
        f_psum_done, f_step, c_done = sem("f_psum_done"), sem("f_step"), sem("c_done")
        fa_step = sem("fa_step")
        bcast_done, bcast_copied = sem("bcast_done"), sem("bcast_copied")
        k_proj, k_raw, k_rot, k_ready = sem("k_proj"), sem("k_raw"), sem("k_rot"), sem("k_ready")
        kr_step, v_proj, v_ready = sem("kr_step"), sem("v_proj"), sem("v_ready")
        chunk_done, chunk_copied = sem("chunk_done"), sem("chunk_copied")
        scores_done, biased, max_done = sem("scores_done"), sem("biased"), sem("max_done")
        exp_done, turned, turn_copied = sem("exp_done"), sem("turned"), sem("turn_copied")
        inv_done, pv_done, out_scaled = sem("inv_done"), sem("pv_done"), sem("out_scaled")
        flipped, flip_hi, flip_copied = sem("flipped"), sem("flip_hi"), sem("flip_copied")
        pair_stored = [sem(f"pair_stored{k}") for k in range(2)]
        sq_step, sq_ready = sem("sq_step"), sem("sq_ready")
        sw_scores, sw_max, sw_neg_max, sw_gap = sem("sw_scores"), sem("sw_max"), sem("sw_neg_max"), sem("sw_gap")
        sw_exp, sw_sum, sw_turned, sw_turn_copied = sem("sw_exp"), sem("sw_sum"), sem("sw_turned"), sem("sw_turn_copied")
        sw_inv, sw_pv, sw_out_scaled = sem("sw_inv"), sem("sw_pv"), sem("sw_out_scaled")

        with nc.Block() as block:
            @block.sync
            def _(sp):
                for k in range(2):
                    sp.sem_inc(pair_stored[k], 32)
                sp.dma_start(w_f_raw[:, :, :], w_forget).then_inc(w_first_in, 16)
                sp.dma_start(x_raw[:, 0], x_t[0]).then_inc(x_in[0], 16)
                sp.dma_start(w_kv_raw, w_skv).then_inc(w_first_in, 16)
                for c in range(1, KD):
                    sp.dma_start(x_raw[:, c], x_t[c]).then_inc(x_in[c // 2], 16)
                sp.dma_start(b_f[:, :], b_forget).then_inc(const_in, 16)
                sp.dma_start(ident[:, :], consts["ident"]).then_inc(const_in, 16)
                sp.dma_start(rot[:, :], consts["rot"]).then_inc(const_in, 16)
                sp.dma_start(minus_row, consts["minus_row"]).then_inc(const_in, 16)
                sp.dma_start(cos[:, :], consts["cos"]).then_inc(const_in, 16)
                sp.dma_start(sin[:, :], consts["sin"]).then_inc(const_in, 16)
                sp.dma_start(masks[:, :], consts["masks"]).then_inc(const_in, 16)
                sp.dma_start(sink[:, :, :].rearrange("p j g -> p (j g)"), sinks.partition_broadcast(P)
                             ).then_inc(const_in, 16)
                def store(pair):
                    sp.wait_ge(flip_copied, TILES * (pair + 1))
                    for h in range(2):
                        sp.dma_start(mixed_t[:, :, h, pair, :].rearrange("t p n -> p t n"),
                                     pair_out[:, pair % 2, h].rearrange("p (t n) -> p t n", t=TILES)
                                     ).then_inc(pair_stored[pair % 2], 16)

                def load_weights(n):
                    if n >= 1:
                        sp.wait_ge(pair_lo, n)
                    if n < PAIRS:
                        sp.dma_start(w_raw[:, :, :, :], w_fox[n]).then_inc(w_pair_in, 16)
                    else:
                        sp.dma_start(w_raw[:, 0], w_swa[n - PAIRS]).then_inc(w_pair_in, 16)

                for n in range(3):
                    load_weights(n)
                for pair in range(2 * PAIRS):
                    if pair + 3 < 2 * PAIRS:
                        load_weights(pair + 3)
                    store(pair)
                    if pair == PAIRS - 1:
                        sp.dma_start(w_o_raw[:, :, :], w_out).then_inc(w_o_in, 16)
                for k in range(2):
                    sp.wait_ge(pair_stored[k], 32 * (PAIRS + 1))

            @block.tensor
            def _(pe):
                def products(out, left, right, start, stop):
                    for a, b in ((0, 0), (0, 1), (1, 0)):
                        mm = pe.matmul(out, left(a), right(b), start=start and a + b == 0, stop=stop and a == 1)
                    return mm

                def project_fox(pair, kp, first, last):
                    for piece in range(first, last):
                        chunk, c = divmod(piece, KD)
                        n = FOX_CHUNKS * pair + chunk
                        if piece == 0:
                            pe.wait_ge(pair_lo, pair + 1)
                        if c == 0 and past(n):
                            pe.wait_ge(chunk_copied, n)
                        half = chunk % 2
                        if chunk < 4:
                            mm = products(p_psum[:, :], lambda a: w_pair[:, kp, a, chunk // 2, c],
                                          lambda b: xt[:, b, c, half * 512:half * 512 + 512], c == 0, c == KD - 1)
                        else:
                            col, t = c // 2 * P, 4 * half + c // 2
                            for m in range(c % 2 * KD // 2, (c % 2 + 1) * KD // 2):
                                mm = products(p_psum[:, col:col + P], lambda a: xt[:, a, m, t * P:(t + 1) * P],
                                              lambda b: w_pair[:, kp, b, 2, m], m == 0, m == KD - 1)
                        if c == KD - 1:
                            mm.then_inc(chunk_done, 1)

                def project_swa(pair, kp, first, last):
                    for piece in range(first, last):
                        chunk = min(piece // KD, 2) + (piece == 2 * KD + 1)
                        c, half = piece - KD * chunk if chunk < 2 else 0, chunk % 2
                        n = FOX_CHUNKS * PAIRS + SWA_CHUNKS * pair + chunk
                        if piece == 0:
                            pe.wait_ge(pair_lo, PAIRS + pair + 1)
                        if c == 0:
                            pe.wait_ge(chunk_copied, n)
                        if chunk < 2:
                            mm = products(p_psum[:, :], lambda a: w_sq[:, kp, a, c],
                                          lambda b: xt[:, b, c, half * 512:half * 512 + 512], c == 0, c == KD - 1)
                        else:
                            mm = pe.matmul(p_psum[:, :], rot[:, :], raw[:, half * 512:half * 512 + 512],
                                           start=True, stop=True)
                        if c == KD - 1 or chunk >= 2:
                            mm.then_inc(chunk_done, 1)

                def flip():
                    pe.transpose(o_psum[:, 1], o_rows[:, :], ident[:, :]).then_inc(flipped, 1)

                pe.wait_ge(w_lo, 2)
                for c in range(KD):
                    pe.wait_ge(x_lo, c + 1)
                    for half in range(2):
                        def x_half(b):
                            return xt[:, b, c, half * 512:half * 512 + 512]

                        f_mm = products(s_psum[0][0:FOX_HEADS, half], lambda a: w_f[:, a, c], x_half,
                                        c == 0, c == KD - 1)
                        k_mm = products(s_psum[1][:, half], lambda a: w_kv[:, a, 0, c], x_half,
                                        c == 0, c == KD - 1)
                f_mm.then_inc(f_psum_done, 1)
                k_mm.then_inc(k_proj, 1)
                for t in range(TILES):
                    for c in range(KD):
                        mm = products(t_psum[t // 4][:, t % 4 * P:t % 4 * P + P],
                                      lambda a: xt[:, a, c, t * P:(t + 1) * P], lambda b: w_kv[:, b, 1, c],
                                      c == 0, c == KD - 1)
                mm.then_inc(v_proj, 1)
                project_fox(0, 0, 0, KD)
                pe.wait_ge(const_in, 16 * 8)
                pe.wait_ge(const_made, 4)
                pe.wait_ge(k_raw, 1)
                for half in range(2):
                    mm = pe.matmul(s_psum[1][:, half], rot[:, :], raw[:, half * 512:half * 512 + 512],
                                   start=True, stop=True)
                mm.then_inc(k_rot, 1)
                project_fox(0, 0, KD, 2 * KD)
                pe.wait_ge(c_done, 1)
                for h in range(FOX_HEADS):
                    if h == 1:
                        pe.wait_ge(k_ready, 1)
                    if h >= 2:
                        pe.wait_ge(bcast_copied, h - 1)
                    for half in range(2):
                        mm = pe.matmul(s_psum[h % 2][:, half], minus_row[:, h], c_row[:, half * 512:half * 512 + 512],
                                       start=True, stop=True)
                    mm.then_inc(bcast_done, 1)
                    project_fox(0, 0, 2 * KD + h * KD // 2, 2 * KD + (h + 1) * KD // 2)
                pe.wait_ge(v_ready, 2)
                for t in range(TILES):
                    mm = pe.transpose(t_psum[0][:, t * FOX_HEADS:(t + 1) * FOX_HEADS], c_row[:, t * P:(t + 1) * P],
                                      ident[0:FOX_HEADS, 0:FOX_HEADS])
                mm.then_inc(bcast_done, 1)

                def scores(pair, kp, u):
                    qb, hh, k = u // 2, u % 2, u % 2
                    length = (qb + 1) * P
                    if u == 0:
                        pe.wait_ge(chunk_copied, FOX_CHUNKS * pair + 4)
                    if u >= 2 or past(pair):
                        pe.wait_ge(biased, UNITS * pair + u - 1)
                    rows = slice(HEAD_DIM * hh, HEAD_DIM * hh + HEAD_DIM)
                    for half in range((length + 511) // 512):
                        n = min(512, length - half * 512)
                        pe.matmul(s_psum[k][:, half, 0:n], q_t[kp][rows, qb * P:(qb + 1) * P],
                                  k_t[kp][rows, half * 512:half * 512 + n], start=True, stop=True)
                    mm = pe.matmul(s_psum[k][:, half, n - P:n], ident16[:, :], masks16[:, P:2 * P],
                                   start=False, stop=True, skip_group_check=True)
                    mm.then_inc(scores_done, 1)

                def turn(pair, u):
                    qb, n = u // 2, UNITS * pair + u
                    pe.wait_ge(exp_done, n + 1)
                    if past(n):
                        pe.wait_ge(turn_copied, n)
                    for b in range(qb + 1):
                        mm = pe.transpose(t_psum[b // 4][:, b % 4 * P:b % 4 * P + P],
                                          probs[:, u % PROBS, b * P:(b + 1) * P], ident[:, :])
                    mm.then_inc(turned, 1)

                def values(pair, kp, u):
                    qb, hh, n = u // 2, u % 2, UNITS * pair + u
                    if u == 0:
                        pe.wait_ge(chunk_copied, FOX_CHUNKS * pair + FOX_CHUNKS)
                    pe.wait_ge(turn_copied, n + 1)
                    if past(n):
                        pe.wait_ge(out_scaled, n)
                    if hh == 0 and past(n):
                        pe.wait_ge(flip_copied, TILES * pair + qb)
                    cols = slice(HEAD_DIM * hh, HEAD_DIM * hh + HEAD_DIM)
                    for b in range(qb + 1):
                        mm = pe.matmul(o_psum[:, 0, cols], probs_t[:, u % 2, b * P:(b + 1) * P],
                                       v_rows[kp][:, b, cols], start=(b == 0), stop=(b == qb))
                    mm.then_inc(pv_done, 1)

                def flip_fox(pair, u):
                    pe.wait_ge(out_scaled, UNITS * pair + u)
                    flip()

                def attend(pair, kp, last=False):
                    done = 0
                    for u in range(UNITS):
                        if u + 2 < UNITS:
                            scores(pair, kp, u + 2)
                        elif not last:
                            scores(pair + 1, 1 - kp, u + 2 - UNITS)
                        share = LAST_FOX_SHARES[u] if last else FOX_SHARES[u]
                        for part, pieces in enumerate((share // 2, share - share // 2)):
                            if last:
                                project_swa(0, 0, done, done + pieces)
                            else:
                                project_fox(pair + 1, 1 - kp, done, done + pieces)
                            done += pieces
                            if part == 0:
                                turn(pair, u)
                                if u >= 1:
                                    values(pair, kp, u - 1)
                                elif past(pair):
                                    values(pair - 1, 1 - kp, UNITS - 1)
                        if u >= 2 and u % 2 == 0:
                            flip_fox(pair, u)
                        elif u == 0 and past(pair):
                            flip_fox(pair - 1, UNITS)
                    if last:
                        values(pair, kp, UNITS - 1)
                        flip_fox(pair, UNITS)

                pe.wait_ge(bcast_copied, FOX_HEADS + 1)
                scores(0, 0, 0)
                scores(0, 0, 1)
                attend(0, 0)
                with pe.Fori(0, PAIRS // 2 - 1) as i:
                    attend(2 * i + 1, 1)
                    attend(2 * i + 2, 0)
                attend(PAIRS - 1, 1, last=True)

                def sw_score(pair, kp, qb):
                    k, n = qb % 2, TILES * pair + qb
                    if qb % 4 == 0:
                        pe.wait_ge(sq_ready, 2 * pair + qb // 4 + 1)
                    if qb >= 2 or past(pair):
                        pe.wait_ge(sw_exp, n - 1)
                    first = P * max(qb - 1, 0)
                    keys = (qb + 1) * P - first
                    for g in range(2):
                        rows = slice(HEAD_DIM * g, HEAD_DIM * g + HEAD_DIM)
                        pe.matmul(s_psum[k][:, g, 0:keys], q_t[kp][rows, qb * P:(qb + 1) * P],
                                  sk_t[rows, first:first + keys], start=True, stop=True)
                        mm = pe.matmul(s_psum[k][:, g, 0:keys], ident16[:, :], masks16[:, 2 * P - keys:2 * P],
                                       start=False, stop=True, skip_group_check=True)
                    mm.then_inc(sw_scores, 1)

                def sw_turn(pair, qb):
                    k, n = qb % 2, TILES * pair + qb
                    pe.wait_ge(sw_exp, n + 1)
                    if qb >= 2 or past(pair):
                        pe.wait_ge(sw_turn_copied, n - 1)
                    for b in range(4):
                        if qb == 0 and b % 2:
                            continue
                        mm = pe.transpose(t_psum[k][:, b * P:(b + 1) * P], probs[:, qb % PROBS, b * P:(b + 1) * P],
                                          ident[:, :])
                    mm.then_inc(sw_turned, 1)

                def sw_values(pair, qb):
                    n = TILES * pair + qb
                    pe.wait_ge(sw_turn_copied, n + 1)
                    pe.wait_ge(flip_copied, TILES * (PAIRS + pair) + qb)
                    first, blocks = max(qb - 1, 0), min(qb + 1, 2)
                    for g in range(2):
                        cols = slice(HEAD_DIM * g, HEAD_DIM * g + HEAD_DIM)
                        for b in range(blocks):
                            at = (2 * g + b) * P
                            mm = pe.matmul(o_psum[:, 0, cols], probs_t[:, qb % 2, at:at + P],
                                           sv_rows[:, first + b, cols], start=(b == 0), stop=(b == blocks - 1))
                    mm.then_inc(sw_pv, 1)

                def sw_flip(pair, qb):
                    pe.wait_ge(sw_out_scaled, TILES * pair + qb + 1)
                    flip()

                def sw_attend(pair, kp, last=False):
                    done = 0
                    for qb in range(TILES):
                        if qb + 2 < TILES:
                            sw_score(pair, kp, qb + 2)
                        elif not last:
                            sw_score(pair + 1, 1 - kp, qb + 2 - TILES)
                        share = 0 if last else SWA_SHARES[qb]
                        if share:
                            project_swa(pair + 1, 1 - kp, done, done + share // 2)
                        sw_turn(pair, qb)
                        if qb >= 1:
                            sw_values(pair, qb - 1)
                        elif past(pair):
                            sw_values(pair - 1, TILES - 1)
                        if share:
                            project_swa(pair + 1, 1 - kp, done + share // 2, done + share)
                        done += share
                        if qb >= 1:
                            sw_flip(pair, qb - 1)
                        elif past(pair):
                            sw_flip(pair - 1, TILES - 1)
                    if last:
                        sw_values(pair, TILES - 1)
                        sw_flip(pair, TILES - 1)

                sw_score(0, 0, 0)
                sw_score(0, 0, 1)
                sw_attend(0, 0)
                with pe.Fori(0, PAIRS // 2 - 1) as i:
                    sw_attend(2 * i + 1, 1)
                    sw_attend(2 * i + 2, 0)
                sw_attend(PAIRS - 1, 1, last=True)

            @block.vector
            def _(dve):
                for c in range(KD):
                    dve.wait_ge(x_hi, c + 1)
                    dve.tensor_tensor(xt[:, 1, c], x_raw[:, c], xt[:, 0, c], ALU.subtract).then_inc(x_lo, 1)
                    if c == 0:
                        dve.wait_ge(w_hi, 2)
                        dve.tensor_tensor(w_f[:, 1], w_f_raw[:, :, :], w_f[:, 0], ALU.subtract).then_inc(w_lo, 1)
                        dve.tensor_tensor(w_kv[:, 1], w_kv_raw, w_kv[:, 0], ALU.subtract).then_inc(w_lo, 1)
                dve.wait_ge(const_in, 16 * 8)
                dve.tensor_copy(ident16[:, :], ident[:, :]).then_inc(const_made, 1)
                dve.tensor_copy(masks16[:, :], masks[:, :]).then_inc(const_made, 1)
                dve.tensor_scalar(neg_sink[:, :, :], sink[:, :, :], -1.0, None, ALU.mult).then_inc(const_made, 1)
                dve.memset(zeros, 0.0).then_inc(const_made, 1)
                dve.wait_ge(f_psum_done, 1)
                dve.tensor_scalar(f_tmp[0], s_flat[0][0:FOX_HEADS], b_f[:, :], None, ALU.add).then_inc(f_step, 1)
                dve.wait_ge(f_step, 1)
                dve.tensor_scalar(f_tmp[1], f_tmp[0], -1.0, None, ALU.mult).then_inc(f_step, 1)
                dve.wait_ge(f_step, 2)
                dve.tensor_tensor(f_tmp[1], f_tmp[0], f_tmp[1], ALU.min).then_inc(f_step, 1)
                dve.wait_ge(fa_step, 2)
                dve.tensor_scalar(f_tmp[0], f_tmp[0], 0.0, None, ALU.min).then_inc(f_step, 1)
                dve.wait_ge(f_step, 4)
                dve.tensor_tensor(f_tmp[0], f_tmp[0], f_tmp[2], ALU.subtract).then_inc(f_step, 1)
                dve.wait_ge(f_step, 5)
                dve.wait_ge(const_made, 4)
                dve.tensor_tensor_scan(c_row, f_tmp[0], zeros, 0.0, ALU.add, ALU.add).then_inc(c_done, 1)
                dve.wait_ge(k_raw, 1)
                dve.tensor_tensor(sk_t[:, :], raw[:, :], cos[:, :], ALU.mult).then_inc(kr_step, 1)
                dve.wait_ge(k_rot, 1)
                dve.tensor_tensor(neg_c[:, FOX_HEADS - 1], s_flat[1], sin[:, :], ALU.mult).then_inc(kr_step, 1)
                dve.wait_ge(kr_step, 2)
                dve.tensor_tensor(sk_t[:, :], sk_t[:, :], neg_c[:, FOX_HEADS - 1], ALU.add).then_inc(k_ready, 1)

                def copy_flipped(pair, kp, qb, stored):
                    dve.wait_ge(flipped, TILES * pair + qb + 1)
                    if qb == 0:
                        dve.wait_ge(pair_stored[kp], 32 * (stored + 1))
                    cols = slice(qb * P, (qb + 1) * P)
                    dve.tensor_copy(pair_out[:, kp, 0, cols], o_psum[:, 1]).then_inc(flip_hi, 1)
                    dve.wait_ge(flip_hi, TILES * pair + qb + 1)
                    dve.tensor_tensor(pair_out[:, kp, 1, cols], o_psum[:, 1], pair_out[:, kp, 0, cols], ALU.subtract
                                      ).then_inc(flip_copied, 1)

                def rope(pair, kp, half):
                    n = 2 * pair + half
                    part = slice(half * 512, half * 512 + 512)
                    dve.wait_ge(chunk_done, FOX_CHUNKS * PAIRS + SWA_CHUNKS * pair + 3 + half)
                    dve.tensor_tensor(rope_tmp[:, 0:512], p_psum[:, :], sin[:, part], ALU.mult).then_inc(chunk_copied, 1)
                    dve.tensor_tensor(q_t[kp][:, part], raw[:, part], cos[:, part], ALU.mult).then_inc(sq_step, 1)
                    dve.wait_ge(sq_step, n + 1)
                    dve.wait_ge(chunk_copied, FOX_CHUNKS * PAIRS + SWA_CHUNKS * pair + 3 + half)
                    dve.tensor_tensor(q_t[kp][:, part], q_t[kp][:, part], rope_tmp[:, 0:512], ALU.add).then_inc(sq_ready, 1)

                def bias_and_max(pair, u):
                    qb, hh, n = u // 2, u % 2, UNITS * pair + u
                    length = (qb + 1) * P
                    head = 2 * pair + hh
                    dve.wait_ge(scores_done, n + 1)
                    if u >= PROBS or past(pair):
                        dve.wait_ge(turned, n - PROBS + 1)
                    dve.scalar_tensor_tensor(
                        probs[:, u % PROBS, 0:length],
                        neg_c[:, bass.ds(head, 1), 0:length].rearrange("p o n -> p (o n)"),
                        c_col[:, qb, bass.ds(head, 1)], s_flat[u % 2][:, 0:length],
                        ALU.add, ALU.add).then_inc(biased, 1)
                    dve.wait_ge(biased, n + 1)
                    dve.tensor_reduce(neg_max[:, u % PROBS, 0:1], probs[:, u % PROBS, 0:length], AX.X, ALU.max,
                                      negate=True).then_inc(max_done, 1)

                def scale_out(pair, u):
                    qb, hh, n = u // 2, u % 2, UNITS * pair + u
                    cols = slice(HEAD_DIM * hh, HEAD_DIM * hh + HEAD_DIM)
                    dve.wait_ge(exp_done, n + 1)
                    dve.reciprocal(row_sum[:, u % PROBS, 0:1], row_sum[:, u % PROBS, 0:1]).then_inc(inv_done, 1)
                    dve.wait_ge(pv_done, n + 1)
                    dve.wait_ge(inv_done, n + 1)
                    dve.tensor_scalar(o_rows[:, cols], o_psum[:, 0, cols], row_sum[:, u % PROBS, 0:1], None,
                                      ALU.mult).then_inc(out_scaled, 1)

                def attend(pair, kp, stored, last=False):
                    for u in range(UNITS):
                        if u + 1 < UNITS:
                            bias_and_max(pair, u + 1)
                        elif not last:
                            bias_and_max(pair + 1, 0)
                        if u >= 1:
                            scale_out(pair, u - 1)
                        elif past(pair):
                            scale_out(pair - 1, UNITS - 1)
                        if u >= 2 and u % 2 == 0:
                            copy_flipped(pair, kp, (u - 2) // 2, stored)
                        elif u == 0 and past(pair):
                            copy_flipped(pair - 1, 1 - kp, TILES - 1, 0)
                        if last and u in LAST_FOX_ROTATED:
                            rope(0, 0, LAST_FOX_ROTATED.index(u))
                    if last:
                        scale_out(pair, UNITS - 1)
                        copy_flipped(pair, kp, TILES - 1, 0)

                dve.wait_ge(bcast_copied, FOX_HEADS + 1)
                bias_and_max(0, 0)
                attend(0, 0, 0)
                with dve.Fori(0, PAIRS // 2 - 1) as i:
                    attend(2 * i + 1, 1, i)
                    attend(2 * i + 2, 0, i + 1)
                attend(PAIRS - 1, 1, PAIRS // 2 - 1, last=True)

                def maxima(pair, qb):
                    k, s, n = qb % 2, qb % PROBS, TILES * pair + qb + 1
                    dve.wait_ge(sw_scores, n)
                    dve.tensor_reduce(neg_max[:, s], s_psum[k][:, :, 0:min(qb + 1, 2) * P], AX.X, ALU.max, negate=True
                                      ).then_inc(sw_max, 1)
                    dve.wait_ge(sw_max, n)
                    dve.tensor_tensor(neg_max[:, s], neg_max[:, s],
                                      neg_sink[:, bass.ds(pair, 1), :].rearrange("p o g -> p (o g)"), ALU.min
                                      ).then_inc(sw_neg_max, 1)
                    dve.wait_ge(sw_neg_max, n)
                    dve.tensor_tensor(sink_exp[:, s], neg_max[:, s],
                                      neg_sink[:, bass.ds(pair, 1), :].rearrange("p o g -> p (o g)"), ALU.subtract
                                      ).then_inc(sw_gap, 1)

                def sw_scale_out(pair, qb):
                    s, n = qb % PROBS, TILES * pair + qb + 1
                    dve.wait_ge(sw_exp, n)
                    dve.tensor_tensor(row_sum[:, s], row_sum[:, s], sink_exp[:, s], ALU.add).then_inc(sw_sum, 1)
                    dve.wait_ge(sw_sum, n)
                    dve.reciprocal(row_sum[:, s], row_sum[:, s]).then_inc(sw_inv, 1)
                    dve.wait_ge(sw_pv, n)
                    dve.wait_ge(sw_inv, n)
                    for g in range(2):
                        cols = slice(HEAD_DIM * g, HEAD_DIM * g + HEAD_DIM)
                        scaled = dve.tensor_scalar(o_rows[:, cols], o_psum[:, 0, cols],
                                                   row_sum[:, s, g:g + 1], None, ALU.mult)
                    scaled.then_inc(sw_out_scaled, 1)

                def sw_attend(pair, kp, stored, last=False):
                    for qb in range(TILES):
                        if qb + 1 < TILES:
                            maxima(pair, qb + 1)
                        elif not last:
                            maxima(pair + 1, 0)
                        if qb >= 1:
                            sw_scale_out(pair, qb - 1)
                        elif past(pair):
                            sw_scale_out(pair - 1, TILES - 1)
                        if qb >= 1:
                            copy_flipped(PAIRS + pair, kp, qb - 1, stored)
                        elif past(pair):
                            copy_flipped(PAIRS + pair - 1, 1 - kp, TILES - 1, 0)
                        if not last and qb in SWA_ROTATED:
                            rope(pair + 1, 1 - kp, SWA_ROTATED.index(qb))
                    if last:
                        sw_scale_out(pair, TILES - 1)
                        copy_flipped(PAIRS + pair, kp, TILES - 1, 0)

                maxima(0, 0)
                sw_attend(0, 0, PAIRS // 2)
                with dve.Fori(0, PAIRS // 2 - 1) as i:
                    sw_attend(2 * i + 1, 1, PAIRS // 2 + i)
                    sw_attend(2 * i + 2, 0, PAIRS // 2 + i + 1)
                sw_attend(PAIRS - 1, 1, PAIRS - 1, last=True)

            @block.gpsimd
            def _(pool):
                for n in range(2 * PAIRS):
                    pool.wait_ge(w_pair_in, 16 * (n + 1))
                    pair, k = n % PAIRS, n % 2
                    if n < PAIRS:
                        raw_w, split = w_raw[:, :, :, :], w_pair[:, k]
                        if pair >= 2:
                            pool.wait_ge(chunk_done, FOX_CHUNKS * (pair - 1))
                    else:
                        raw_w, split = w_raw[:, 0], w_sq[:, k]
                        if pair >= 2:
                            pool.wait_ge(chunk_done, FOX_CHUNKS * PAIRS + SWA_CHUNKS * (pair - 2) + 2)
                    pool.tensor_copy(split[:, 0], raw_w).then_inc(pair_hi, 1)
                    pool.wait_ge(pair_hi, n + 1)
                    pool.tensor_tensor(split[:, 1], raw_w, split[:, 0], ALU.subtract).then_inc(pair_lo, 1)
                for c in range(KD):
                    pool.wait_ge(w_o_hi, c + 1)
                    pool.tensor_tensor(xt[:, 1, c], w_o_raw[:, c], xt[:, 0, c], ALU.subtract).then_inc(w_o_lo, 1)

            @block.scalar
            def _(act):
                def copy_chunk(pair, kp, chunk):
                    act.wait_ge(chunk_done, FOX_CHUNKS * pair + chunk + 1)
                    half = chunk % 2
                    part = slice(half * 512, half * 512 + 512)
                    if chunk < 2:
                        cp = act.activation(q_t[kp][:, part], p_psum[:, :], ACT.Copy, scale=SCALE)
                    elif chunk < 4:
                        cp = act.activation(k_t[kp][:, part], p_psum[:, :], ACT.Copy)
                    else:
                        cp = act.activation(v_rows[kp][:, 4 * half:4 * half + 4].rearrange("p t c -> p (t c)"),
                                            p_psum[:, :], ACT.Copy)
                    cp.then_inc(chunk_copied, 1)

                def copy_raw(pair, half):
                    act.wait_ge(chunk_done, FOX_CHUNKS * PAIRS + SWA_CHUNKS * pair + half + 1)
                    if past(pair):
                        act.wait_ge(sq_ready, 2 * pair)
                    act.activation(raw[:, half * 512:half * 512 + 512], p_psum[:, :], ACT.Copy, scale=SCALE
                                   ).then_inc(chunk_copied, 1)

                for c in range(KD):
                    if c % 2 == 0:
                        act.wait_ge(x_in[c // 2], 32)
                    act.activation(xt[:, 0, c], x_raw[:, c], ACT.Copy).then_inc(x_hi, 1)
                    if c == 0:
                        act.wait_ge(w_first_in, 32)
                        act.activation(w_f[:, 0], w_f_raw[:, :, :], ACT.Copy).then_inc(w_hi, 1)
                        act.activation(w_kv[:, 0], w_kv_raw, ACT.Copy).then_inc(w_hi, 1)
                act.wait_ge(f_step, 3)
                act.activation(f_tmp[2], f_tmp[1], ACT.Exp).then_inc(fa_step, 1)
                act.wait_ge(fa_step, 1)
                act.activation(f_tmp[2], f_tmp[2], ACT.Ln, bias=1.0).then_inc(fa_step, 1)
                act.wait_ge(k_proj, 1)
                act.activation(raw[:, :], s_flat[1], ACT.Copy).then_inc(k_raw, 1)
                act.wait_ge(v_proj, 1)
                for k in range(2):
                    act.activation(sv_rows[:, 4 * k:4 * k + 4].rearrange("p t c -> p (t c)"), t_psum[k][:, :],
                                   ACT.Copy).then_inc(v_ready, 1)
                copy_chunk(0, 0, 0)
                copy_chunk(0, 0, 1)
                for h in range(FOX_HEADS):
                    act.wait_ge(bcast_done, h + 1)
                    if h == FOX_HEADS - 1:
                        act.wait_ge(k_ready, 1)
                    act.activation(neg_c[:, h], s_flat[h % 2], ACT.Copy).then_inc(bcast_copied, 1)
                    if h % 2:
                        copy_chunk(0, 0, 2 + h // 2)
                act.wait_ge(bcast_done, FOX_HEADS + 1)
                act.activation(c_col[:, :, :].rearrange("p t h -> p (t h)"), t_psum[0][:, 0:TILES * FOX_HEADS],
                               ACT.Copy).then_inc(bcast_copied, 1)

                def exponentials(pair, u):
                    length = (u // 2 + 1) * P
                    act.wait_ge(max_done, UNITS * pair + u + 1)
                    act.activation(probs[:, u % PROBS, 0:length], probs[:, u % PROBS, 0:length], ACT.Exp,
                                   bias=neg_max[:, u % PROBS, 0:1], accum_out=row_sum[:, u % PROBS, 0:1]
                                   ).then_inc(exp_done, 1)

                def copy_turned(pair, u):
                    n = UNITS * pair + u
                    act.wait_ge(turned, n + 1)
                    if u >= 2 or past(pair):
                        act.wait_ge(pv_done, n - 1)
                    blocks = u // 2 + 1
                    for bank in range((blocks + 3) // 4):
                        width = min(4, blocks - 4 * bank) * P
                        cp = act.activation(probs_t[:, u % 2, bank * 512:bank * 512 + width],
                                            t_psum[bank][:, 0:width], ACT.Copy)
                    cp.then_inc(turn_copied, 1)

                def attend(pair, kp, last=False):
                    for u in range(UNITS):
                        if u + 1 < UNITS:
                            exponentials(pair, u + 1)
                        elif not last:
                            exponentials(pair + 1, 0)
                        copy_turned(pair, u)
                        if last and u in LAST_FOX_PROJECTED:
                            copy_raw(0, LAST_FOX_PROJECTED.index(u))
                        if not last and u in FOX_PROJECTED:
                            copy_chunk(pair + 1, 1 - kp, FOX_PROJECTED.index(u))

                exponentials(0, 0)
                attend(0, 0)
                with act.Fori(0, PAIRS // 2 - 1) as i:
                    attend(2 * i + 1, 1)
                    attend(2 * i + 2, 0)
                attend(PAIRS - 1, 1, last=True)

                def sw_exponentials(pair, qb):
                    k, s, n = qb % 2, qb % PROBS, TILES * pair + qb + 1
                    act.wait_ge(sw_gap, n)
                    if qb >= PROBS or past(pair):
                        act.wait_ge(sw_turned, n - PROBS)
                    for g in range(2):
                        keys = min(qb + 1, 2) * P
                        act.activation(probs[:, s, g * 256:g * 256 + keys], s_psum[k][:, g, 0:keys],
                                       ACT.Exp, bias=neg_max[:, s, g:g + 1], accum_out=row_sum[:, s, g:g + 1])
                    act.activation(sink_exp[:, s], sink_exp[:, s], ACT.Exp).then_inc(sw_exp, 1)

                def sw_copy_turned(pair, qb):
                    k, n = qb % 2, TILES * pair + qb + 1
                    act.wait_ge(sw_turned, n)
                    if qb >= 2 or past(pair):
                        act.wait_ge(sw_pv, n - 2)
                    keys = min(qb + 1, 2) * P
                    act.activation(probs_t[:, k, 0:512].rearrange("p (g n) -> p g n", g=2)[:, :, 0:keys],
                                   t_psum[k][:, :].rearrange("p (g n) -> p g n", g=2)[:, :, 0:keys],
                                   ACT.Copy).then_inc(sw_turn_copied, 1)

                def sw_attend(pair, last=False):
                    if last:
                        act.wait_ge(chunk_done, (FOX_CHUNKS + SWA_CHUNKS) * PAIRS)
                    for qb in range(TILES):
                        if qb + 1 < TILES:
                            sw_exponentials(pair, qb + 1)
                        elif not last:
                            sw_exponentials(pair + 1, 0)
                        sw_copy_turned(pair, qb)
                        if last:
                            if qb == 0:
                                act.wait_ge(w_o_in, 16)
                            act.activation(xt[:, 0, qb], w_o_raw[:, qb], ACT.Copy).then_inc(w_o_hi, 1)
                        if not last and qb in SWA_PROJECTED:
                            copy_raw(pair + 1, SWA_PROJECTED.index(qb))

                sw_exponentials(0, 0)
                sw_attend(0)
                with act.Fori(0, PAIRS // 2 - 1) as i:
                    sw_attend(2 * i + 1)
                    sw_attend(2 * i + 2)
                sw_attend(PAIRS - 1, last=True)


def routing_phase(nc, mixed_t, x_rows, ln1_g, ln1_b, w_query, sub_keys, consts, x1_rows, x1_split, gates,
                  pick_index, pick_gate, wide, early, load_early, load_rows_of_x1):
    with ExitStack() as ctx:
        sem = lambda name: ctx.enter_context(nc.semaphore(name))

        def tiles_in(scope):
            return lambda name, shape, dt=F32: scope.enter_context(nc.sbuf_tensor("rt_" + name, shape, dt))

        sb = tiles_in(ctx)
        w_q = early.rearrange("p (s c n) -> p s c n", s=SETS, c=KD)
        keys = sb("keys", [P, SETS, N_KEYS])
        x1_t = sb("x1_t", [P, KD, SEQ])
        ident = sb("ident", [P, P])
        iota = sb("iota", [P, N_KEYS])
        wide_psum = ctx.enter_context(nc.psum_tensor("wide_psum", [P, D_MODEL], F32))
        t_psum = [ctx.enter_context(nc.psum_tensor(f"r_t_psum{k}", [P, 512], F32)) for k in range(2)]
        s_psum = [ctx.enter_context(nc.psum_tensor(f"r_s_psum{k}", [P, 512], F32)) for k in range(2)]
        g_psum = [ctx.enter_context(nc.psum_tensor(f"g_psum{k}", [P, 4, N_KEYS], F32)) for k in range(2)]
        keys_in, const_in = sem("keys_in"), sem("r_const_in")
        first_sets_in, q_done = sem("first_sets_in"), sem("q_done")

        with ExitStack() as scope:
            sb = tiles_in(scope)
            w_o = wide.rearrange("p c n -> p (c n)").bitcast(BF16).rearrange("p (h c n) -> p h c n", h=2, c=KD)
            mixed = sb("mixed", [P, 2, 2, KD, P], BF16)
            rows = sb("rows", [P, 2, D_MODEL])
            split = sb("split", [P, 2, 2, KD, P], BF16)
            ln_g, ln_b = sb("ln_g", [P, D_MODEL]), sb("ln_b", [P, D_MODEL])
            eps = sb("eps", [P, 1])
            stats, moments = sb("stats", [P, 2, 6]), sb("moments", [P, 2])
            std, rstd, newton = sb("std", [P, 1]), sb("rstd", [P, 1]), sb("newton", [P, 1])
            ln_in = sem("r_ln_in")
            mixed_in = [sem(f"mixed_in{k}") for k in range(2)]
            rows_in = [sem(f"rows_in{k}") for k in range(2)]
            eps_set, mix_done, summed, stats_done = sem("r_eps_set"), sem("mix_done"), sem("summed"), sem("r_stats_done")
            moments_done, std_done, rstd_step = sem("r_moments_done"), sem("r_std_done"), sem("r_rstd_step")
            norm_step, x1_done, turned = sem("norm_step"), sem("x1_done"), sem("r_turned")
            x1_t_ready, hi_ready, lo_ready = sem("x1_t_ready"), sem("hi_ready"), sem("lo_ready")
            x1_stored = [sem(f"x1_stored{k}") for k in range(2)]
            split_stored = [sem(f"split_stored{k}") for k in range(2)]

            with nc.Block() as block:
                @block.sync
                def _(sp):
                    def load_mixed(t):
                        sp.dma_start(mixed[:, t % 2], mixed_t[t]).then_inc(mixed_in[t % 2], 16)

                    def load_rows(t):
                        sp.dma_start(rows[:, t % 2], x_rows[t]).then_inc(rows_in[t % 2], 16)

                    load_mixed(0)
                    load_rows(0)
                    sp.dma_start(ln_g[:, :], ln1_g.partition_broadcast(P)).then_inc(ln_in, 16)
                    sp.dma_start(ln_b[:, :], ln1_b.partition_broadcast(P)).then_inc(ln_in, 16)
                    load_mixed(1)
                    load_rows(1)
                    sp.dma_start(ident[:, :], consts["ident"]).then_inc(const_in, 16)
                    sp.dma_start(iota[:, :], consts["iota"]).then_inc(const_in, 16)
                    for t in range(TILES):
                        k = t % 2
                        if t + 2 < TILES:
                            sp.wait_ge(mix_done, t + 1)
                            load_mixed(t + 2)
                        sp.wait_ge(x1_done, t + 1)
                        sp.dma_start(x1_rows[t], rows[:, k]).then_inc(x1_stored[k], 16)
                        sp.dma_start(w_q[:, 2 * t:2 * t + 2], w_query[:, 2 * t:2 * t + 2]
                                     ).then_inc(first_sets_in if t < 4 else keys_in, 16)
                        if t + 2 < TILES:
                            sp.wait_ge(x1_stored[k], 16 * (t // 2 + 1))
                            sp.wait_ge(turned, t + 1)
                            load_rows(t + 2)
                        sp.wait_ge(lo_ready, t + 1)
                        sp.dma_start(x1_split[t], split[:, k]).then_inc(split_stored[k], 16)
                    sp.dma_start(keys[:, :, :], sub_keys).then_inc(keys_in, 16)
                    for k in range(2):
                        sp.wait_ge(x1_stored[k], 16 * (TILES // 2))
                        sp.wait_ge(split_stored[k], 16 * (TILES // 2))
                    sp.wait_ge(keys_in, 16 * (TILES - 4 + 1))

                @block.tensor
                def _(pe):
                    def mix(t, k, n):
                        pe.wait_ge(mixed_in[k], 16 * n)
                        if past(t):
                            pe.wait_ge(summed, t)
                        for c in range(KD):
                            for a, b in ((0, 0), (0, 1), (1, 0)):
                                for half in range(2):
                                    mm = pe.matmul(wide_psum[:, half * 512:half * 512 + 512], mixed[:, k, a, c],
                                                   w_o[:, b, c, half * 512:half * 512 + 512],
                                                   start=(c == 0 and a + b == 0), stop=(c == KD - 1 and a == 1))
                        mm.then_inc(mix_done, 1)

                    def turn(t, k):
                        pe.wait_ge(x1_done, t + 1)
                        if past(t):
                            pe.wait_ge(hi_ready, t)
                        for c in range(KD):
                            mm = pe.transpose(t_psum[c // 4][:, c % 4 * P:c % 4 * P + P],
                                              rows[:, k, c * P:(c + 1) * P], ident[:, :])
                        mm.then_inc(turned, 1)

                    mix(0, 0, 1)
                    pe.wait_ge(const_in, 32)
                    mix(1, 1, 1)
                    turn(0, 0)
                    with pe.Fori(1, TILES // 2) as i:
                        mix(2 * i, 0, i + 1)
                        turn(2 * i - 1, 1)
                        mix(2 * i + 1, 1, i + 1)
                        turn(2 * i, 0)
                    pe.wait_ge(first_sets_in, 16 * 4)
                    for unit in range(8):
                        for c in range(KD):
                            mm = pe.matmul(g_psum[unit // 4][:, unit % 4], w_q[:, unit, c], x1_t[:, c, 0:P],
                                           start=(c == 0), stop=(c == KD - 1))
                        if unit % 4 == 3:
                            mm.then_inc(q_done, 1)
                    turn(TILES - 1, 1)

                @block.vector
                def _(dve):
                    dve.memset(eps[:, :], LN_EPS).then_inc(eps_set, 1)

                    def normalise(t, k, n):
                        dve.wait_ge(rows_in[k], 16 * n)
                        dve.wait_ge(mix_done, t + 1)
                        dve.scalar_tensor_tensor(rows[:, k], rows[:, k], ALPHA, wide_psum[:, :], ALU.mult, ALU.add
                                                 ).then_inc(summed, 1)
                        dve.wait_ge(summed, t + 1)
                        dve.bn_stats(stats[:, 0], rows[:, k, 0:512])
                        dve.bn_stats(stats[:, 1], rows[:, k, 512:1024]).then_inc(stats_done, 1)
                        dve.wait_ge(stats_done, t + 1)
                        dve.nop(nofuse=True)
                        dve.bn_aggr(moments[:, :], stats[:, :, :]).then_inc(moments_done, 1)
                        newton_rstd(dve, moments[:, :], std[:, :], rstd[:, :], newton[:, :],
                                    moments_done, t + 1, std_done, t + 1, rstd_step, 5 * t)
                        dve.tensor_scalar(rows[:, k], rows[:, k], moments[:, 0:1], rstd[:, :],
                                          ALU.subtract, ALU.mult).then_inc(norm_step, 1)
                        dve.wait_ge(norm_step, 2 * t + 1)
                        dve.tensor_tensor(rows[:, k], rows[:, k], ln_g[:, :], ALU.mult).then_inc(norm_step, 1)
                        dve.wait_ge(norm_step, 2 * t + 2)
                        dve.tensor_tensor(rows[:, k], rows[:, k], ln_b[:, :], ALU.add).then_inc(x1_done, 1)

                    dve.wait_ge(ln_in, 32)
                    with dve.Fori(0, TILES // 2) as i:
                        normalise(2 * i, 0, i + 1)
                        normalise(2 * i + 1, 1, i + 1)

                @block.scalar
                def _(act):
                    def root_and_copies(t, k, stored):
                        act.wait_ge(moments_done, t + 1)
                        act.activation(std[:, :], moments[:, 1:2], ACT.Sqrt, bias=eps[:, :]).then_inc(std_done, 1)
                        act.wait_ge(turned, t + 1)
                        for bank in range(2):
                            cp = act.activation(x1_t[:, 4 * bank:4 * bank + 4, bass.ds(t * P, P)],
                                                t_psum[bank][:, :].rearrange("p (c n) -> p c n", n=P), ACT.Copy)
                        cp.then_inc(x1_t_ready, 1)
                        if past(stored):
                            act.wait_ge(split_stored[k], 16 * stored)
                        for bank in range(2):
                            cp = act.activation(split[:, k, 0, 4 * bank:4 * bank + 4],
                                                t_psum[bank][:, :].rearrange("p (c n) -> p c n", n=P), ACT.Copy)
                        cp.then_inc(hi_ready, 1)

                    act.wait_ge(eps_set, 1)
                    root_and_copies(0, 0, 0)
                    root_and_copies(1, 1, 0)
                    with act.Fori(1, TILES // 2) as i:
                        root_and_copies(2 * i, 0, i)
                        root_and_copies(2 * i + 1, 1, i)

                @block.gpsimd
                def _(pool):
                    def low_half(t, k):
                        pool.wait_ge(x1_t_ready, t + 1)
                        pool.wait_ge(hi_ready, t + 1)
                        pool.tensor_tensor(split[:, k, 1], x1_t[:, :, bass.ds(t * P, P)], split[:, k, 0],
                                           ALU.subtract).then_inc(lo_ready, 1)

                    with pool.Fori(0, TILES // 2) as i:
                        low_half(2 * i, 0)
                        low_half(2 * i + 1, 1)

        sb = tiles_in(ctx)
        q_t = sb("q_t", [P, 4, 4, P])
        scores = sb("scores", [P, SETS, N_KEYS])
        top = sb("top", [P, SETS, TOPK])
        top_u = sb("top_u", [P, SETS, TOPK], U32)
        top_i = sb("top_i", [P, 2, TOPK, PEER_HEADS], BF16)
        FEW = 4
        SUMS = FEW * TOPK + (TOPK - FEW) * FEW
        cand = sb("cand", [P, PEER_HEADS, SUMS])
        best = sb("best", [P, PEER_HEADS, TOPK])
        pos = sb("pos", [P, PEER_HEADS * TOPK], U32)
        pair_u = sb("pair_u", [P, 2, PEER_HEADS * TOPK], U32)
        pair_f = sb("pair_f", [P, TOPK, PEER_HEADS])
        pair_i = sb("pair_i", [P, 2, TOPK, PEER_HEADS], BF16)
        found = sb("found", [P, 2, TOPK, TOPK, PEER_HEADS], BF16)
        places = sb("places", [P, TOPK, PEER_HEADS * TOPK], BF16)
        picked = sb("picked", [P, 3, PEER_HEADS * TOPK])
        gate_sum = sb("gate_sum", [P, PEER_HEADS])
        picked_t = sb("picked_t", [P, 4, P], BF16)
        gate_t = sb("gate_t", [P, P])
        HOTS = 2
        BATCH = 8
        hot = sb("hot", [P, HOTS, 4, N_KEYS, BATCH], BF16)
        key_table = sb("key_table", [P, N_KEYS, BATCH], BF16)
        stage = wide.rearrange("p (k r) (h t) -> p k (r h) t", k=2, t=CHUNK)
        q_copied, s_done, s_copied = sem("q_copied"), sem("s_done"), sem("s_copied")
        top_step, floated = sem("top_step"), sem("floated")
        cand_made, cand_step, pair_step, low_placed, halved, soft_step, exp_done = (
            sem("cand_made"), sem("cand_step"), sem("pair_step"), sem("low_placed"), sem("halved"), sem("soft_step"), sem("r_exp_done"))
        find_dve, find_pool, picked_ready = sem("find_dve"), sem("find_pool"), sem("picked_ready")
        table_made, high_made, gate_split, kept = sem("table_made"), sem("high_made"), sem("gate_split"), sem("kept")
        picks_turned, picks_copied = sem("picks_turned"), sem("picks_copied")
        hot_dve, hot_low, summed_gates, g_copied = sem("hot_dve"), sem("hot_low"), sem("summed_gates"), sem("g_copied")
        stage_stored = [sem(f"stage_stored{k}") for k in range(2)]
        SLOTS = P // BATCH
        CHUNKS = P // CHUNK
        UNITS_DONE = (2, 4, 6, 8, 9, 10, 11, 12, 13, 14, 15, 16, 16, 16, 16, 16)
        SCORES_SLOT = (5, 6, 9, 13)
        PRODUCTS_SLOT = 6
        LOW_KEY_SLOT = PRODUCTS_SLOT + 4
        SOFTMAX_SLOT = PRODUCTS_SLOT + 4
        DVE_LOW_SLOTS = (4, 11)

        with nc.Block() as block:
            @block.sync
            def _(sp):
                for k in range(2):
                    sp.sem_inc(stage_stored[k], 16)
                with sp.Fori(0, DENSE * CHUNKS // 2) as i:
                    for k in range(2):
                        sp.wait_ge(g_copied, (2 * i + k + 1) * (CHUNK // 4) + 2)
                        sp.dma_start(gates[:, bass.ds(2 * i + k, 1)].rearrange("p o h t -> p (o h t)"),
                                     stage[:, k].rearrange("p h t -> p (h t)")).then_inc(stage_stored[k], 16)
                sp.wait_ge(q_done, 4 * TILES)
                load_early(sp)
                for k in range(2):
                    sp.wait_ge(stage_stored[k], 16 * (DENSE * CHUNKS // 2 + 1))
                load_rows_of_x1(sp)

            @block.tensor
            def _(pe):
                def query(t, unit):
                    n, j = unit // 4, unit % 4
                    if j == 0 and past(t):
                        pe.wait_ge(q_copied, 4 * t + n - 1)
                    for c in range(KD):
                        mm = pe.matmul(t_psum[n % 2][:, j * P:(j + 1) * P], w_q[:, unit, c],
                                       x1_t[:, c, bass.ds(t * P, P)], start=(c == 0), stop=(c == KD - 1))
                    if j == 3:
                        mm.then_inc(q_done, 1)

                def key_scores(t, n, picks=0):
                    pe.wait_ge(q_copied, 4 * t + n + 1)
                    if n >= 2 or past(t):
                        pe.wait_ge(s_copied, 4 * t + n - 1)
                    if n == 0 and past(picks):
                        pe.wait_ge(picks_copied, picks)
                    for j in range(4):
                        mm = pe.matmul(s_psum[n % 2][:, j * P:(j + 1) * P], q_t[:, n, j], keys[:, 4 * n + j],
                                       start=True, stop=True)
                    mm.then_inc(s_done, 1)

                def turn_picks(d):
                    pe.wait_ge(picked_ready, d + 1)
                    pe.wait_ge(s_copied, 4 * d + 7)
                    for j in range(3):
                        mm = pe.transpose(s_psum[0][:, j * P:(j + 1) * P], picked[:, j], ident[:, :])
                    mm.then_inc(picks_turned, 1)

                def gate_batch(d, m):
                    n = SLOTS * d + m
                    pe.wait_ge(hot_dve, n + 1)
                    pe.wait_ge(hot_low, n + 1)
                    for four in range(BATCH // 4):
                        pe.wait_ge(g_copied, 2 * n + four + 1)
                        for j in range(4 * four, 4 * four + 4):
                            for part in range(2):
                                mm = pe.matmul(g_psum[four % 2][:, j % 4], hot[:, m % HOTS, 1, :, j],
                                               hot[:, m % HOTS, 2 + part, :, j], start=(part == 0), stop=(part == 1))
                        mm.then_inc(summed_gates, 1)

                def step(t):
                    turn_picks(t - 1)
                    for m in range(SLOTS):
                        for unit in range(UNITS_DONE[m - 1] if m else 0, UNITS_DONE[m]):
                            query(t + 1, unit)
                        if m in SCORES_SLOT:
                            key_scores(t + 1, SCORES_SLOT.index(m), t)
                        gate_batch(t - 1, m)

                pe.sem_inc(summed_gates, 2 * HOTS)
                pe.sem_inc(g_copied, 2)
                pe.sem_inc(picks_turned, 1)
                for t in range(2):
                    if t > 0:
                        for unit in range(4):
                            query(t, unit)
                    for n in range(4):
                        for unit in range(4 * n + 4, min(4 * n + 8, SETS)):
                            if t > 0 or unit >= 8:
                                query(t, unit)
                        key_scores(t, n)
                with pe.Fori(1, DENSE + 1) as t:
                    step(t)

            @block.scalar
            def _(act):
                def copy_query(t, n):
                    act.wait_ge(q_done, 4 * t + n + 1)
                    if past(t):
                        act.wait_ge(s_done, 4 * t + n - 3)
                    if past(t) or n >= 2:
                        source = t_psum[n % 2][:, :]
                    else:
                        source = g_psum[n][:, :, :].rearrange("p j n -> p (j n)")
                    act.activation(q_t[:, n].rearrange("p j n -> p (j n)"), source, ACT.Copy).then_inc(q_copied, 1)

                def copy_scores(t, n):
                    act.wait_ge(s_done, 4 * t + n + 1)
                    if n == 0 and past(t):
                        act.wait_ge(top_step, 5 * t)
                    act.activation(scores[:, 4 * n:4 * n + 4].rearrange("p j n -> p (j n)"),
                                   s_psum[n % 2][:, :], ACT.Copy).then_inc(s_copied, 1)

                def softmax(t):
                    act.wait_ge(soft_step, 3 * t + 1)
                    act.activation(best[:, :, :], best[:, :, :], ACT.Exp).then_inc(exp_done, 1)

                def copy_gates(d, m):
                    for four in range(2):
                        token = (BATCH * m + 4 * four) % CHUNK
                        chunk, k = BATCH * m // CHUNK, BATCH * m // CHUNK % 2
                        act.wait_ge(summed_gates, 2 * (SLOTS * d + m) + four + 1 + 2 * HOTS)
                        if token == 0:
                            act.wait_ge(stage_stored[k], 16 * (CHUNKS // 2 * d + chunk // 2 + 1))
                        act.activation(stage[:, k, :, token:token + 4].rearrange("p h t -> p t h"),
                                       g_psum[four][:, :, :], ACT.Copy).then_inc(g_copied, 1)

                def step(t):
                    act.wait_ge(picks_turned, t + 1)
                    act.activation(picked_t[:, 0:2].rearrange("p j n -> p (j n)"), s_psum[0][:, 0:2 * P], ACT.Copy)
                    act.activation(gate_t[:, :], s_psum[0][:, 2 * P:3 * P], ACT.Copy)
                    act.activation(picked_t[:, 2], s_psum[0][:, 2 * P:3 * P], ACT.Copy).then_inc(picks_copied, 1)
                    for m in range(SLOTS):
                        if UNITS_DONE[m] % 4 == 0 and (UNITS_DONE[m - 1] if m else 0) < UNITS_DONE[m]:
                            copy_query(t + 1, UNITS_DONE[m] // 4 - 1)
                        if m in SCORES_SLOT:
                            copy_scores(t + 1, SCORES_SLOT.index(m))
                        copy_gates(t - 1, m)
                        if m == SOFTMAX_SLOT:
                            softmax(t)

                for t in range(2):
                    copy_query(t, 0)
                    for n in range(4):
                        if n < 3:
                            copy_query(t, n + 1)
                        copy_scores(t, n)
                softmax(0)
                with act.Fori(1, DENSE + 1) as t:
                    step(t)
                softmax(TILES - 1)

            @block.gpsimd
            def _(pool):
                def products(t):
                    tops = top[:, :, :].rearrange("p (h s) a -> p h s a", s=2)
                    pool.wait_ge(top_step, 5 * t + 4)
                    pool.nop(nofuse=True)
                    for i0, i1, js in ((0, FEW, TOPK), (FEW, TOPK, FEW)):
                        at, shape = i0 * TOPK, [P, PEER_HEADS, i1 - i0, js]
                        op = pool.tensor_tensor(
                            cand[:, :, at:at + (i1 - i0) * js].rearrange("p h (i j) -> p h i j", j=js),
                            tops[:, :, 0, i0:i1].unsqueeze(3).broadcast_to(shape),
                            tops[:, :, 1:2, 0:js].broadcast_to(shape), ALU.add)
                    op.then_inc(cand_made, 1)

                def float_index(t):
                    pool.wait_ge(top_step, 5 * t + 5)
                    pool.nop(nofuse=True)
                    pool.tensor_copy(top_i[:, :, :, :], top_u[:, :, :].rearrange("p (h s) a -> p s a h", s=2)
                                     ).then_inc(floated, 1)

                def low_key(t):
                    pool.wait_ge(find_dve, 3 * t + 1)
                    pool.wait_ge(floated, t + 2)
                    pool.tensor_tensor(found[:, 1], found[:, 1], top_i[:, 1].unsqueeze(2).broadcast_to(
                        [P, TOPK, TOPK, PEER_HEADS]), ALU.mult).then_inc(find_pool, 1)

                def low_half(d, m):
                    n = SLOTS * d + m
                    pool.wait_ge(high_made, n + 1)
                    pool.wait_ge(summed_gates, 2 * n + 2)
                    pool.nop(nofuse=True)
                    pool.tensor_tensor(hot[:, m % HOTS, 3], hot[:, m % HOTS, 0],
                                       picked_t[:, 3, BATCH * m:BATCH * (m + 1)].unsqueeze(1)
                                       .broadcast_to([P, N_KEYS, BATCH]), ALU.mult).then_inc(hot_low, 1)

                def step(t):
                    pool.wait_ge(picks_copied, t)
                    pool.tensor_tensor(picked_t[:, 3], gate_t[:, :], picked_t[:, 2], ALU.subtract
                                       ).then_inc(gate_split, 1)
                    pool.wait_ge(gate_split, t)
                    pool.nop(nofuse=True)
                    for m in range(SLOTS):
                        if m not in DVE_LOW_SLOTS:
                            low_half(t - 1, m)
                        if m == PRODUCTS_SLOT - 3:
                            products(t)
                        if m == PRODUCTS_SLOT - 2:
                            float_index(t)
                        if m == LOW_KEY_SLOT:
                            low_key(t)

                pool.sem_inc(floated, 1)
                products(0)
                float_index(0)
                low_key(0)
                with pool.Fori(1, DENSE + 1) as t:
                    step(t)
                products(TILES - 1)
                float_index(TILES - 1)
                low_key(TILES - 1)

            @block.vector
            def _(dve):
                tops = (lambda s, a: top[:, s, 8 * a:8 * a + 8], lambda s, a: top_u[:, s, 8 * a:8 * a + 8])

                def top_of_sets(t, stage_no):
                    if stage_no == 0:
                        dve.wait_ge(s_copied, 4 * t + 4)
                    else:
                        dve.wait_ge(top_step, 5 * t + stage_no)
                    if stage_no == 1:
                        dve.wait_ge(floated, t + 1)
                    dve.nop(nofuse=True)
                    for s in range(SETS):
                        if stage_no in (0, 3):
                            op = dve.max(tops[0](s, stage_no // 3), scores[:, s])
                        elif stage_no in (1, 4):
                            op = dve.max_index(tops[1](s, stage_no // 4), tops[0](s, stage_no // 4), scores[:, s])
                        else:
                            op = dve.match_replace(scores[:, s], tops[0](s, 0), scores[:, s], LOW)
                    op.then_inc(top_step, 1)

                def top_of_products(t, stage_no):
                    if stage_no == 0:
                        dve.wait_ge(cand_made, t + 1)
                    else:
                        dve.wait_ge(cand_step, 5 * t + stage_no)
                    dve.nop(nofuse=True)
                    for h in range(PEER_HEADS):
                        a = stage_no // 3
                        place = pos[:, h * TOPK + 8 * a:h * TOPK + 8 * a + 8]
                        if stage_no in (0, 3):
                            op = dve.max(best[:, h, 8 * a:8 * a + 8], cand[:, h])
                        elif stage_no in (1, 4):
                            op = dve.max_index(place, best[:, h, 8 * a:8 * a + 8], cand[:, h])
                        else:
                            op = dve.match_replace(cand[:, h], best[:, h, 0:8], cand[:, h], LOW)
                    op.then_inc(cand_step, 1)

                def find_low(t):
                    first, width = FEW * TOPK - FEW * FEW, PEER_HEADS * TOPK
                    dve.wait_ge(cand_step, 5 * t + 5)
                    dve.nop(nofuse=True)
                    dve.tensor_scalar(pair_u[:, 1], pos[:, :], float(first), float(first), ALU.max, ALU.subtract
                                      ).then_inc(pair_step, 1)
                    dve.tensor_scalar(pair_u[:, 0], pos[:, :], 4, None, ALU.logical_shift_right)
                    dve.tensor_copy(gate_sum[:, :], best[:, :, 0]).then_inc(pair_step, 1)
                    dve.wait_ge(pair_step, 6 * t + 1)
                    dve.tensor_scalar(pair_u[:, 1], pair_u[:, 1], 2, None, ALU.logical_shift_right).then_inc(pair_step, 1)
                    dve.wait_ge(pair_step, 6 * t + 2)
                    dve.tensor_tensor(best[:, :, :], best[:, :, :],
                                      gate_sum[:, :].unsqueeze(2).broadcast_to([P, PEER_HEADS, TOPK]),
                                      ALU.subtract).then_inc(soft_step, 1)
                    dve.wait_ge(pair_step, 6 * t + 3)
                    by_head = "p (h k) -> p k h"
                    dve.tensor_tensor(pair_i[:, 0], pair_u[:, 0].rearrange(by_head, k=TOPK),
                                      pair_u[:, 1].rearrange(by_head, k=TOPK), ALU.max).then_inc(pair_step, 1)
                    dve.wait_ge(pair_step, 6 * t + 4)
                    dve.tensor_scalar(pair_f[:, :, :], pair_i[:, 0], -float(FEW), -float(first), ALU.mult, ALU.add
                                      ).then_inc(pair_step, 1)
                    dve.wait_ge(pair_step, 6 * t + 5)
                    dve.scalar_tensor_tensor(pair_f[:, :, :], pair_i[:, 0], -float(TOPK), pair_f[:, :, :], ALU.mult, ALU.max
                                             ).then_inc(pair_step, 1)
                    dve.wait_ge(pair_step, 6 * t + 6)
                    dve.tensor_tensor(pair_i[:, 1], pos[:, :].rearrange(by_head, k=TOPK), pair_f[:, :, :], ALU.add).then_inc(low_placed, 1)
                    dve.wait_ge(low_placed, t + 1)
                    dve.tensor_tensor(found[:, 1].rearrange("p a k h -> p a (k h)"),
                                      pair_i[:, 1].rearrange("p k h -> p (k h)").unsqueeze(1)
                                      .broadcast_to([P, TOPK, PEER_HEADS * TOPK]), places[:, :, :], ALU.is_equal
                                      ).then_inc(find_dve, 1)

                def find_high(t):
                    dve.tensor_tensor(found[:, 0].rearrange("p a k h -> p a (k h)"),
                                      pair_i[:, 0].rearrange("p k h -> p (k h)").unsqueeze(1)
                                      .broadcast_to([P, TOPK, PEER_HEADS * TOPK]), places[:, :, :], ALU.is_equal
                                      ).then_inc(find_dve, 1)
                    dve.wait_ge(find_dve, 3 * t + 2)
                    dve.wait_ge(floated, t + 2)
                    dve.tensor_tensor(found[:, 0], found[:, 0], top_i[:, 0].unsqueeze(2).broadcast_to(
                        [P, TOPK, TOPK, PEER_HEADS]), ALU.mult).then_inc(find_dve, 1)

                def halve(t, level):
                    half = TOPK >> (level + 1)
                    if level == 0:
                        dve.wait_ge(find_dve, 3 * t + 3)
                        dve.wait_ge(find_pool, t + 1)
                    else:
                        dve.wait_ge(halved, 4 * t + level)
                    if half > 1:
                        total = found[:, :, 0:half]
                    else:
                        total = picked[:, 0:2].rearrange("p s (h k) -> p s k h", k=TOPK).unsqueeze(2)
                    dve.tensor_tensor(total, found[:, :, 0:half], found[:, :, half:2 * half], ALU.add
                                      ).then_inc(halved, 1)

                def sum_gates(t):
                    dve.wait_ge(exp_done, t + 1)
                    dve.tensor_reduce(gate_sum[:, :], best[:, :, :], AX.X, ALU.add).then_inc(soft_step, 1)

                def pick_gates(t):
                    dve.wait_ge(soft_step, 3 * t + 2)
                    dve.reciprocal(gate_sum[:, :], gate_sum[:, :]).then_inc(soft_step, 1)
                    dve.wait_ge(soft_step, 3 * t + 3)
                    dve.wait_ge(halved, 4 * t + 4)
                    dve.tensor_tensor(picked[:, 2].rearrange("p (h k) -> p h k", k=TOPK), best[:, :, :],
                                      gate_sum[:, :].unsqueeze(2).broadcast_to([P, PEER_HEADS, TOPK]),
                                      ALU.mult).then_inc(picked_ready, 1)

                def pick(t, slot, picks):
                    if slot < 5:
                        top_of_sets(t, slot)
                    elif PRODUCTS_SLOT <= slot < PRODUCTS_SLOT + 5:
                        top_of_products(t, slot - PRODUCTS_SLOT)
                    elif slot == PRODUCTS_SLOT + 5:
                        find_low(t)
                    elif slot == PRODUCTS_SLOT + 6:
                        find_high(t)
                    elif slot == PRODUCTS_SLOT + 7:
                        halve(t, 0)
                        sum_gates(t)
                    elif slot == PRODUCTS_SLOT + 8:
                        halve(t, 1)
                        halve(t, 2)
                    elif slot == PRODUCTS_SLOT + 9:
                        dve.wait_ge(picks_turned, picks)
                        halve(t, 3)
                        pick_gates(t)

                def keep_picks(t):
                    dve.wait_ge(picked_ready, t + 1)
                    dve.scalar_tensor_tensor(pick_index[:, t - DENSE], picked[:, 0], float(N_KEYS), picked[:, 1],
                                             ALU.mult, ALU.add)
                    dve.tensor_copy(pick_gate[:, t - DENSE], picked[:, 2]).then_inc(kept, 1)

                def one_hots(d, m):
                    n, slot = SLOTS * d + m, m % HOTS
                    if m == 0:
                        dve.wait_ge(picks_copied, d + 1)
                    dve.wait_ge(summed_gates, 2 * n + 2)
                    dve.tensor_tensor(hot[:, slot, 0:2],
                                      key_table[:, :, :].unsqueeze(1).broadcast_to([P, 2, N_KEYS, BATCH]),
                                      picked_t[:, 0:2, BATCH * m:BATCH * (m + 1)].unsqueeze(2)
                                      .broadcast_to([P, 2, N_KEYS, BATCH]), ALU.is_equal).then_inc(high_made, 1)
                    dve.wait_ge(high_made, n + 1)
                    dve.tensor_tensor(hot[:, slot, 2], hot[:, slot, 0],
                                      picked_t[:, 2, BATCH * m:BATCH * (m + 1)].unsqueeze(1)
                                      .broadcast_to([P, N_KEYS, BATCH]), ALU.mult).then_inc(hot_dve, 1)
                    if m in DVE_LOW_SLOTS:
                        dve.wait_ge(gate_split, d + 1)
                        dve.wait_ge(hot_low, n)
                        dve.tensor_tensor(hot[:, slot, 3], hot[:, slot, 0],
                                          picked_t[:, 3, BATCH * m:BATCH * (m + 1)].unsqueeze(1)
                                          .broadcast_to([P, N_KEYS, BATCH]), ALU.mult).then_inc(hot_low, 1)

                dve.tensor_copy(key_table[:, :, :], iota[:, :].unsqueeze(2).broadcast_to([P, N_KEYS, BATCH])
                                ).then_inc(table_made, 1)
                dve.tensor_copy(places[:, :, :], iota[:, 0:TOPK].unsqueeze(2).broadcast_to(
                    [P, TOPK, PEER_HEADS * TOPK])).then_inc(table_made, 1)
                dve.wait_ge(table_made, 2)
                for slot in range(SLOTS):
                    pick(0, slot, 1)
                with dve.Fori(1, DENSE + 1) as t:
                    pick(t, 0, t + 1)
                    for slot in range(SLOTS):
                        if slot + 1 < SLOTS:
                            pick(t, slot + 1, t + 1)
                        one_hots(t - 1, slot)
                keep_picks(DENSE)
                dve.wait_ge(kept, 1)
                for slot in range(SLOTS):
                    pick(TILES - 1, slot, DENSE + 1)
                keep_picks(TILES - 1)
                dve.wait_ge(kept, GATHERED)


EARLY = DENSE * 2 * KD * P // 2 + 4 * D_MODEL


def early_xs(early):
    return (early[:, 0:DENSE * KD * P].bitcast(BF16)
            .rearrange("p (t h c n) -> p t h c n", t=DENSE, h=2, c=KD))


def early_blocks(early):
    at = DENSE * KD * P
    return [early[:, at + 2 * D_MODEL * j:at + 2 * D_MODEL * (j + 1)].rearrange("p (k n) -> p k n", k=2)
            for j in range(2)]


def picks_of(p, first):
    middle = 2 * GROUP if first else PICKS // 2
    return (0, middle) if p == 0 else (middle, PICKS)


def load_block(sp, raw, blocks, arrived, b, k):
    sp.dma_start(raw[:, k], blocks[bass.ds(b, 1)].rearrange("o p d -> p (o d)")).then_inc(arrived[k], 16)


def expert_phase(nc, u_blocks, v_blocks, u_rows, v_rows, gates, ln2_g, ln2_b, out,
                 pick_index, pick_gate, acc, early, xs_in, u_in, v_in, acc_in):
    groups = N_KEYS // GROUP
    with ExitStack() as ctx:
        sb = lambda name, shape, dt: ctx.enter_context(nc.sbuf_tensor(name, shape, dt))
        sem = lambda name: ctx.enter_context(nc.semaphore(name))
        xs = early_xs(early)
        u_raw, v_raw = early_blocks(early)
        u_split = (early[:, EARLY:EARLY + 2 * KD * P].bitcast(BF16)
                   .rearrange("p (k h c n) -> p k h c n", k=2, h=2, c=KD))
        v_split = sb("v_split", [P, 2, GROUP, 2, D_MODEL], BF16)
        gate = sb("gate", [P, 2, TOKENS // CHUNK, GROUP, CHUNK], F32)
        act_out = sb("act_out", [P, 2, TOKENS], F32)
        w_split = sb("w_split", [P, 2, GROUP, 2, TOKENS], BF16)
        ln_g = sb("ln2_g_sb", [P, D_MODEL], F32)
        ln_b = sb("ln2_b_sb", [P, D_MODEL], F32)
        fetched = (early[:, EARLY + 2 * KD * P:EARLY + 2 * KD * P + RING * D_MODEL]
                   .rearrange("p (r d) -> p r d", r=RING))
        index_now = sb("index_now", [P, PICKS], U32)
        gate_now = sb("gate_now", [P, PICKS], F32)
        dots = sb("dots", [P, PICKS], F32)
        dots_all = sb("dots_all", [P, STINT * PICKS], F32)
        stats = sb("c_stats", [P, 2, 6], F32)
        moments = sb("c_moments", [P, TILES, 2], F32)
        eps = sb("c_eps", [P, 1], F32)
        std = sb("c_std", [P, TILES], F32)
        rstd = sb("c_rstd", [P, TILES], F32)
        newton = sb("c_newton", [P, TILES], F32)
        h_psum = [ctx.enter_context(nc.psum_tensor(f"h_psum{k}", [P, 2, 512], F32)) for k in range(2)]
        o_psum = [ctx.enter_context(nc.psum_tensor(f"o_psum{k}", [P, D_MODEL], F32)) for k in range(2)]

        ln_in = sem("ln_in")
        gate_in = [sem(f"gate_in{k}") for k in range(2)]
        u_hi_done, u_lo_done = sem("u_hi_done"), sem("u_lo_done")
        v_hi_done, v_split_done = sem("v_hi_done"), sem("v_split_done")
        h_done, gelu_done = sem("h_done"), sem("gelu_done")
        gated, w_hi_done, w_done = sem("gated"), sem("w_hi_done"), sem("w_done")
        o_done, o_added = sem("o_done"), sem("o_added")
        eps_set, stats_done, moments_done = sem("eps_set"), sem("stats_done2"), sem("moments_done2")
        std_done, rstd_step, centred = sem("std_done2"), sem("rstd_step2"), sem("centred2")
        scaled, rows_done, out_stored = sem("scaled2"), sem("rows_done2"), sem("out_stored")

        fetched_in = [sem(f"fetched_in{k}") for k in range(RING)]
        row_used, index_copied, dots_kept, dots_ready = sem("row_used"), sem("index_copied"), sem("dots_kept"), sem("dots_ready")
        weight_step, weights_copied, rows_scaled = sem("weight_step"), sem("weights_copied"), sem("rows_scaled")
        dots_gelu = sem("dots_gelu")

        last = groups // 2 - 1

        with nc.Block() as block:
            @block.sync
            def _(sp):
                def load_u(b, k):
                    load_block(sp, u_raw, u_blocks, u_in, b, k)

                def load_v(b, k):
                    load_block(sp, v_raw, v_blocks, v_in, b, k)

                def load_gate(g, p):
                    sp.dma_start(gate[:, p], gates[:, :, bass.ds(g * GROUP, GROUP), :]).then_inc(gate_in[p], 16)

                load_gate(0, 0)
                load_gate(1, 1)
                sp.dma_start(ln_g[:, :], ln2_g.partition_broadcast(P)).then_inc(ln_in, 16)
                sp.dma_start(ln_b[:, :], ln2_b.partition_broadcast(P)).then_inc(ln_in, 16)

                def refill(i, end):
                    for j in range(2 * GROUP):
                        b = 2 * GROUP * i + j
                        if not (end and j >= 2 * GROUP - 2):
                            sp.wait_ge(u_hi_done, b + 1)
                            sp.wait_ge(u_lo_done, b + 1)
                            load_u(b + 2, j % 2)
                            sp.wait_ge(v_split_done, b + 1)
                            load_v(b + 2, j % 2)
                        if j % GROUP == GROUP - 1 and not end:
                            sp.wait_ge(w_done, b + 1)
                            load_gate(2 * i + 2 + j // GROUP, j // GROUP)

                with sp.Fori(0, last) as i:
                    refill(i, False)
                refill(last, True)
                for n in range(TILES):
                    sp.wait_ge(rows_done, n + 1)
                    sp.dma_start(out[(DENSE + n) % TILES], acc[:, n]).then_inc(out_stored, 16)
                sp.wait_ge(out_stored, 16 * TILES)

            @block.scalar
            def _(act):
                def split_u_hi(b, k, n):
                    act.wait_ge(u_in[k], 16 * n)
                    if past(b - 1):
                        act.wait_ge(h_done, b - 1)
                    act.activation(u_split[:, k, 0], u_raw[:, k].rearrange("p (c n) -> p c n", c=KD), ACT.Copy
                                   ).then_inc(u_hi_done, 1)

                def gelu(b, k):
                    act.wait_ge(h_done, b + 1)
                    if past(b - 1):
                        act.wait_ge(w_done, b - 1)
                    act.activation(act_out[:, k].rearrange("p (a n) -> p a n", a=2), h_psum[k][:, :, 0:TOKENS // 2],
                                   ACT.Gelu).then_inc(gelu_done, 1)

                def split_v_hi(i, j):
                    p, q = j // GROUP, j % GROUP
                    act.wait_ge(v_in[j % 2], 16 * (GROUP * i + j // 2 + 1))
                    if q == 0 and past(2 * i + p - 1):
                        act.wait_ge(o_done, DENSE * (2 * i + p - 1))
                    act.activation(v_split[:, p, q, 0], v_raw[:, j % 2], ACT.Copy).then_inc(v_hi_done, 1)

                def blocks_of(i, end):
                    for j in range(2 * GROUP):
                        b = 2 * GROUP * i + j
                        gelu(b, j % 2)
                        split_v_hi(i, j)
                        if not (end and j >= 2 * GROUP - 2):
                            split_u_hi(b + 2, j % 2, GROUP * i + j // 2 + 2)

                split_u_hi(0, 0, 1)
                split_u_hi(1, 1, 1)
                blocks_of(0, False)
                for stint in range(2 * GATHERED):
                    with act.Fori(max(1, stint * STINT), min(last, (stint + 1) * STINT)) as i:
                        blocks_of(i, False)
                    if stint % 2 == 0:
                        act.wait_ge(dots_ready, stint // 2 + 1)
                        act.activation(dots_all[:, :], dots_all[:, :], ACT.Gelu).then_inc(dots_gelu, 1)
                blocks_of(last, True)
                act.wait_ge(eps_set, 1)
                for t in range(TILES):
                    act.wait_ge(moments_done, t + 1)
                    act.activation(std[:, t:t + 1], moments[:, t, 1:2], ACT.Sqrt, bias=eps[:, :]
                                   ).then_inc(std_done, 1)

            @block.gpsimd
            def _(pool):
                def split_u_lo(b, k, n):
                    pool.wait_ge(u_in[k], 16 * n)
                    pool.wait_ge(u_hi_done, b + 1)
                    if past(b - 1):
                        pool.wait_ge(h_done, b - 1)
                    pool.tensor_tensor(u_split[:, k, 1], u_raw[:, k].rearrange("p (c n) -> p c n", c=KD),
                                       u_split[:, k, 0], ALU.subtract).then_inc(u_lo_done, 1)

                def split_v(i, b, j, n):
                    p, q = j // GROUP, j % GROUP
                    pool.wait_ge(v_in[j % 2], 16 * n)
                    pool.wait_ge(v_hi_done, b + 1)
                    pool.tensor_tensor(v_split[:, p, q, 1], v_raw[:, j % 2], v_split[:, p, q, 0], ALU.subtract
                                       ).then_inc(v_split_done, 1)

                def fetch(i, source, n, first=False):
                    if not (first and n < RING):
                        pool.wait_ge(row_used, PICKS * i + n - RING + 1)
                        pool.nop(nofuse=True)
                    pool.indirect_dma_start(fetched[:, n % RING], None, source,
                                            bass.IndirectOffsetOnAxis(ap=index_now[:, n:n + 1], axis=0)
                                            ).then_inc(fetched_in[n % RING], 16)

                def blocks_of(i, j0, tile, source, end=False, first=False):
                    if not first:
                        pool.wait_ge(row_used, PICKS * i)
                        pool.nop(nofuse=True)
                    pool.tensor_copy(index_now[:, :], pick_index[:, tile, bass.ds(PICKS * (i - j0), PICKS)]
                                     ).then_inc(index_copied, 1)
                    pool.wait_ge(index_copied, i + 1)
                    pool.nop(nofuse=True)
                    for p in range(2):
                        start, stop = picks_of(p, first)
                        for q in range(GROUP):
                            j = p * GROUP + q
                            b = 2 * GROUP * i + j
                            n = GROUP * i + j // 2 + 1
                            split_v(i, b, j, n)
                            if not (end and j >= 2 * GROUP - 2):
                                split_u_lo(b + 2, j % 2, n + 1)
                            for r in range(2):
                                fetch(i, source, start + 2 * q + r, first)
                        for n in range(start + 2 * GROUP, stop):
                            fetch(i, source, n, first)

                split_u_lo(0, 0, 1)
                split_u_lo(1, 1, 1)
                blocks_of(0, 0, 0, u_rows, first=True)
                for stint in range(2 * GATHERED):
                    j0 = stint * STINT
                    args = (j0, stint // 2, v_rows if stint % 2 else u_rows)
                    with pool.Fori(max(1, j0), min(last, j0 + STINT)) as i:
                        blocks_of(i, *args)
                blocks_of(last, *args, end=True)
                pool.wait_ge(ln_in, 32)
                for n, t in enumerate(range(TILES)):
                    pool.wait_ge(centred, n + 1)
                    pool.tensor_tensor(acc[:, t], acc[:, t], ln_g[:, :], ALU.mult).then_inc(scaled, 1)

            @block.vector
            def _(dve):
                dve.memset(eps[:, :], LN_EPS).then_inc(eps_set, 1)

                def gate_and_split(b, g, p, q, n):
                    k = q % 2
                    dve.wait_ge(gelu_done, b + 1)
                    if q == 0:
                        dve.wait_ge(gate_in[p], 16 * n)
                        if past(g - 1):
                            dve.wait_ge(o_done, DENSE * (g - 1))
                    rows = act_out[:, k].rearrange("p (c t) -> p c t", t=CHUNK)
                    dve.tensor_tensor(rows, rows, gate[:, p, :, q, :], ALU.mult).then_inc(gated, 1)
                    dve.wait_ge(gated, b + 1)
                    dve.tensor_copy(w_split[:, p, q, 0], act_out[:, k]).then_inc(w_hi_done, 1)
                    dve.wait_ge(w_hi_done, b + 1)
                    dve.tensor_tensor(w_split[:, p, q, 1], act_out[:, k], w_split[:, p, q, 0], ALU.subtract
                                      ).then_inc(w_done, 1)

                def add(g, t, scale=1.0):
                    dve.wait_ge(o_done, DENSE * g + t + 1)
                    row = acc[:, GATHERED + t]
                    dve.scalar_tensor_tensor(row, row, scale, o_psum[t % 2][:, :], ALU.mult, ALU.add
                                             ).then_inc(o_added, 1)

                def take(i, j0, tile, kind, n):
                    dve.wait_ge(fetched_in[n % RING], 16 * (PICKS // RING * i + n // RING + 1))
                    if kind == "U":
                        dve.tensor_tensor_reduce(fetched[:, n % RING], fetched[:, n % RING], acc[:, tile], 1.0, 0.0,
                                                 ALU.mult, ALU.add, dots[:, n:n + 1]).then_inc(row_used, 1)
                    else:
                        dve.wait_ge(row_used, PICKS * i + n)
                        dve.scalar_tensor_tensor(acc[:, tile], fetched[:, n % RING], dots[:, n:n + 1], acc[:, tile],
                                                 ALU.mult, ALU.add).then_inc(row_used, 1)

                def step(g, i, p, n, j0, tile, kind, first):
                    start, stop = picks_of(p, first)
                    for q in range(GROUP):
                        gate_and_split(GROUP * g + q, g, p, q, n)
                        if q < GROUP - 1:
                            for r in range(2):
                                take(i, j0, tile, kind, start + 2 * q + r)
                    r = taken = start + 2 * (GROUP - 1)
                    for t in range(DENSE):
                        if not (first and p == 0):
                            if t == 0 and not first:
                                dve.wait_ge(o_added, DENSE * (g - 1))
                            add(g - 1, t)
                        upto = taken + (stop - taken) * (t + 1) // DENSE
                        for r in range(r, upto):
                            take(i, j0, tile, kind, r)
                        r = upto

                def pair(i, j0, tile, kind, first=False):
                    if kind == "V":
                        dve.wait_ge(row_used, PICKS * i)
                        dve.tensor_copy(dots[:, :], dots_all[:, bass.ds(PICKS * (i - j0), PICKS)]
                                        ).then_inc(weights_copied, 1)
                        dve.wait_ge(weights_copied, i - j0 + 1 + STINT * tile)
                    step(2 * i, i, 0, i + 1, j0, tile, kind, first)
                    step(2 * i + 1, i, 1, i + 1, j0, tile, kind, first)
                    if kind == "U":
                        dve.wait_ge(row_used, PICKS * (i + 1))
                        dve.tensor_copy(dots_all[:, bass.ds(PICKS * (i - j0), PICKS)], dots[:, :]
                                        ).then_inc(dots_kept, 1)
                        dve.wait_ge(dots_kept, i - j0 + 1 + STINT * tile)

                def weigh(tile):
                    dve.tensor_scalar(acc[:, tile], acc[:, tile], ALPHA, None, ALU.mult).then_inc(rows_scaled, 1)
                    dve.wait_ge(dots_gelu, tile + 1)
                    dve.tensor_tensor(dots_all[:, :], dots_all[:, :], pick_gate[:, tile], ALU.mult
                                      ).then_inc(weight_step, 1)
                    dve.wait_ge(weight_step, tile + 1)
                    dve.wait_ge(rows_scaled, DENSE + tile + 1)

                dve.wait_ge(acc_in, 16 * TILES)
                for t in range(DENSE):
                    dve.tensor_scalar(acc[:, GATHERED + t], acc[:, GATHERED + t], ALPHA, None, ALU.mult
                                      ).then_inc(rows_scaled, 1)
                dve.wait_ge(rows_scaled, DENSE)
                pair(0, 0, 0, "U", first=True)
                for stint in range(2 * GATHERED):
                    j0, tile, kind = stint * STINT, stint // 2, "UV"[stint % 2]
                    if kind == "V":
                        weigh(tile)
                    with dve.Fori(max(1, j0), min(last + 1, j0 + STINT)) as i:
                        pair(i, j0, tile, kind)
                    if kind == "U":
                        dve.drain().then_inc(dots_ready, 1)

                dve.wait_ge(ln_in, 32)
                dve.wait_ge(row_used, PICKS * groups // 2)

                def finish(t):
                    dve.wait_ge(scaled, t + 1)
                    dve.tensor_tensor(acc[:, t], acc[:, t], ln_b[:, :], ALU.add).then_inc(rows_done, 1)

                for t in range(TILES):
                    if t >= GATHERED:
                        add(groups - 1, t - GATHERED)
                        dve.wait_ge(o_added, DENSE * (groups - 1) + t - GATHERED + 1)
                    dve.bn_stats(stats[:, 0], acc[:, t, 0:512])
                    dve.bn_stats(stats[:, 1], acc[:, t, 512:1024]).then_inc(stats_done, 1)
                    dve.wait_ge(stats_done, t + 1)
                    dve.bn_aggr(moments[:, t], stats[:, :, :]).then_inc(moments_done, 1)
                    if t:
                        finish(t - 1)
                    newton_rstd(dve, moments[:, t], std[:, t:t + 1], rstd[:, t:t + 1], newton[:, t:t + 1],
                                moments_done, t + 1, std_done, t + 1, rstd_step, 5 * t)
                    dve.tensor_scalar(acc[:, t], acc[:, t], moments[:, t, 0:1], rstd[:, t:t + 1],
                                      ALU.subtract, ALU.mult).then_inc(centred, 1)
                finish(TILES - 1)

            @block.tensor
            def _(pe):
                def up(b, k):
                    pe.wait_ge(u_hi_done, b + 1)
                    pe.wait_ge(u_lo_done, b + 1)
                    if past(b - 1):
                        pe.wait_ge(gelu_done, b - 1)
                    for c in range(KD):
                        for part in range(2):
                            for xpart in range(2 - part):
                                for half in range(2):
                                    mm = pe.matmul(
                                        h_psum[k][:, half, 0:TOKENS // 2], u_split[:, k, part, c],
                                        xs[:, DENSE // 2 * half:DENSE // 2 * (half + 1), xpart, c, :],
                                        start=(c == 0 and part == 0 and xpart == 0),
                                        stop=(c == KD - 1 and part == 1))
                    mm.then_inc(h_done, 1)

                def down(g, p):
                    pe.wait_ge(w_done, GROUP * (g + 1))
                    pe.wait_ge(v_split_done, GROUP * (g + 1))
                    for t in range(DENSE):
                        if past(DENSE * g + t - 1):
                            pe.wait_ge(o_added, DENSE * g + t - 1)
                        for q in range(GROUP):
                            for part in range(2):
                                for vpart in range(2 - part):
                                    for half in range(2):
                                        mm = pe.matmul(
                                            o_psum[t % 2][:, half * 512:half * 512 + 512],
                                            w_split[:, p, q, part, t * P:(t + 1) * P],
                                            v_split[:, p, q, vpart, half * 512:half * 512 + 512],
                                            start=(q == 0 and part == 0 and vpart == 0),
                                            stop=(q == GROUP - 1 and part == 1))
                        mm.then_inc(o_done, 1)

                def pair(i, end=False):
                    for q in range(GROUP):
                        up(GROUP * (2 * i + 1) + q, q % 2)
                    down(2 * i, 0)
                    if not end:
                        for q in range(GROUP):
                            up(GROUP * (2 * i + 2) + q, q % 2)
                    down(2 * i + 1, 1)

                pe.wait_ge(xs_in, 16 * DENSE)
                for q in range(GROUP):
                    up(q, q % 2)
                pair(0, last == 0)
                if last > 1:
                    with pe.Fori(1, last) as i:
                        pair(i)
                if last > 0:
                    pair(last, True)


def shape_constants():
    token = np.arange(SEQ, dtype=np.float32)
    half = HEAD_DIM // 2
    inv = (10000.0 ** (-(np.arange(half, dtype=np.float32) / half)).astype(np.float64)).astype(np.float32)
    angle = (token[None, :] * inv[:, None]).astype(np.float64)
    rot = np.zeros((P, P), np.float32)
    for d in range(P):
        rot[d + half if d % HEAD_DIM < half else d - half, d] = -1.0 if d % HEAD_DIM < half else 1.0
    minus_row = np.zeros((FOX_HEADS, FOX_HEADS, P), np.float32)
    for h in range(FOX_HEADS):
        minus_row[h, h] = -1.0
    q, k = np.arange(P)[:, None], np.arange(P)[None, :]
    masks = np.concatenate([np.where(k > q, 0.0, LOW), np.where(k <= q, 0.0, LOW)], 1).astype(np.float32)
    return {
        "ident": np.eye(P, dtype=np.float32),
        "rot": rot,
        "minus_row": minus_row,
        "cos": np.tile(np.cos(angle).astype(np.float32), (P // half, 1)),
        "sin": np.tile(np.sin(angle).astype(np.float32), (P // half, 1)),
        "masks": masks,
        "iota": np.tile(np.arange(P, dtype=np.float32), (P, 1)),
    }


def column_blocks(w):
    return np.ascontiguousarray(w.reshape(KD, P, -1, P).transpose(2, 1, 0, 3))


def laid_out(x, w_in, b_forget, swa_sinks, w_out, ln1_g, ln1_b, w_query, sub_keys, expert_u, expert_v,
             ln2_g, ln2_b):
    fox = FOX_HEADS * HEAD_DIM
    w, x = w_in[0], x[0]
    swa = 3 * fox + FOX_HEADS
    skv = swa + SWA_HEADS * HEAD_DIM
    beside = (np.arange(SWA_HEADS * HEAD_DIM).reshape(2, PAIRS, HEAD_DIM).transpose(1, 0, 2)).ravel()
    w_fox = column_blocks(w[:, :3 * fox]).reshape(3, PAIRS, P, KD, P).transpose(1, 2, 0, 3, 4)
    rows = np.concatenate([np.arange(fox), fox + beside])
    return {
        "x_t": np.ascontiguousarray(x.T.reshape(KD, P, SEQ)),
        "x_rows": np.ascontiguousarray(x.reshape(TILES, P, D_MODEL)),
        "w_fox": np.ascontiguousarray(w_fox),
        "w_swa": column_blocks(w[:, swa:skv][:, beside]),
        "w_skv": np.ascontiguousarray(column_blocks(w[:, skv:]).transpose(1, 0, 2, 3)),
        "w_forget": np.ascontiguousarray(w[:, 3 * fox:swa].reshape(KD, P, FOX_HEADS).transpose(1, 0, 2)),
        "b_forget": np.ascontiguousarray(b_forget[0][:, None]),
        "sinks": np.ascontiguousarray(swa_sinks[0].reshape(2, PAIRS).T.ravel()),
        "w_out": np.ascontiguousarray(w_out[0][rows].reshape(KD, P, D_MODEL).transpose(1, 0, 2)),
        "ln1_g": np.ascontiguousarray(ln1_g[0]),
        "ln1_b": np.ascontiguousarray(ln1_b[0]),
        "w_query": np.ascontiguousarray(w_query[0].reshape(KD, P, SETS, P).transpose(1, 2, 0, 3)),
        "sub_keys": np.ascontiguousarray(sub_keys[0].reshape(SETS, N_KEYS, P).transpose(2, 0, 1)),
        "u_blocks": np.ascontiguousarray(
            expert_u[0].reshape(N_KEYS, P, KD, P).transpose(0, 3, 2, 1).reshape(N_KEYS, P, D_MODEL)),
        "u_rows": np.ascontiguousarray(expert_u[0]),
        "v_blocks": np.ascontiguousarray(expert_v[0].reshape(N_KEYS, P, D_MODEL)),
        "ln2_g": np.ascontiguousarray(ln2_g[0]),
        "ln2_b": np.ascontiguousarray(ln2_b[0]),
    }


def build(nc, dram, out):
    mixed_t = nc.dram_tensor("mixed_t", (TILES, P, 2, 2 * PAIRS, P), BF16, kind="Internal").ap()
    x1_rows = nc.dram_tensor("x1_rows", (TILES, P, D_MODEL), F32, kind="Internal").ap()
    x1_split = nc.dram_tensor("x1_split", (TILES, P, 2, KD, P), BF16, kind="Internal").ap()
    gates = nc.dram_tensor("gates", (P, TOKENS // CHUNK, N_KEYS, CHUNK), F32, kind="Internal").ap()
    with ExitStack() as ctx:
        sb = lambda name, shape, dt=F32: ctx.enter_context(nc.sbuf_tensor(name, shape, dt))
        sem = lambda name: ctx.enter_context(nc.semaphore(name))
        pick_index = sb("pick_index", [P, GATHERED, PEER_HEADS * TOPK], U32)
        pick_gate = sb("pick_gate", [P, GATHERED, PEER_HEADS * TOPK])
        wide = sb("wide", [P, KD, D_MODEL])[:, :, :]
        xs_in, acc_in = sem("xs_in"), sem("acc_in")
        u_in = [sem(f"u_in{k}") for k in range(2)]
        v_in = [sem(f"v_in{k}") for k in range(2)]
        attention_phase(nc, dram["x_t"], dram["w_fox"], dram["w_swa"], dram["w_skv"], dram["w_forget"],
                        dram["b_forget"], dram["sinks"], dram["w_out"], dram, mixed_t, wide)
        early = sb("early", [P, SETS * KD * P])[:, :]

        def load_early(sp):
            for t in range(DENSE):
                sp.dma_start(early_xs(early)[:, t], x1_split[t]).then_inc(xs_in, 16)
            u_raw, v_raw = early_blocks(early)
            for k in range(2):
                load_block(sp, u_raw, dram["u_blocks"], u_in, k, k)
            for k in range(2):
                load_block(sp, v_raw, dram["v_blocks"], v_in, k, k)

        def load_rows_of_x1(sp):
            for t in range(TILES):
                sp.dma_start(wide[:, t], x1_rows[(DENSE + t) % TILES]).then_inc(acc_in, 16)

        routing_phase(nc, mixed_t, dram["x_rows"], dram["ln1_g"], dram["ln1_b"], dram["w_query"],
                      dram["sub_keys"], dram, x1_rows, x1_split, gates, pick_index, pick_gate, wide,
                      early, load_early, load_rows_of_x1)
        expert_phase(nc, dram["u_blocks"], dram["v_blocks"], dram["u_rows"],
                     dram["v_blocks"].rearrange("b p d -> (b p) d"), gates,
                     dram["ln2_g"], dram["ln2_b"], out, pick_index, pick_gate, wide, early, xs_in, u_in, v_in,
                     acc_in)


def kernel(**inputs):
    import concourse.bacc as bacc
    from concourse.bass_utils import run_bass_kernel_spmd

    arrays = laid_out(**{name: np.asarray(a) for name, a in inputs.items()}) | shape_constants()
    nc = bacc.Bacc("TRN2", target_bir_lowering=False, num_devices=1)
    dram = {name: nc.dram_tensor(name, a.shape, F32, kind="ExternalInput").ap() for name, a in arrays.items()}
    out = nc.dram_tensor("out", (TILES, P, D_MODEL), F32, kind="ExternalOutput").ap()
    build(nc, dram, out)
    result = run_bass_kernel_spmd(nc, [arrays], core_ids=[0])
    return result.results[0]["out"].reshape(1, SEQ, D_MODEL)
```
